# Optimizing a Trainium2 kernel written in Bass

```python
import math
import jax, jax.numpy as jnp
from jax import lax
import numpy as np

D_MODEL = 1024
BATCH = 1
SEQ = 512
DEPTH = 1

D_MIX = D_MODEL
D_POOL = D_MIX // 2
POOL_WINDOWS = (2, 4, 8, 16)
N_POOL_GROUPS = len(POOL_WINDOWS)
POOL_GROUP = D_POOL // N_POOL_GROUPS
D_SSM = D_MIX - D_POOL
SSM_GROUP = 16
N_SSM_GROUPS = D_SSM // SSM_GROUP
SSM_STATE = 64
N_DIR = 2
DT_MIN = 0.001
DT_MAX = 0.1
N_EXPERT_GROUPS = 4
EXPERTS_PER_GROUP = 8
TOP_K_IN_GROUP = 2
D_EXPERT = D_MODEL // 4
D_PLE = 256
RMS_EPS = 1e-6

kernel_name = 'hymba_pool_s5_hmoe_block'

F32 = jnp.float32

def rmsnorm(x, g):
    xf = x.astype(F32)
    y = xf * lax.rsqrt(jnp.mean(xf * xf, axis=-1, keepdims=True) + RMS_EPS)
    return (y * g.astype(F32)).astype(x.dtype)

def centred_window_mean(x, w):
    s = x.shape[1]
    xf = x.astype(F32)
    cs = jnp.concatenate([jnp.zeros_like(xf[:, :1]), jnp.cumsum(xf, axis=1)], axis=1)
    t = jnp.arange(s)
    lo = jnp.clip(t - w // 2, 0, s)
    hi = jnp.clip(t - w // 2 + w, 0, s)
    total = jnp.take(cs, hi, axis=1) - jnp.take(cs, lo, axis=1)
    return total / (hi - lo).astype(F32)[None, :, None]

def pool_mixer(u, pool_w, pool_scale):
    outs = []
    for gi, w in enumerate(POOL_WINDOWS):
        ug = u[..., gi * POOL_GROUP:(gi + 1) * POOL_GROUP]
        diff = (centred_window_mean(ug, w) - ug.astype(F32)).astype(u.dtype)
        outs.append(diff @ pool_w[gi])
    return jnp.concatenate(outs, axis=-1) * pool_scale

def ssm_scan_direction(u_c, lam_bar, b_bar, c):
    bu = jnp.einsum('bsgc,gnc->bsgn', u_c, b_bar)
    a = jnp.broadcast_to(lam_bar, bu.shape)

    def combine(left, right):
        a_l, b_l = left
        a_r, b_r = right
        return a_l * a_r, a_r * b_l + b_r

    _, states = lax.associative_scan(combine, (a, bu), axis=1)
    return jnp.einsum('bsgn,gcn->bsgc', states, c).real

def ssm_mixer(u, a_re, a_im, log_dt, b_re, b_im, c_re, c_im, d, glu_w, glu_b):
    bsz, s, _ = u.shape
    uf = u.astype(F32)
    u_c = uf.reshape(bsz, s, N_SSM_GROUPS, SSM_GROUP).astype(jnp.complex64)
    y = uf * d.astype(F32)
    for di in range(N_DIR):
        lam = lax.complex(a_re[di].astype(F32), a_im[di].astype(F32))
        dt = jnp.exp(log_dt[di].astype(F32))[:, None]
        lam_bar = jnp.exp(lam * dt)
        b_bar = ((lam_bar - 1.0) / lam)[..., None] * lax.complex(b_re[di].astype(F32), b_im[di].astype(F32))
        c = lax.complex(c_re[di].astype(F32), c_im[di].astype(F32))
        if di == 0:
            yd = ssm_scan_direction(u_c, lam_bar, b_bar, c)
        else:
            yd = jnp.flip(ssm_scan_direction(jnp.flip(u_c, axis=1), lam_bar, b_bar, c), axis=1)
        y = y + yd.reshape(bsz, s, D_SSM)
    z = jax.nn.gelu(y)
    gate = jax.nn.sigmoid(z @ glu_w.astype(F32) + glu_b.astype(F32))
    return (z * gate).astype(u.dtype)

def hierarchical_moe(v, grp_w, grp_b, exp_w, exp_b, w_gate, w_up, w_down):
    bsz, s, dm = v.shape
    t = v.reshape(-1, dm)
    tf = t.astype(F32)
    grp_prob = jax.nn.softmax(tf @ grp_w.astype(F32) + grp_b.astype(F32), axis=-1)
    grp_p, grp_idx = lax.top_k(grp_prob, 1)
    exp_logits = jnp.einsum('td,gde->tge', tf, exp_w.astype(F32)) + exp_b.astype(F32)
    sel_logits = jnp.take_along_axis(exp_logits, grp_idx[:, :, None], axis=1)[:, 0]
    exp_prob = jax.nn.softmax(sel_logits, axis=-1)
    top_w, top_idx = lax.top_k(exp_prob, TOP_K_IN_GROUP)
    top_w = top_w / jnp.sum(top_w, axis=-1, keepdims=True)
    exp_comb = jnp.sum(jax.nn.one_hot(top_idx, EXPERTS_PER_GROUP, dtype=F32) * top_w[..., None], axis=1)
    combine = jax.nn.one_hot(grp_idx[:, 0], N_EXPERT_GROUPS, dtype=F32)[:, :, None] * (grp_p * exp_comb)[:, None, :]
    out = jnp.zeros((t.shape[0], dm), F32)
    for g in range(N_EXPERT_GROUPS):
        hg = jax.nn.silu(jnp.einsum('td,edf->tef', t, w_gate[g])) * jnp.einsum('td,edf->tef', t, w_up[g])
        hg = hg * combine[:, g, :, None].astype(hg.dtype)
        out = out + jnp.einsum('tef,efd->td', hg, w_down[g]).astype(F32)
    return out.astype(v.dtype).reshape(bsz, s, dm)

def setup_inputs(seed: int = 0) -> dict:
    key = jax.random.key(seed)
    ks = jax.random.split(key, 32)
    L = DEPTH
    G, N, C = N_SSM_GROUPS, SSM_STATE, SSM_GROUP
    GE, E, F = N_EXPERT_GROUPS, EXPERTS_PER_GROUP, D_EXPERT
    nrm = lambda k, shape, scale: jax.random.normal(k, shape, F32) * scale
    a_im_base = jnp.pi * jnp.arange(N, dtype=F32)
    return {
        'x': jax.random.normal(ks[0], (BATCH, SEQ, D_MODEL), F32),
        'p': jax.random.normal(ks[1], (DEPTH, BATCH, SEQ, D_PLE), F32),
        'g_mix': 1.0 + nrm(ks[2], (L, D_MODEL), 0.05),
        'w_in': nrm(ks[3], (L, D_MODEL, D_MIX), D_MODEL ** -0.5),
        'pool_w': nrm(ks[4], (L, N_POOL_GROUPS, POOL_GROUP, POOL_GROUP), POOL_GROUP ** -0.5),
        'pool_scale': 1.0 + nrm(ks[5], (L, D_POOL), 0.05),
        'ssm_a_re': -0.5 + nrm(ks[6], (L, N_DIR, G, N), 0.01),
        'ssm_a_im': a_im_base + nrm(ks[7], (L, N_DIR, G, N), 0.01),
        'ssm_log_dt': jax.random.uniform(ks[8], (L, N_DIR, G), F32, math.log(DT_MIN), math.log(DT_MAX)),
        'ssm_b_re': nrm(ks[9], (L, N_DIR, G, N, C), (2 * C) ** -0.5),
        'ssm_b_im': nrm(ks[10], (L, N_DIR, G, N, C), (2 * C) ** -0.5),
        'ssm_c_re': nrm(ks[11], (L, N_DIR, G, C, N), 0.5),
        'ssm_c_im': nrm(ks[12], (L, N_DIR, G, C, N), 0.5),
        'ssm_d': nrm(ks[13], (L, D_SSM), 1.0),
        'glu_w': nrm(ks[14], (L, D_SSM, D_SSM), D_SSM ** -0.5),
        'glu_b': nrm(ks[15], (L, D_SSM), 0.02),
        'w_out': nrm(ks[16], (L, D_MIX, D_MODEL), D_MIX ** -0.5),
        'g_ffn': 1.0 + nrm(ks[17], (L, D_MODEL), 0.05),
        'router_grp_w': nrm(ks[18], (L, D_MODEL, GE), D_MODEL ** -0.5),
        'router_grp_b': nrm(ks[19], (L, GE), 0.01),
        'router_exp_w': nrm(ks[20], (L, GE, D_MODEL, E), D_MODEL ** -0.5),
        'router_exp_b': nrm(ks[21], (L, GE, E), 0.01),
        'exp_w_gate': nrm(ks[22], (L, GE, E, D_MODEL, F), D_MODEL ** -0.5),
        'exp_w_up': nrm(ks[23], (L, GE, E, D_MODEL, F), D_MODEL ** -0.5),
        'exp_w_down': nrm(ks[24], (L, GE, E, F, D_MODEL), F ** -0.5),
        'g_ple': 1.0 + nrm(ks[25], (L, D_MODEL), 0.05),
        'ple_gate_w': nrm(ks[26], (L, D_MODEL, D_MODEL), D_MODEL ** -0.5),
        'ple_gate_b': nrm(ks[27], (L, D_MODEL), 0.02),
        'ple_proj_w': nrm(ks[28], (L, D_PLE, D_MODEL), D_PLE ** -0.5),
        'g_final': 1.0 + nrm(ks[29], (D_MODEL,), 0.05),
    }

def reference(x, p, g_mix, w_in, pool_w, pool_scale, ssm_a_re, ssm_a_im, ssm_log_dt,
              ssm_b_re, ssm_b_im, ssm_c_re, ssm_c_im, ssm_d, glu_w, glu_b, w_out,
              g_ffn, router_grp_w, router_grp_b, router_exp_w, router_exp_b,
              exp_w_gate, exp_w_up, exp_w_down, g_ple, ple_gate_w, ple_gate_b,
              ple_proj_w, g_final):
    h = x
    for i in range(DEPTH):
        u = rmsnorm(h, g_mix[i])
        z = u @ w_in[i]
        a = pool_mixer(z[..., :D_POOL], pool_w[i], pool_scale[i])
        s = ssm_mixer(z[..., D_POOL:], ssm_a_re[i], ssm_a_im[i], ssm_log_dt[i],
                      ssm_b_re[i], ssm_b_im[i], ssm_c_re[i], ssm_c_im[i], ssm_d[i],
                      glu_w[i], glu_b[i])
        h = h + jnp.concatenate([a, s], axis=-1) @ w_out[i]
        h = h + hierarchical_moe(rmsnorm(h, g_ffn[i]), router_grp_w[i], router_grp_b[i],
                                 router_exp_w[i], router_exp_b[i], exp_w_gate[i],
                                 exp_w_up[i], exp_w_down[i])
        gate = jax.nn.sigmoid(rmsnorm(h, g_ple[i]) @ ple_gate_w[i] + ple_gate_b[i])
        h = h + gate * (p[i] @ ple_proj_w[i])
    return rmsnorm(h, g_final)


_drawn_inputs = setup_inputs


def setup_inputs(seed=0):
    import zlib

    import numpy as np

    out = dict(_drawn_inputs(seed))
    spreads = {}
    factors = {'ssm_a_re': 200.0,
     'glu_b': 17.111,
     'router_grp_b': 6.151,
     'router_exp_b': 5.533,
     'g_ple': 7.125,
     'ple_gate_b': 44.974,
     'ssm_a_im': 2.733,
     'ssm_b_re': 2.979,
     'ssm_b_im': 2.879,
     'ssm_c_im': 2.823}
    for name, (base, spread) in spreads.items():
        noise = np.random.default_rng([zlib.crc32(name.encode()), seed]).standard_normal(out[name].shape)
        drawn = base * np.exp(spread * noise) if base else spread * noise
        out[name] = __import__('jax').numpy.asarray(drawn.astype(out[name].dtype))
    for name, factor in factors.items():
        out[name] = (out[name] * factor).astype(out[name].dtype)
    return out
```

```python
from contextlib import ExitStack

import concourse.bass as bass
import numpy as np
from concourse import mybir

ALU = mybir.AluOpType
ACT = mybir.ActivationFunctionType
AX = mybir.AxisListType
F32 = mybir.dt.float32
I32 = mybir.dt.int32

P = 128
T = 512
DM = 1024
NT = T // P
KC = DM // P
DP = 512
WINDOWS = (2, 4, 8, 16)
PAD = 8
PW_ = T + 2 * PAD
G = 32
CH = 16
NS = 64
L = 8
NCH = T // L
GB = 8
NB = G // GB
NG = 4
NEG = 8
NE = NG * NEG
DE = 256
DPLE = 256
EPS = 1e-6
CAP = 64
ROUNDS = T // CAP
RING = 4
TWO_PI = 6.283185307179586
PI_LO = 3.1415925
TP1 = 6.28125
TP2 = 0.0019350051879882812
TP3 = TWO_PI - TP1 - TP2
ROUND = 12582912.0
EMPTY = 2 * T


def constants():
    ident = np.eye(P, dtype=np.float32)
    tri = np.triu(np.ones((P, P), np.float32), 1)
    ones = np.ones((P, P), np.float32)
    edge = np.ones((4, 2, PAD), np.float32)
    for i, w in enumerate(WINDOWS):
        for k in range(PAD):
            edge[i, 0, k] = w / (min(k - w // 2 + w, T) - max(k - w // 2, 0))
            t = T - PAD + k
            edge[i, 1, k] = w / (min(t - w // 2 + w, T) - max(t - w // 2, 0))
    edge = np.broadcast_to(edge.reshape(1, -1), (P, 64))
    number = np.broadcast_to(np.arange(NE, dtype=np.float32), (P, NE))
    lower = np.broadcast_to(np.arange(NEG, 0, -1).astype(np.float32), (P, NEG))
    pair = (2 * (np.arange(NT)[None, :, None] * P + np.arange(P)[:, None, None])
            + np.arange(2)[None, None, :]).reshape(P, 2 * NT).astype(np.float32)
    half = (np.arange(P) // CAP).astype(np.float32)[:, None]
    return np.ascontiguousarray(np.concatenate([ident, tri, ones, edge, number, lower, pair, half], 1), np.float32)


C_ID, C_TRI, C_ONE, C_EDGE, C_NUM, C_LOW, C_PAIR, C_HALF, C_END = 0, 128, 256, 384, 448, 480, 488, 496, 497


def at(t, parts, off, dims):
    p0, p1 = parts
    width = t.shape[1]
    return bass.AP(t, p0 * width + off, [[width, p1 - p0]] + [list(d) for d in dims])


def dr(a, off, dims):
    return bass.AP(a.tensor, off, [list(d) for d in dims])


def least(eng, sem, value):
    if isinstance(value, int) and value <= 0:
        return
    eng.wait_ge(sem, value)


class Chain:

    def __init__(self, eng, sem):
        self.eng, self.sem, self.n = eng, sem, 0

    def do(self, ins):
        ins.then_inc(self.sem, 1)
        self.n += 1
        return self.n

    def settle(self):
        self.eng.wait_ge(self.sem, self.n)


def build(nc, A, out):
    ctx = ExitStack()
    with ctx:
        def sb(name, width, dt=F32):
            return ctx.enter_context(nc.sbuf_tensor(name, [P, width], dt))

        def sem(name):
            return ctx.enter_context(nc.semaphore(name))

        def scratch(name, shape, dt=F32):
            return nc.dram_tensor(name, shape, dt, kind="Internal").ap()

        ALL = (0, P)
        FWD, BWD = (0, NS), (NS, P)
        SLOT = 3 * KC * DE
        ring = sb("ring", RING * SLOT)
        h = sb("h", NT * DM)
        big = sb("big", KC * DM)
        ut = sb("ut", KC * T)
        moe = sb("moe", 6144)
        zbuf = sb("zbuf", NB * T + 4 * PW_)
        cst = sb("cst", C_END)
        rw = sb("rw", KC * (NG + NE))
        vec = sb("vec", 24 + 12)
        small = sb("small", 64 + 8 * G)
        rbias = sb("rbias", NG + NE)
        tblw = sb("tblw", NE, I32)
        gidx_all = sb("gidx_all", NE // 2 + 1, I32)
        sidx_all = sb("sidx_all", NE, I32)
        gidx = [sb(f"gidx{k}", 1, I32) for k in range(2)]
        sidx = [sb(f"sidx{k}", 1, I32) for k in range(2)]
        flag = sb("flag", 1, I32)
        slot_i = sb("slot_i", 2 * NT, I32)
        pair_i = sb("pair_i", 2 * NT, I32)
        fill = sb("fill", P, I32)
        vrow = sb("vrow", P)
        bank = [ctx.enter_context(nc.psum_tensor(f"bank{k}", [P, 512], F32)) for k in range(8)]

        V_MIX, V_FFN, V_PLE, V_POOL, V_D, V_GLU = 0, 8, 16, 24, 28, 32
        S_SS, S_RS, S_EPS, S_W1, S_W2, S_SS2, S_RS2, S_SS3, S_RS3, S_SS4, S_RS4 = (
            0, 4, 8, 12, 16, 20, 24, 28, 32, 36, 40)
        S_A2, S_T1, S_T2 = 64, 64 + 4 * G, 64 + 6 * G
        R_CW, R_CWN = 0, 4608
        R_U = 9216
        R_BB, R_BBI = R_U + 2048, R_U + 2048 + 528
        R_CL = R_BB + 1056
        R_W = R_CL + 1024
        R_T = R_W + 2048
        R_X = R_T + 4096
        R_CRAW = R_CW
        R_PW = R_T
        R_PIN = R_PW + 18 * G
        R_PC = R_PIN + 16 * G
        R_COEF = R_PC + 18 * G
        R_TMP = R_COEF + 2 * G
        R_GLU = R_T
        R_Y = R_U
        R_YC = R_X
        R_ZG = R_X + 2048
        R_LAM = R_X
        R_BRAW = R_X + 2560
        assert R_TMP + 1152 <= R_X and R_X + 65 * 64 <= RING * SLOT
        M_WT, M_XO, M_XN = 0, 0, 0
        M_PT, M_PW = 4096, 4096 + 2 * PW_
        M_PPW, M_PIN, M_PPT = 0, 2048, 3072
        M_XT, M_HG, M_SG, M_HT, M_Y, M_XG = 0, 2048, 2176, 2432, 2688, 4096
        Z_SSM, Z_POOL = 0, NB * T
        Q = {}
        q = 0
        for name, n in (("L", NT * 36), ("gm", NT), ("d4", NT * 4), ("e4", NT * 4), ("gs", NT), ("gp", NT),
                        ("g1", NT * 4), ("g2", NT), ("goh", NT * 4), ("pr", NT * 32), ("sel", NT * 8),
                        ("m1", NT), ("q1", NT * 8), ("q2", NT), ("oh1", NT * 8), ("s2", NT * 8), ("m2", NT),
                        ("q3", NT * 8), ("q4", NT), ("oh2", NT * 8), ("df", NT), ("ex", NT), ("dn", NT),
                        ("M1", NT * 32), ("M2", NT * 32), ("MS", NT * 32), ("rk", NT * 32), ("tot", 32),
                        ("pa", NT * 32), ("pb", NT * 32), ("r1", NT), ("r2", NT), ("e1", NT), ("e2", NT),
                        ("sf", 2 * NT), ("mx", 1)):
            Q[name] = q
            q += n
        assert q <= 4096

        z_d = scratch("z_d", [P, G * NCH])
        y_d = scratch("y_d", [P, G * NCH])
        k_d = scratch("k_d", [G * CH, 15 * CH])
        v_d = scratch("v_d", [T, DM])
        tbl_d = scratch("tbl_d", [T * NE, 1], I32)
        pairs_d = scratch("pairs_d", [4 * T, DM // 2])

        ld_c, ld_small, ld_vec, ld_win0, ld_win1, ld_b, ld_craw, ld_poolw = (
            sem(n) for n in ("ld_c", "ld_small", "ld_vec", "ld_win0", "ld_win1", "ld_b", "ld_craw", "ld_poolw"))
        ld_x = [sem(f"ld_x{t}") for t in range(NT)]
        ld_wout0, ld_wout1, ld_glu, ld_ppw, ld_wple, ld_fin = (
            sem(n) for n in ("ld_wout0", "ld_wout1", "ld_glu", "ld_ppw", "ld_wple", "ld_fin"))
        w_ready = [sem(f"w_ready{k}") for k in range(RING)]
        dve_step, pool_step = sem("dve_step"), sem("pool_step")
        ss_done, rms_root, rstd_done, turned_ps, ut_done = (
            sem(n) for n in ("ss_done", "rms_root", "rstd_done", "turned_ps", "ut_done"))
        xn_done, vec_done = sem("xn_done"), sem("vec_done")
        vec_ps, c_ps, c_done, lam_dt, lam_arg, lam_exp, lam_red, lam_sin, lam_done, lam_ps, lam_lane = (
            sem(n) for n in ("vec_ps", "c_ps", "c_done", "lam_dt", "lam_arg", "lam_exp", "lam_red", "lam_sin",
                             "lam_done", "lam_ps", "lam_lane"))
        pow_done, pin_done, pc_done = sem("pow_done"), sem("pin_done"), sem("pc_done")
        win_ps, zs_done, zs_stored = sem("win_ps"), sem("zs_done"), sem("zs_stored")
        u_ready = [sem(f"u_ready{m}") for m in range(NB)]
        yc_ready = [sem(f"yc_ready{m}") for m in range(NB)]
        w_built, wt_ps, wt_done, e_ps, e_done = (
            sem(n) for n in ("w_built", "wt_ps", "wt_done", "e_ps", "e_done"))
        cw_built, k_ps, k_done, k_stored, toep_ready, tu_done = (
            sem(n) for n in ("cw_built", "k_ps", "k_done", "k_stored", "toep_ready", "tu_done"))
        zp_ps, zp_done, diff_done, a_ps, a_done, wo0_ps, wo0_sb, wo0_done = (
            sem(n) for n in ("zp_ps", "zp_done", "diff_done", "a_ps", "a_done", "wo0_ps", "wo0_sb", "wo0_done"))
        scan_a, scan_b, xo_re, xo_im, y_ps, y_sb, y_stored = (
            sem(n) for n in ("scan_a", "scan_b", "xo_re", "xo_im", "y_ps", "y_sb", "y_stored"))
        yd_done, zg_done, glu_ps, gate_done, cat_done, wo1_ps, h_done = (
            sem(n) for n in ("yd_done", "zg_done", "glu_ps", "gate_done", "cat_done", "wo1_ps", "h_done"))
        v_done, v_stored, log_ps = sem("v_done"), sem("v_stored"), sem("log_ps")
        d4_done, df_done, ex_done, mask_done, rank_ps, slot_done, tbl_filled, tbl_set, tbl_read, idx_done = (
            sem(n) for n in ("d4_done", "df_done", "ex_done", "mask_done", "rank_ps", "slot_done",
                             "tbl_filled", "tbl_set", "tbl_read", "idx_done"))
        ppt_ps, ppt_sb, pp_ps, pp_done = sem("ppt_ps"), sem("ppt_sb"), sem("pp_ps"), sem("pp_done")
        x_zero = sem("x_zero")
        xg_ready = [sem(f"xg_ready{k}") for k in range(2)]
        ys_stored = [sem(f"ys_stored{k}") for k in range(2)]
        gi_set, si_set = sem("gi_set"), sem("si_set")
        xT_ps, xT_sb, gu_ps, sg_sb, hg_sb, hT_ps, hT_sb, dn_ps, dn_sb = (
            sem(n) for n in ("xT_ps", "xT_sb", "gu_ps", "sg_sb", "hg_sb", "hT_ps", "hT_sb", "dn_ps", "dn_sb"))
        o_w, o_tbl, o_idx, o_xg, o_xT_ps, o_xT, o_gu, o_sg, o_hg, o_hT_ps, o_hT, o_dn, o_dn_sb, o_st, o_turn = (
            sem("o_" + n) for n in ("w", "tbl", "idx", "xg", "xT_ps", "xT", "gu", "sg", "hg", "hT_ps", "hT",
                                    "dn", "dn_sb", "st", "turn"))
        moe_done, eps_set = sem("moe_done"), sem("eps_set")
        ld_pairs = [sem(f"ld_pairs{t}") for t in range(NT)]
        comb, r_done, gate_ps, gate_sb, gated, fin_done = (
            sem(n) for n in ("comb", "r_done", "gate_ps", "gate_sb", "gated", "fin_done"))
        stored = sem("stored")

        ident = at(cst, ALL, C_ID, [[1, P]])
        ident32 = at(cst, (0, 32), C_ID, [[1, 32]])
        E_YP, E_RN, E_SG, E_GF, E_BP, E_O = 0, 4096, 8192, 12288, 13312, 14336

        x_d = A["x"].rearrange("b s d -> (b s) d")
        wg_d = A["exp_w_gate"].rearrange("l g e d f -> (l g e) d f")
        wu_d = A["exp_w_up"].rearrange("l g e d f -> (l g e) d f")
        wd_d = A["exp_w_down"].rearrange("l g e f d -> (l g e) f d")
        out_d = out.rearrange("b s d -> (b s) d")

        block = ctx.enter_context(nc.Block())

        def vcol(c):
            return at(vec, ALL, c, [[1, 1]])

        def lam(k):
            return at(ring, (0, G), R_LAM + k * P, [[1, P]])

        def shift(i, u, d):
            return i + (u + d) // RING, (u + d) % RING

        def valid(i, u):
            return not isinstance(i, int) or 0 <= i < NE // RING

        def sweep(eng, step):
            for u in range(RING):
                step(0, u)
            with eng.Fori(1, NE // RING - 1) as i:
                for u in range(RING):
                    step(i, u)
            for u in range(RING):
                step(NE // RING - 1, u)

        def most(eng):
            return eng.value_load(at(flag, (0, 1), 0, [[1, 1]]), min_val=0, max_val=T)

        def load_expert(eng, e, slot, done):
            base = slot * SLOT
            for n, w in enumerate((wg_d, wu_d)):
                eng.dma_start(at(ring, ALL, base + n * KC * DE, [[1, KC * DE]]),
                              w[e].rearrange("(p j) f -> p (j f)", p=P)).then_inc(done, 16)
            eng.dma_start(at(ring, ALL, base + 2 * KC * DE, [[1, 2 * DM]]),
                          wd_d[e].rearrange("(p j) d -> p (j d)", p=P)).then_inc(done, 16)

        @block.sync
        def _(sp):
            sp.dma_start(cst[:, :], A["consts"]).then_inc(ld_c, 16)
            for t in range(NT):
                sp.dma_start(at(h, ALL, t * DM, [[1, DM]]), x_d[t * P:(t + 1) * P, :]).then_inc(ld_x[t], 16)
            for n, name in enumerate(("ssm_a_re", "ssm_a_im")):
                sp.dma_start(at(ring, (0, G), R_LAM + n * P, [[NS, 2], [1, NS]]),
                             dr(A[name], 0, [[NS, G], [G * NS, 2], [1, NS]])).then_inc(ld_small, 16)
            for d in range(2):
                sp.dma_start(at(ring, (0, G), R_LAM + 2 * P + d, [[1, 1]]),
                             dr(A["ssm_log_dt"], d * G, [[1, G], [1, 1]])).then_inc(ld_small, 16)
            for n, name in enumerate(("g_mix", "g_ffn", "g_ple")):
                sp.dma_start(at(vec, ALL, 8 * n, [[1, KC]]), dr(A[name], 0, [[KC, P], [1, KC]])).then_inc(ld_vec, 16)
            for n, name in enumerate(("pool_scale", "ssm_d", "glu_b")):
                sp.dma_start(at(vrow, (4 * n, 4 * n + 4), 0, [[1, P]]),
                             dr(A[name], 0, [[P, 4], [1, P]])).then_inc(ld_vec, 16)
            sp.dma_start(at(big, ALL, 0, [[DP, KC], [1, DP]]),
                         dr(A["w_in"], DP, [[KC * DM, P], [DM, KC], [1, DP]])).then_inc(ld_win0, 16)
            for n, name in enumerate(("ssm_c_re", "ssm_c_im")):
                for d in range(2):
                    sp.dma_start(at(ring, ALL, R_CRAW + n * 4 * P + d * NS, [[P, NB], [1, NS]]),
                                 dr(A[name], d * G * CH * NS, [[NS, P], [GB * CH * NS, NB], [1, NS]])
                                 ).then_inc(ld_craw, 16)
            for n, name in enumerate(("ssm_b_re", "ssm_b_im")):
                for d in range(2):
                    sp.dma_start(at(ring, (d * NS, d * NS + NS), R_BRAW + n * G * CH, [[CH, G], [1, CH]]),
                                 dr(A[name], d * G * NS * CH, [[CH, NS], [NS * CH, G], [1, CH]])
                                 ).then_inc(ld_b, 16)
            sp.dma_start(at(big, ALL, KC * DP, [[DP, KC], [1, DP]]),
                         dr(A["w_in"], 0, [[KC * DM, P], [DM, KC], [1, DP]])).then_inc(ld_win1, 16)
            sp.wait_ge(turned_ps, 1)
            sp.dma_start(at(moe, ALL, M_PW, [[P, 4], [1, P]]),
                         dr(A["pool_w"], 0, [[P, P], [P * P, 4], [1, P]])).then_inc(ld_poolw, 16)
            sp.dma_start(at(rw, ALL, 0, [[NG + NE, KC], [1, NG]]),
                         dr(A["router_grp_w"], 0, [[KC * NG, P], [NG, KC], [1, NG]])).then_inc(ld_poolw, 16)
            for g in range(NG):
                sp.dma_start(at(rw, ALL, NG + g * NEG, [[NG + NE, KC], [1, NEG]]),
                             dr(A["router_exp_w"], g * DM * NEG, [[KC * NEG, P], [NEG, KC], [1, NEG]])
                             ).then_inc(ld_poolw, 16)
            sp.dma_start(at(rbias, (0, 1), 0, [[1, NG]]), dr(A["router_grp_b"], 0, [[NG, 1], [1, NG]])
                         ).then_inc(ld_poolw, 16)
            sp.dma_start(at(rbias, (0, 1), NG, [[1, NE]]), dr(A["router_exp_b"], 0, [[NE, 1], [1, NE]])
                         ).then_inc(ld_poolw, 16)
            for m in range(NB):
                sp.wait_ge(zs_done, m + 1)
                for g in range(GB):
                    sp.dma_start(dr(z_d, (m * GB + g) * NCH, [[G * NCH, CH], [CH * G * NCH, L], [1, NCH]]),
                                 at(zbuf, (CH * g, CH * g + CH), Z_SSM + m * T, [[NCH, L], [1, NCH]])
                                 ).then_inc(zs_stored, 16)
                sp.wait_ge(zs_stored, 16 * GB * (m + 1))
                sp.dma_start(at(ring, ALL, R_U + m * T, [[1, T]]),
                             dr(z_d, m * T, [[G * NCH, P], [1, T]])).then_inc(u_ready[m], 16)
            sp.wait_ge(win_ps, NB)
            sp.dma_start(at(big, ALL, 0, [[DM, 4], [1, DM]]),
                         dr(A["w_out"], 0, [[DM, P], [P * DM, 4], [1, DM]])).then_inc(ld_wout0, 16)
            for hh in range(2):
                sp.wait_ge(k_done, 3 * (hh + 1))
                for q in range(4):
                    sp.dma_start(dr(k_d, (hh * 16 + q) * CH * 15 * CH,
                                    [[15 * CH, CH], [4 * CH * 15 * CH, 4], [1, 15 * CH]]),
                                 at(ring, (32 * q, 32 * q + CH), R_W + hh * 960, [[240, 4], [1, 240]])
                                 ).then_inc(k_stored, 16)
            sp.wait_ge(k_stored, 16 * 8)
            sp.wait_ge(cw_built, NB)
            for s in range(L):
                sp.dma_start(at(ring, (CH * s, CH * s + CH), R_T, [[P, G], [1, P]]),
                             dr(k_d, (L - 1 - s) * CH, [[15 * CH, CH], [CH * 15 * CH, G], [1, P]])
                             ).then_inc(toep_ready, 16)
            sp.wait_ge(tu_done, 1)
            sp.dma_start(at(ring, ALL, R_GLU, [[DP, 4], [1, DP]]),
                         dr(A["glu_w"], 0, [[DP, P], [P * DP, 4], [1, DP]])).then_inc(ld_glu, 16)
            sp.wait_ge(zp_ps, NB)
            sp.dma_start(at(big, ALL, 4 * DM, [[DM, 4], [1, DM]]),
                         dr(A["w_out"], 4 * P * DM, [[DM, P], [P * DM, 4], [1, DM]])).then_inc(ld_wout1, 16)
            sp.wait_ge(xo_re, 4)
            sp.wait_ge(xo_im, 4)
            for m in range(NB):
                sp.wait_ge(y_sb, m + 1)
                sp.dma_start(dr(y_d, m * T, [[G * NCH, P], [1, T]]),
                             at(ring, ALL, R_Y + m * T, [[1, T]])).then_inc(y_stored, 16)
                sp.wait_ge(y_stored, 16 * (m + 1))
                for g in range(GB):
                    sp.dma_start(at(ring, (CH * g, CH * g + CH), R_YC + m * T, [[NCH, L], [1, NCH]]),
                                 dr(y_d, (m * GB + g) * NCH, [[G * NCH, CH], [CH * G * NCH, L], [1, NCH]])
                                 ).then_inc(yc_ready[m], 16)
            load_expert(sp, 0, 0, w_ready[0])
            sp.dma_start(at(moe, ALL, M_PIN, [[DPLE, NT], [1, DPLE]]),
                         dr(A["p"], 0, [[DPLE, P], [P * DPLE, NT], [1, DPLE]])).then_inc(ld_ppw, 16)
            sp.dma_start(at(moe, ALL, M_PPW, [[DM, 2], [1, DM]]),
                         dr(A["ple_proj_w"], 0, [[DM, P], [P * DM, 2], [1, DM]])).then_inc(ld_ppw, 16)
            load_expert(sp, 1, 1, w_ready[1])
            sp.wait_ge(cat_done, NB)
            load_expert(sp, 2, 2, w_ready[2])
            load_expert(sp, 3, 3, w_ready[3])
            for t in range(NT):
                sp.wait_ge(v_done, t + 1)
                sp.dma_start(v_d[t * P:(t + 1) * P, :], at(big, ALL, t * DM, [[1, DM]])).then_inc(v_stored, 16)
            sp.wait_ge(v_stored, 16 * NT)
            sp.wait_ge(turned_ps, 2)
            sp.dma_start(at(big, ALL, 0, [[1, KC * DM]]),
                         dr(A["ple_gate_w"], 0, [[KC * DM, P], [1, KC * DM]])).then_inc(ld_wple, 16)
            with sp.Fori(1, NE // RING) as i:
                for u in range(RING):
                    e = sp.snap(i * RING + u)
                    free = sp.snap(i * RING + (u - RING + 1))
                    sp.wait_ge(dn_ps, free)
                    load_expert(sp, e, u, w_ready[u])
            with sp.If(most(sp) > CAP):
                with sp.Fori(1, ROUNDS) as r:
                    with sp.Fori(0, NE) as e0:
                        e = sp.snap(e0 + 0)
                        turn = sp.snap((r - 1) * NE + e0 + 1)
                        sp.wait_ge(o_turn, turn)
                        load_expert(sp, e, 0, o_w)
            with sp.Else():
                pass
            sp.wait_ge(moe_done, 1)
            sp.dma_start(at(ring, ALL, E_GF, [[1, DM]]),
                         dr(A["g_final"], 0, [[0, P], [1, DM]])).then_inc(ld_fin, 16)
            sp.dma_start(at(ring, (0, 1), E_BP, [[1, DM]]),
                         dr(A["ple_gate_b"], 0, [[DM, 1], [1, DM]])).then_inc(ld_fin, 16)
            for t in range(NT):
                if t >= 2:
                    sp.wait_ge(comb, 2 * (t - 1))
                sp.dma_start(at(ring, ALL, E_YP + (t % 2) * 2 * DM, [[1, 2 * DM]]),
                             dr(pairs_d, t * P * 2 * DM, [[2 * DM, P], [1, 2 * DM]])).then_inc(ld_pairs[t], 16)
            for t in range(NT):
                sp.wait_ge(fin_done, t + 1)
                sp.dma_start(out_d[t * P:(t + 1) * P, :], at(ring, ALL, E_O + t * DM, [[1, DM]])
                             ).then_inc(stored, 16)
            sp.wait_ge(stored, 16 * NT)

        @block.scalar
        def _(act):

            def copy(o, i, signal):
                act.activation(o, i, ACT.Copy).then_inc(signal, 1)

            def mean_root(src, junk, ss, t, done):
                act.activation(junk, src, ACT.Square, accum_out=at(small, ALL, ss + t, [[1, 1]])).then_inc(done, 1)

            act.wait_ge(eps_set, 1)
            for t in range(NT):
                act.wait_ge(ld_x[t], 16)
                mean_root(at(h, ALL, t * DM, [[1, DM]]), at(moe, ALL, M_XN + t * DM, [[1, DM]]), S_SS, t, ss_done)
            act.wait_ge(ss_done, NT)
            act.activation(at(small, ALL, S_RS, [[1, NT]]), at(small, ALL, S_SS, [[1, NT]]), ACT.Sqrt,
                           bias=at(small, ALL, S_EPS, [[1, 1]]), scale=1.0 / DM).then_inc(rms_root, 1)
            act.wait_ge(ld_small, 64)
            act.activation(at(ring, (0, G), R_LAM + 2 * P + 2, [[1, 2]]), at(ring, (0, G), R_LAM + 2 * P, [[1, 2]]),
                           ACT.Exp).then_inc(lam_dt, 1)
            act.wait_ge(lam_arg, 1)
            act.activation(lam(4), lam(3), ACT.Exp).then_inc(lam_exp, 1)
            act.wait_ge(turned_ps, 1)
            act.wait_ge(ld_vec, 96)
            for j in range(KC):
                act.activation(at(ut, ALL, j * T, [[1, T]]), bank[j][:, :], ACT.Copy, scale=vcol(V_MIX + j)
                               ).then_inc(ut_done, 1)
            act.wait_ge(c_ps, 1)
            act.activation(at(ring, ALL, R_CL, [[1, 512]]), bank[4][:, :], ACT.Copy).then_inc(c_done, 1)
            act.activation(at(ring, ALL, R_CL + 512, [[1, 512]]), bank[5][:, :], ACT.Copy, scale=-1.0
                           ).then_inc(c_done, 1)
            act.activation(at(vec, ALL, V_POOL, [[1, 12]]), bank[6][:, 0:12], ACT.Copy).then_inc(vec_done, 1)
            act.wait_ge(lam_red, 1)
            act.activation(lam(8), lam(7), ACT.Sin).then_inc(lam_sin, 1)
            act.activation(lam(9), lam(7), ACT.Sin, scale=0.5).then_inc(lam_sin, 1)

            def zs_out(m):
                act.wait_ge(win_ps, m + 1)
                copy(at(zbuf, ALL, Z_SSM + m * T, [[1, NCH], [NCH, L]]),
                     at(bank[m], ALL, 0, [[L, NCH], [1, L]]), zs_done)

            zs_out(0)
            zs_out(1)
            act.wait_ge(lam_ps, 1)
            copy(at(ring, ALL, R_PW + G, [[9 * G, 2], [1, G]]), at(bank[6], ALL, 128, [[G, 2], [1, G]]), lam_lane)
            copy(at(ring, ALL, R_COEF, [[1, 2 * G]]), bank[6][:, 192:256], lam_lane)
            zs_out(2)
            zs_out(3)
            act.wait_ge(pow_done, 1)
            for ri in range(2):
                pw, pin, pc = R_PW + ri * 9 * G, R_PIN + ri * 8 * G, R_PC + ri * 9 * G
                copy(at(ring, FWD, pin, [[G, L], [1, G]]), at(ring, FWD, pw + 7 * G, [[-G, L], [1, G]]), pin_done)
                copy(at(ring, BWD, pin, [[1, L * G]]), at(ring, BWD, pw, [[1, L * G]]), pin_done)
                copy(at(ring, FWD, pc, [[1, 9 * G]]), at(ring, FWD, pw, [[1, 9 * G]]), pin_done)
                copy(at(ring, BWD, pc, [[1, G]]), at(ring, BWD, pw, [[1, G]]), pin_done)
                copy(at(ring, BWD, pc + G, [[G, 8], [1, G]]), at(ring, BWD, pw + 8 * G, [[-G, 8], [1, G]]), pin_done)
            for b in range(NB):
                act.wait_ge(wt_ps, b + 1)
                if b >= 2:
                    act.wait_ge(e_ps, b - 1)
                for k in range(4):
                    copy(at(moe, ALL, M_WT + (b % 2) * 2048 + k * 512, [[1, 512]]), bank[4 + k][:, :], wt_done)
                act.wait_ge(e_ps, b + 1)
                for ri in range(2):
                    src = bank[2 * (b % 2) + ri]
                    copy(at(ring, FWD, R_X + 64 + ri * G + b * GB, [[1, GB], [64, NCH]]),
                         at(src, FWD, 0, [[NCH, GB], [1, NCH]]), e_done)
                    copy(at(ring, BWD, R_X + 64 * NCH + ri * G + b * GB, [[1, GB], [-64, NCH]]),
                         at(src, BWD, 0, [[NCH, GB], [1, NCH]]), e_done)
            act.wait_ge(wt_ps, NB)
            for hh in range(2):
                act.wait_ge(k_ps, hh + 1)
                for src, off, n in ((5, 0, 112), (6, 112, 16), (4, 128, 112)):
                    copy(at(ring, ALL, R_W + hh * 960 + off, [[240, 4], [1, n]]),
                         at(bank[src], ALL, 0, [[n, 4], [1, n]]), k_done)
            for m in range(4):
                act.wait_ge(zp_ps, m + 1)
                copy(at(zbuf, ALL, Z_POOL + m * PW_ + PAD, [[1, T]]), bank[4 + m][:, :], zp_done)
            for m in range(4):
                act.wait_ge(a_ps, m + 1)
                act.activation(at(ut, ALL, m * T, [[1, T]]), bank[4 + m][:, :], ACT.Copy, scale=vcol(V_POOL + m)
                               ).then_inc(a_done, 1)
            for n in range(2 * NT):
                act.wait_ge(wo0_ps, n + 1)
                least(act, wo0_done, n - 1)
                copy(at(moe, ALL, M_PT + (n % 2) * 512, [[1, 512]]), bank[4 + n % 4][:, :], wo0_sb)
            act.wait_ge(scan_b, NCH - 1)
            for gh in range(2):
                copy(at(moe, FWD, M_XO + gh * 16 * NCH, [[NCH, 16], [1, NCH]]),
                     at(ring, FWD, R_X + gh * 16, [[1, 16], [64, NCH]]), xo_re)
                copy(at(moe, BWD, M_XO + gh * 16 * NCH, [[NCH, 16], [1, NCH]]),
                     at(ring, BWD, R_X + 64 * (NCH - 1) + gh * 16, [[1, 16], [-64, NCH]]), xo_re)
            act.wait_ge(tu_done, 1)
            for b in range(NB):
                act.wait_ge(y_ps, b + 1)
                copy(at(ring, ALL, R_Y + b * T, [[1, T]]), bank[b][:, :], y_sb)
            for m in range(NB):
                act.wait_ge(yd_done, m + 1)
                act.activation(at(ring, ALL, R_ZG + m * T, [[1, T]]), at(ring, ALL, R_YC + m * T, [[1, T]]),
                               ACT.Gelu_apprx_tanh).then_inc(zg_done, 1)
            for m in range(NB):
                act.wait_ge(glu_ps, m + 1)
                act.activation(at(ring, ALL, R_YC + m * T, [[1, T]]), bank[4 + m][:, :], ACT.Sigmoid,
                               bias=vcol(V_GLU + m)).then_inc(gate_done, 1)
            for t in range(NT):
                act.wait_ge(h_done, 2 * (t + 1))
                mean_root(at(h, ALL, t * DM, [[1, DM]]), at(big, ALL, t * DM, [[1, DM]]), S_SS2, t, ss_done)
            act.wait_ge(ss_done, 2 * NT)
            act.activation(at(small, ALL, S_RS2, [[1, NT]]), at(small, ALL, S_SS2, [[1, NT]]), ACT.Sqrt,
                           bias=at(small, ALL, S_EPS, [[1, 1]]), scale=1.0 / DM).then_inc(rms_root, 1)
            for j in range(KC):
                act.wait_ge(turned_ps, 2)
                act.activation(at(ut, ALL, j * T, [[1, T]]), bank[j][:, :], ACT.Copy, scale=vcol(V_FFN + j)
                               ).then_inc(ut_done, 1)
            act.wait_ge(d4_done, 1)
            act.activation(at(ut, ALL, Q["e4"], [[1, NT * 4]]), at(ut, ALL, Q["d4"], [[1, NT * 4]]), ACT.Exp
                           ).then_inc(ex_done, 1)
            act.wait_ge(df_done, 1)
            act.activation(at(ut, ALL, Q["ex"], [[1, NT]]), at(ut, ALL, Q["df"], [[1, NT]]), ACT.Exp
                           ).then_inc(ex_done, 1)
            act.wait_ge(ppt_ps, 1)
            for j in range(2):
                copy(at(moe, ALL, M_PPT + j * T, [[1, T]]), bank[1 + j][:, :], ppt_sb)
            for n in range(2 * NT):
                act.wait_ge(pp_ps, n + 1)
                copy(at(zbuf, ALL, n * 512, [[1, 512]]), bank[3 + n % 4][:, :], pp_done)

            def silu(i, u):
                e = i * RING + u
                act.wait_ge(gu_ps, e + 1)
                least(act, hg_sb, 2 * e)
                act.activation(at(moe, (0, CAP), M_SG, [[1, DE]]), at(bank[1 + u % 2], (0, CAP), 0, [[1, DE]]),
                               ACT.Silu).then_inc(sg_sb, 1)

            def y_out(i, u):
                if not valid(i, u):
                    return
                act.wait_ge(dn_ps, i * RING + u + 1)
                least(act, ys_stored[u % 2], i * 32 + 16 * (u // 2))
                copy(at(moe, ALL, M_Y + (u % 2) * 512, [[1, 512]]), bank[4 + u % 2][:, :], dn_sb)

            def step(i, u):
                silu(i, u)
                y_out(*shift(i, u, -1))

            sweep(act, step)
            y_out(NE // RING - 1, RING - 1)
            with act.If(most(act) > CAP):
                act.wait_ge(dn_sb, NE)
                with act.Fori(1, ROUNDS) as r:
                    with act.Fori(0, NE) as e:
                        turn = act.snap((r - 1) * NE + e + 1)
                        act.wait_ge(o_gu, turn)
                        act.activation(at(moe, (0, CAP), M_SG, [[1, DE]]), at(bank[1], (0, CAP), 0, [[1, DE]]),
                                       ACT.Silu).then_inc(o_sg, 1)
                        act.wait_ge(o_dn, turn)
                        copy(at(moe, ALL, M_Y, [[1, 512]]), bank[4][:, :], o_dn_sb)
            with act.Else():
                pass
            for t in range(NT):
                act.wait_ge(comb, 2 * (t + 1))
                mean_root(at(h, ALL, t * DM, [[1, DM]]), at(ring, ALL, E_RN + t * DM, [[1, DM]]), S_SS3, t, ss_done)
                act.wait_ge(ss_done, 2 * NT + t + 1)
                act.activation(at(small, ALL, S_RS3 + t, [[1, 1]]), at(small, ALL, S_SS3 + t, [[1, 1]]), ACT.Sqrt,
                               bias=at(small, ALL, S_EPS, [[1, 1]]), scale=1.0 / DM).then_inc(rms_root, 1)
            act.wait_ge(turned_ps, 3)
            for j in range(KC):
                act.activation(at(ut, ALL, j * T, [[1, T]]), bank[j][:, :], ACT.Copy, scale=vcol(V_PLE + j)
                               ).then_inc(ut_done, 1)
            for n in range(2 * NT):
                act.wait_ge(gate_ps, n + 1)
                act.activation(at(ring, ALL, E_SG + n * 512, [[1, 512]]), bank[n % 8][:, :], ACT.Sigmoid
                               ).then_inc(gate_sb, 1)
            for t in range(NT):
                act.wait_ge(gated, 2 * (t + 1))
                mean_root(at(h, ALL, t * DM, [[1, DM]]), at(ring, ALL, E_SG + t * DM, [[1, DM]]), S_SS4, t, ss_done)
            act.wait_ge(ss_done, 4 * NT)
            act.activation(at(small, ALL, S_RS4, [[1, NT]]), at(small, ALL, S_SS4, [[1, NT]]), ACT.Sqrt,
                           bias=at(small, ALL, S_EPS, [[1, 1]]), scale=1.0 / DM).then_inc(rms_root, 1)

        @block.vector
        def _(dve):
            own = Chain(dve, dve_step)

            def tt(o, a, b, op):
                return dve.tensor_tensor(o, a, b, op)

            def seq(ins):
                own.do(ins)
                own.settle()

            def inverse(col, n, count):
                dve.wait_ge(rms_root, count)
                o = at(small, ALL, col, [[1, n]])
                dve.reciprocal(o, o).then_inc(rstd_done, 1)
                dve.wait_ge(rstd_done, count)

            def normalise(dst, base, t, col):
                return dve.tensor_scalar(at(dst, ALL, base + t * DM, [[1, P], [P, KC]]),
                                         at(h, ALL, t * DM, [[KC, P], [1, KC]]),
                                         at(small, ALL, col + t, [[1, 1]]), None, ALU.mult)

            dve.memset(at(small, ALL, S_EPS, [[1, 1]]), EPS).then_inc(eps_set, 1)
            inverse(S_RS, NT, 1)
            for t in range(NT):
                normalise(moe, M_XN, t, S_RS).then_inc(xn_done, 1)
            gdn = [[NS, 2], [1, NS]]
            are, aim, dt = lam(0), lam(1), at(ring, (0, G), R_LAM + 2 * P + 2, [[1, 2], [0, NS]])

            def lam3(k):
                return at(ring, (0, G), R_LAM + k * P, gdn)

            dve.wait_ge(lam_dt, 1)
            tt(lam3(3), lam3(0), dt, ALU.mult).then_inc(lam_arg, 1)
            seq(tt(lam3(5), lam3(1), dt, ALU.mult))
            seq(dve.tensor_scalar(lam(6), lam(5), 1.0 / TWO_PI, ROUND, ALU.mult, ALU.add))
            seq(dve.tensor_scalar(lam(6), lam(6), ROUND, None, ALU.subtract))
            seq(dve.scalar_tensor_tensor(lam(5), lam(6), -TP1, lam(5), ALU.mult, ALU.add))
            seq(dve.scalar_tensor_tensor(lam(5), lam(6), -TP2, lam(5), ALU.mult, ALU.add))
            seq(dve.scalar_tensor_tensor(lam(5), lam(6), -TP3, lam(5), ALU.mult, ALU.add))
            dve.tensor_scalar(lam(7), lam(5), PI_LO, -PI_LO, ALU.min, ALU.max).then_inc(lam_red, 1)
            seq(tt(lam(10), are, are, ALU.mult))
            seq(tt(lam(11), aim, aim, ALU.mult))
            seq(tt(lam(10), lam(10), lam(11), ALU.add))
            seq(dve.reciprocal(lam(10), lam(10)))
            dve.wait_ge(lam_sin, 2)
            seq(tt(lam(9), lam(9), lam(9), ALU.mult))
            seq(dve.tensor_scalar(lam(9), lam(9), -2.0, 1.0, ALU.mult, ALU.add))
            dve.wait_ge(lam_exp, 1)
            seq(tt(lam(12), lam(4), lam(9), ALU.mult))
            seq(tt(lam(13), lam(4), lam(8), ALU.mult))
            seq(dve.tensor_scalar(lam(5), lam(12), 1.0, None, ALU.subtract))
            seq(tt(lam(6), lam(5), are, ALU.mult))
            seq(tt(lam(7), lam(13), aim, ALU.mult))
            seq(tt(lam(6), lam(6), lam(7), ALU.add))
            seq(tt(lam(14), lam(6), lam(10), ALU.mult))
            seq(tt(lam(6), lam(13), are, ALU.mult))
            seq(tt(lam(7), lam(5), aim, ALU.mult))
            seq(tt(lam(6), lam(6), lam(7), ALU.subtract))
            tt(lam(15), lam(6), lam(10), ALU.mult).then_inc(lam_done, 1)

            def grid(off, dims):
                return at(ring, ALL, off, dims)

            dve.wait_ge(lam_lane, 2)
            pr, pi = R_PW, R_PW + 9 * G
            own.do(dve.memset(grid(pr, [[1, G]]), 1.0))
            own.do(dve.memset(grid(pi, [[1, G]]), 0.0))
            for lo, n in ((1, 1), (1, 2), (1, 4)):
                by = lo + n - 1
                rng, cst_ = [[G, n], [1, G]], [[0, n], [1, G]]
                src_r, src_i = grid(pr + lo * G, rng), grid(pi + lo * G, rng)
                by_r, by_i = grid(pr + by * G, cst_), grid(pi + by * G, cst_)
                dst_r, dst_i = grid(pr + (by + 1) * G, rng), grid(pi + (by + 1) * G, rng)
                tmp_r, tmp_i = grid(R_TMP, rng), grid(R_TMP + n * G, rng)
                own.settle()
                own.do(tt(dst_r, src_r, by_r, ALU.mult))
                own.do(tt(tmp_r, src_i, by_i, ALU.mult))
                own.do(tt(dst_i, src_r, by_i, ALU.mult))
                own.do(tt(tmp_i, src_i, by_r, ALU.mult))
                own.settle()
                own.do(tt(dst_r, dst_r, tmp_r, ALU.subtract))
                ins = tt(dst_i, dst_i, tmp_i, ALU.add)
                if n < 4:
                    own.do(ins)
                else:
                    ins.then_inc(pow_done, 1)
            dve.wait_ge(pow_done, 1)
            own.settle()
            own.do(dve.tensor_copy(at(small, ALL, S_A2, [[G, 2], [1, G]]), grid(pr + 8 * G, [[0, 2], [1, G]])))
            own.do(dve.tensor_copy(at(small, ALL, S_A2 + 2 * G, [[1, G]]), grid(pi + 8 * G, [[1, G]])))
            own.do(dve.tensor_scalar(at(small, ALL, S_A2 + 3 * G, [[1, G]]), grid(pi + 8 * G, [[1, G]]), -1.0, None, ALU.mult))
            dve.wait_ge(ld_b, 64)
            gc = [[CH, G], [1, CH]]
            cr, ci = grid(R_COEF, [[1, G], [0, CH]]), grid(R_COEF + G, [[1, G], [0, CH]])
            br, bi = grid(R_BRAW, gc), grid(R_BRAW + 512, gc)
            own.do(dve.memset(grid(R_BB + 512, [[1, 16]]), 0.0))
            own.do(dve.memset(grid(R_BBI + 512, [[1, 16]]), 0.0))
            own.do(tt(grid(R_BB, gc), cr, br, ALU.mult))
            own.do(tt(grid(R_TMP, gc), ci, bi, ALU.mult))
            own.do(tt(grid(R_BBI, gc), cr, bi, ALU.mult))
            own.do(tt(grid(R_TMP + 512, gc), ci, br, ALU.mult))
            own.settle()
            own.do(tt(grid(R_BB, gc), grid(R_BB, gc), grid(R_TMP, gc), ALU.subtract))
            own.do(tt(grid(R_BBI, gc), grid(R_BBI, gc), grid(R_TMP + 512, gc), ALU.add))
            dve.wait_ge(pin_done, 10)
            for b in range(NB):
                if b:
                    dve.wait_ge(wt_ps, b)
                for hb in range(2):
                    g0 = b * GB + hb * 4
                    gsc = [[P, 4], [CH, L], [1, CH]]
                    pw_r = grid(R_PIN + g0, [[1, 4], [G, L], [0, CH]])
                    pw_i = grid(R_PIN + L * G + g0, [[1, 4], [G, L], [0, CH]])
                    b_r = grid(R_BB + g0 * CH, [[CH, 4], [0, L], [1, CH]])
                    b_i = grid(R_BBI + g0 * CH, [[CH, 4], [0, L], [1, CH]])
                    w_r, w_i = grid(R_W + hb * 512, gsc), grid(R_W + 1024 + hb * 512, gsc)
                    t_r, t_i = grid(R_TMP, gsc), grid(R_TMP + 512, gsc)
                    own.settle()
                    own.do(tt(w_r, pw_r, b_r, ALU.mult))
                    own.do(tt(t_r, pw_i, b_i, ALU.mult))
                    own.do(tt(w_i, pw_r, b_i, ALU.mult))
                    own.do(tt(t_i, pw_i, b_r, ALU.mult))
                    own.settle()
                    own.do(tt(w_r, w_r, t_r, ALU.subtract))
                    tt(w_i, w_i, t_i, ALU.add).then_inc(w_built, 1)
                    dve.wait_ge(w_built, 2 * b + hb + 1)
            dve.wait_ge(c_done, 2)
            for b in range(NB):
                g0 = b * GB
                gsc = [[9 * CH, GB], [CH, 9], [1, CH]]
                pw_r = grid(R_PC + g0, [[1, GB], [G, 9], [0, CH]])
                pw_i = grid(R_PC + 9 * G + g0, [[1, GB], [G, 9], [0, CH]])
                c_r = grid(R_CL + g0 * CH, [[CH, GB], [0, 9], [1, CH]])
                c_n = grid(R_CL + 512 + g0 * CH, [[CH, GB], [0, 9], [1, CH]])
                o_r, o_n = grid(R_CW + g0 * 9 * CH, gsc), grid(R_CWN + g0 * 9 * CH, gsc)
                tmp = grid(R_TMP, gsc)
                own.settle()
                own.do(tt(o_r, pw_r, c_r, ALU.mult))
                own.do(tt(tmp, pw_i, c_n, ALU.mult))
                own.settle()
                own.do(tt(o_r, o_r, tmp, ALU.add))
                own.do(tt(o_n, pw_r, c_n, ALU.mult))
                own.settle()
                own.do(tt(tmp, pw_i, c_r, ALU.mult))
                own.settle()
                tt(o_n, o_n, tmp, ALU.subtract).then_inc(cw_built, 1)
                dve.wait_ge(cw_built, b + 1)
            dve.memset(grid(R_X, [[1, 64]]), 0.0).then_inc(x_zero, 1)
            dve.wait_ge(e_done, 16)
            a_re2, a_im2 = at(small, ALL, S_A2, [[G, 2], [1, G]]), at(small, ALL, S_A2 + 2 * G, [[G, 2], [1, G]])
            t1, t2 = at(small, ALL, S_T1, [[G, 2], [1, G]]), at(small, ALL, S_T2, [[G, 2], [1, G]])
            UNROLL = 9

            def scan_step(n):
                prev, new = R_X + n * 64 + 64, R_X + n * 64 + 128
                tt(t1, a_re2, grid(prev, [[G, 2], [1, G]]), ALU.mult).then_inc(scan_a, 1)
                tt(t2, a_im2, grid(prev, [[G, 2], [1, G]]), ALU.mult).then_inc(scan_a, 1)
                dve.wait_ge(scan_a, n * 3 + 1)
                tt(grid(new, [[1, 2 * G]]), grid(new, [[1, 2 * G]]), at(small, ALL, S_T1, [[1, 2 * G]]),
                   ALU.add).then_inc(scan_a, 1)
                dve.wait_ge(scan_a, n * 3 + 3)
                tt(grid(new, [[G, 2], [1, G]]), grid(new, [[G, 2], [1, G]]),
                   at(small, ALL, S_T2 + G, [[-G, 2], [1, G]]), ALU.add).then_inc(scan_b, 1)
                dve.wait_ge(scan_b, n + 1)

            assert (NCH - 1) % UNROLL == 0
            with dve.Fori(0, (NCH - 1) // UNROLL) as i:
                for u in range(UNROLL):
                    scan_step(i * UNROLL + u)
            for gh in range(2):
                dve.tensor_copy(at(moe, FWD, M_XO + 2048 + gh * 16 * NCH, [[NCH, 16], [1, NCH]]),
                                at(ring, FWD, R_X + G + gh * 16, [[1, 16], [64, NCH]])).then_inc(xo_im, 1)
                dve.tensor_copy(at(moe, BWD, M_XO + 2048 + gh * 16 * NCH, [[NCH, 16], [1, NCH]]),
                                at(ring, BWD, R_X + 64 * (NCH - 1) + G + gh * 16, [[1, 16], [-64, NCH]])
                                ).then_inc(xo_im, 1)
            for m in range(NB):
                dve.wait_ge(yc_ready[m], 16 * GB)
                yc = at(ring, ALL, R_YC + m * T, [[1, T]])
                dve.scalar_tensor_tensor(yc, at(zbuf, ALL, Z_SSM + m * T, [[1, T]]), vcol(V_D + m), yc,
                                         ALU.mult, ALU.add).then_inc(yd_done, 1)
            for m in range(NB):
                dve.wait_ge(gate_done, m + 1)
                tt(at(ut, ALL, (4 + m) * T, [[1, L], [L, NCH]]), at(ring, ALL, R_ZG + m * T, [[NCH, L], [1, NCH]]),
                   at(ring, ALL, R_YC + m * T, [[NCH, L], [1, NCH]]), ALU.mult).then_inc(cat_done, 1)
            dve.wait_ge(wo0_done, 2 * NT)
            for n in range(2 * NT):
                dve.wait_ge(wo1_ps, n + 1)
                hv = at(h, ALL, n * 512, [[1, 512]])
                tt(hv, bank[n % 8][:, :], hv, ALU.add).then_inc(h_done, 1)
            inverse(S_RS2, NT, 2)
            for t in range(NT):
                normalise(big, 0, t, S_RS2).then_inc(v_done, 1)

            def qv(name, dims, off=0):
                return at(ut, ALL, Q[name] + off, dims)

            def cv(off, dims):
                return at(cst, ALL, off, dims)

            def peak(o, i, op=ALU.max):
                seq(dve.tensor_reduce(o, i, AX.X, op))

            one, four, eight = [[1, NT]], [[4, NT], [1, 4]], [[NEG, NT], [1, NEG]]
            tge = [[NE, NT], [NEG, NG], [1, NEG]]
            dve.wait_ge(log_ps, NT)
            seq(dve.tensor_copy(qv("L", [[1, NT * 36]]), bank[0][:, 0:NT * 36]))
            peak(qv("gm", one), qv("L", [[36, NT], [1, 4]]))
            tt(qv("d4", four), qv("L", [[36, NT], [1, 4]]), qv("gm", [[1, NT], [0, 4]]), ALU.subtract
               ).then_inc(d4_done, 1)
            dve.wait_ge(d4_done, 1)
            seq(dve.scalar_tensor_tensor(qv("g1", four), qv("d4", four), 0.0, cv(C_LOW, [[0, NT], [1, 4]]),
                                         ALU.is_equal, ALU.mult))
            peak(qv("g2", one), qv("g1", four))
            seq(tt(qv("goh", four), qv("g1", four), qv("g2", [[1, NT], [0, 4]]), ALU.is_equal))
            seq(tt(qv("pr", tge), qv("goh", [[4, NT], [1, 4], [0, NEG]]), qv("L", [[36, NT], [NEG, NG], [1, NEG]], 4),
                   ALU.mult))
            peak(qv("sel", eight), qv("pr", [[NE, NT], [1, NEG], [NEG, NG]]), ALU.add)

            def first_best(src, best, a, b, hot):
                peak(qv(best, one), qv(src, eight))
                seq(tt(qv(a, eight), qv(src, eight), qv(best, [[1, NT], [0, NEG]]), ALU.is_equal))
                seq(tt(qv(a, eight), qv(a, eight), cv(C_LOW, [[0, NT], [1, NEG]]), ALU.mult))
                peak(qv(b, one), qv(a, eight))
                seq(tt(qv(hot, eight), qv(a, eight), qv(b, [[1, NT], [0, NEG]]), ALU.is_equal))

            first_best("sel", "m1", "q1", "q2", "oh1")
            seq(dve.scalar_tensor_tensor(qv("s2", eight), qv("oh1", eight), -3.0e38, qv("sel", eight),
                                         ALU.mult, ALU.add))
            first_best("s2", "m2", "q3", "q4", "oh2")
            tt(qv("df", one), qv("m2", one), qv("m1", one), ALU.subtract).then_inc(df_done, 1)
            for k in (1, 2):
                own.do(tt(qv(f"M{k}", tge), qv("goh", [[4, NT], [1, 4], [0, NEG]]),
                          qv(f"oh{k}", [[NEG, NT], [0, NG], [1, NEG]]), ALU.mult))
            own.settle()
            tt(qv("MS", [[1, NT * NE]]), qv("M1", [[1, NT * NE]]), qv("M2", [[1, NT * NE]]), ALU.add
               ).then_inc(mask_done, 1)
            dve.wait_ge(ex_done, 2)
            peak(qv("gs", one), qv("e4", four), ALU.add)
            seq(dve.reciprocal(qv("gp", one), qv("gs", one)))
            seq(dve.tensor_scalar(qv("dn", one), qv("ex", one), 1.0, None, ALU.add))
            seq(dve.reciprocal(qv("dn", one), qv("dn", one)))
            seq(tt(at(small, ALL, S_W1, one), qv("gp", one), qv("dn", one), ALU.mult))
            seq(tt(at(small, ALL, S_W2, one), at(small, ALL, S_W1, one), qv("ex", one), ALU.mult))
            dve.wait_ge(rank_ps, 1)
            te = [[NE, NT], [1, NE]]
            for k in (1, 2):
                seq(tt(qv("pa", te), qv(f"M{k}", te), at(bank[7], ALL, 0, te), ALU.mult))
                peak(qv(f"r{k}", one), qv("pa", te), ALU.add)
                seq(tt(qv("pb", te), qv(f"M{k}", te), cv(C_NUM, [[0, NT], [1, NE]]), ALU.mult))
                peak(qv(f"e{k}", one), qv("pb", te), ALU.add)
                seq(dve.scalar_tensor_tensor(at(slot_i, ALL, k - 1, [[2, NT]]), qv(f"r{k}", one), float(NE),
                                             qv(f"e{k}", one), ALU.mult, ALU.add))
            dve.tensor_reduce(at(flag, ALL, 0, [[1, 1]]), at(bank[7], ALL, NT * NE, [[1, NE]]), AX.X, ALU.max
                              ).then_inc(slot_done, 1)

            def tokens(o, table, done):
                dve.tensor_scalar(o, table, 1, None, ALU.logical_shift_right).then_inc(done, 1)

            def half_rows(o, table, done):
                dve.tensor_scalar(o, table, 2.0, cv(C_HALF, [[1, 1]]), ALU.mult, ALU.add).then_inc(done, 1)

            dve.wait_ge(tbl_read, 32)
            for n, parts in enumerate(((0, CAP), (CAP, P))):
                tokens(at(gidx_all, parts, 0, [[1, NE // 2]]), at(tblw, parts, n, [[2, NE // 2]]), idx_done)
            half_rows(at(sidx_all, ALL, 0, [[1, NE]]), at(tblw, ALL, 0, [[1, NE]]), idx_done)

            def x_out(k, signal):
                for n in range(2):
                    tt(at(moe, ALL, M_XT + k * DM + n * 512, [[P, 4], [1, P]]), at(bank[n * 6], ALL, 0, [[P, 4], [1, P]]),
                       at(vec, ALL, V_FFN + 4 * n, [[1, 4], [0, P]]), ALU.mult).then_inc(signal, 1)

            def hidden(src, signal):
                for j in range(2):
                    tt(at(moe, (j * CAP, j * CAP + CAP), M_HG, [[1, P]]), at(moe, (0, CAP), M_SG + j, [[2, P]]),
                       at(src, (CAP, P), j, [[2, P]]), ALU.mult).then_inc(signal, 1)

            def x_step(i, u):
                if not valid(i, u) or u % 2:
                    return
                e = i * RING + u
                dve.wait_ge(xT_ps, i * 2 + u // 2 + 1)
                least(dve, gu_ps, e - 2)
                x_out(u // 2, xT_sb)

            def step(i, u):
                e = i * RING + u
                dve.wait_ge(sg_sb, e + 1)
                least(dve, hT_ps, e)
                hidden(bank[1 + u % 2], hg_sb)
                x_step(*shift(i, u, 1))
                dve.wait_ge(hT_ps, e + 1)
                least(dve, dn_ps, e - 1)
                dve.tensor_copy(at(moe, ALL, M_HT + (u % 2) * P, [[1, P]]), bank[3][:, 0:P]).then_inc(hT_sb, 1)

            dve.wait_ge(pp_ps, 2 * NT)
            x_step(0, 0)
            sweep(dve, step)
            with dve.If(most(dve) > CAP):
                with dve.Fori(1, ROUNDS) as r:
                    with dve.Fori(0, NE) as e:
                        turn = dve.snap((r - 1) * NE + e + 1)
                        twice = dve.snap(turn * 32)
                        dve.wait_ge(o_tbl, twice)
                        tokens(at(gidx[0], ALL, 0, [[1, 1]]), at(tblw, ALL, e, [[1, 1]]), o_idx)
                        half_rows(at(sidx[0], ALL, 0, [[1, 1]]), at(tblw, ALL, e, [[1, 1]]), o_idx)
                        dve.wait_ge(o_xT_ps, turn)
                        x_out(0, o_xT)
                        dve.wait_ge(o_sg, turn)
                        hidden(bank[1], o_hg)
                        dve.wait_ge(o_hT_ps, turn)
                        dve.tensor_copy(at(moe, ALL, M_HT, [[1, P]]), bank[3][:, 0:P]).then_inc(o_hT, 1)
            with dve.Else():
                pass
            for t in range(NT):
                dve.wait_ge(ld_pairs[t], 16)
                hv = at(h, ALL, t * DM, [[1, DM]])
                for k, col in enumerate((S_W1, S_W2)):
                    dve.scalar_tensor_tensor(hv, at(ring, ALL, E_YP + (t % 2) * 2 * DM + k * DM, [[1, DM]]),
                                             at(small, ALL, col + t, [[1, 1]]), hv, ALU.mult, ALU.add
                                             ).then_inc(comb, 1)
                    dve.wait_ge(comb, 2 * t + k + 1)
                inverse(S_RS3 + t, 1, 3 + t)
                normalise(ring, E_RN, t, S_RS3).then_inc(r_done, 1)
            for n in range(2 * NT):
                dve.wait_ge(gate_sb, n + 1)
                sg, hv = at(ring, ALL, E_SG + n * 512, [[1, 512]]), at(h, ALL, n * 512, [[1, 512]])
                seq(tt(sg, sg, at(zbuf, ALL, n * 512, [[1, 512]]), ALU.mult))
                tt(hv, hv, sg, ALU.add).then_inc(gated, 1)
            dve.wait_ge(ld_fin, 32)
            inverse(S_RS4, NT, 3 + NT)
            for t in range(NT):
                dve.scalar_tensor_tensor(at(ring, ALL, E_O + t * DM, [[1, DM]]), at(h, ALL, t * DM, [[1, DM]]),
                                         at(small, ALL, S_RS4 + t, [[1, 1]]), at(ring, ALL, E_GF, [[1, DM]]),
                                         ALU.mult, ALU.mult).then_inc(fin_done, 1)

        @block.gpsimd
        def _(pool):
            own = Chain(pool, pool_step)

            def seq(ins):
                own.do(ins)
                own.settle()

            own.do(pool.memset(at(gidx_all, ALL, NE // 2, [[1, 1]]), 0))
            seq(pool.memset(fill[:, :], EMPTY))
            pool.dma_start(dr(tbl_d, 0, [[P, P], [1, P]]), fill[:, :]).then_inc(tbl_filled, 16)
            pool.wait_ge(ld_c, 16)
            own.do(pool.tensor_copy(pair_i[:, :], at(cst, ALL, C_PAIR, [[1, 2 * NT]])))
            for off in (0, PAD + T):
                own.do(pool.memset(at(zbuf, ALL, Z_POOL + off, [[PW_, 4], [1, PAD]]), 0.0))
            for i, w in enumerate(WINDOWS):
                pool.wait_ge(zp_done, i + 1)
                z = Z_POOL + i * PW_
                src, base, n, k = zbuf, z, 1, 0
                own.settle()
                while n < w:
                    width = PW_ - 2 * n + 1
                    dst = M_PT + k * PW_
                    seq(pool.tensor_tensor(at(moe, ALL, dst, [[1, width]]), at(src, ALL, base, [[1, width]]),
                                           at(src, ALL, base + n, [[1, width]]), ALU.add))
                    src, base, n, k = moe, dst, 2 * n, 1 - k
                mean = M_PT + k * PW_
                seq(pool.tensor_scalar(at(moe, ALL, mean, [[1, T]]), at(moe, ALL, base + PAD - w // 2, [[1, T]]),
                                       1.0 / w, None, ALU.mult))
                for side in range(2):
                    ev = at(moe, ALL, mean + side * (T - PAD), [[1, PAD]])
                    own.do(pool.tensor_tensor(ev, ev, at(cst, ALL, C_EDGE + (2 * i + side) * PAD, [[1, PAD]]),
                                              ALU.mult))
                own.settle()
                zi = at(zbuf, ALL, z + PAD, [[1, T]])
                pool.tensor_tensor(zi, at(moe, ALL, mean, [[1, T]]), zi, ALU.subtract).then_inc(diff_done, 1)
                pool.wait_ge(diff_done, i + 1)
            for n in range(2 * NT):
                pool.wait_ge(wo0_sb, n + 1)
                hv = at(h, ALL, n * 512, [[1, 512]])
                pool.tensor_tensor(hv, hv, at(moe, ALL, M_PT + (n % 2) * 512, [[1, 512]]), ALU.add
                                   ).then_inc(wo0_done, 1)
            pool.wait_ge(wo0_done, 2 * NT)
            own.do(pool.memset(at(moe, ALL, M_XG, [[1, 2 * DM]]), 0.0))
            pool.wait_ge(slot_done, 1)
            pool.wait_ge(tbl_filled, 16)
            own.settle()
            for c in range(2 * NT):
                pool.indirect_dma_start(tbl_d, bass.IndirectOffsetOnAxis(ap=slot_i[:, c:c + 1], axis=0),
                                        pair_i[:, c:c + 1], None).then_inc(tbl_set, 16)
            pool.wait_ge(tbl_set, 16 * 2 * NT)
            for k in range(2):
                pool.dma_start(at(tblw, (k * CAP, (k + 1) * CAP), 0, [[1, NE]]),
                               dr(tbl_d, 0, [[NE, CAP], [1, NE]])).then_inc(tbl_read, 16)
            pool.wait_ge(idx_done, 3)
            pool.wait_ge(v_stored, 16 * NT)
            pairs = pairs_d

            def rows_in(k, done):
                pool.indirect_dma_start(at(moe, ALL, M_XG + k * DM, [[1, DM]]), None, v_d,
                                        bass.IndirectOffsetOnAxis(ap=gidx[k][:, 0:1], axis=0),
                                        bounds_check=T - 1, oob_is_err=False).then_inc(done, 16)

            def rows_out(k, done):
                pool.indirect_dma_start(pairs, bass.IndirectOffsetOnAxis(ap=sidx[k][:, 0:1], axis=0),
                                        at(moe, ALL, M_Y + k * 512, [[1, 512]]), None,
                                        bounds_check=4 * T - 1, oob_is_err=False).then_inc(done, 16)

            def set_gather(pair, k):
                pool.tensor_copy(gidx[k][:, 0:1], at(gidx_all, ALL, pair, [[1, 1]])).then_inc(gi_set, 1)

            def set_scatter(e, k):
                pool.tensor_copy(sidx[k][:, 0:1], at(sidx_all, ALL, e, [[1, 1]])).then_inc(si_set, 1)

            def gather(i, u):
                if not valid(i, u) or u % 2:
                    return
                q, k = i * 2 + u // 2, u // 2
                least(pool, xT_ps, q - 1)
                pool.wait_ge(gi_set, q + 1)
                if u:
                    pool.wait_ge(xg_ready[0], (i + 1) * 16)
                else:
                    least(pool, xg_ready[1], i * 16)
                set_gather(q + 1, 1 - k)
                rows_in(k, xg_ready[k])

            def scatter(i, u):
                if not valid(i, u):
                    return
                e, k = i * RING + u, u % 2
                pool.wait_ge(si_set, e + 1)
                pool.wait_ge(dn_sb, e + 1)
                if not (isinstance(i, int) and e == NE - 1):
                    least(pool, ys_stored[1 - k], i * 32 + 16 * ((u + 1) // 2))
                    set_scatter(e + 1, 1 - k)
                rows_out(k, ys_stored[k])

            def step(i, u):
                gather(*shift(i, u, 3))
                scatter(*shift(i, u, -1))

            set_gather(0, 0)
            set_scatter(0, 0)
            gather(0, 0)
            gather(0, 2)
            sweep(pool, step)
            scatter(NE // RING - 1, RING - 1)
            for k in range(2):
                pool.wait_ge(ys_stored[k], 16 * NE // 2)

            def note(k):
                return pool.tensor_tensor(at(fill, (0, 1), 4 + k, [[1, 1]]), at(fill, (0, 1), 0, [[1, 1]]),
                                          at(fill, (0, 1), 1, [[1, 1]]), ALU.add)

            with pool.If(most(pool) > CAP):
                note(3).then_inc(o_turn, 1)
                with pool.Fori(1, ROUNDS) as r:
                    with pool.Fori(0, NE) as e:
                        turn = pool.snap((r - 1) * NE + e + 1)
                        dma16 = pool.snap(turn * 16)
                        both = pool.snap(turn * 2)
                        place = pool.snap(r * (CAP * NE))
                        pool.wait_ge(o_turn, turn)
                        for k in range(2):
                            pool.dma_start(at(tblw, (k * CAP, (k + 1) * CAP), 0, [[1, NE]]),
                                           dr(tbl_d, place, [[NE, CAP], [1, NE]])).then_inc(o_tbl, 16)
                        pool.wait_ge(o_idx, both)
                        note(0)
                        rows_in(0, o_xg)
                        pool.wait_ge(o_dn_sb, turn)
                        note(1)
                        rows_out(0, o_st)
                        pool.wait_ge(o_st, dma16)
                        note(2).then_inc(o_turn, 1)
            with pool.Else():
                pass
            pool.memset(at(fill, (0, 1), 12, [[1, 1]]), 0).then_inc(moe_done, 1)

        @block.tensor
        def _(pe):
            def mm(o, a, b, start, stop, loose=False):
                return pe.matmul(o, a, b, start=start, stop=stop, skip_group_check=loose)

            def rv(off, n, parts=ALL):
                return at(ring, parts, off, [[1, n]])

            def transposed(src, base, ready):
                for t in range(NT):
                    pe.wait_ge(ready, t + 1)
                    for j in range(KC):
                        last = pe.transpose(bank[j][:, t * P:(t + 1) * P], at(src, ALL, base + t * DM + j * P, [[1, P]]),
                                            ident)
                last.then_inc(turned_ps, 1)

            def win(m, col):
                for j in range(KC):
                    last = mm(bank[m % 8][:, :], at(big, ALL, col + j * DP + (m % 4) * P, [[1, P]]),
                              at(ut, ALL, j * T, [[1, T]]), j == 0, j == KC - 1)
                return last

            pe.wait_ge(ld_c, 16)
            transposed(moe, M_XN, xn_done)
            pe.wait_ge(ld_win0, 16)
            pe.wait_ge(ut_done, KC)
            win(0, 0).then_inc(win_ps, 1)
            pe.wait_ge(ld_craw, 64)
            pe.wait_ge(ld_vec, 96)
            for ri in range(2):
                for m in range(NB):
                    pe.transpose(bank[4 + ri][:, m * P:(m + 1) * P], rv(R_CRAW + ri * 512 + m * P, P), ident)
            pe.transpose(bank[6][:, 0:12], at(vrow, (0, 12), 0, [[1, P]]), at(cst, (0, 12), C_ID, [[1, 12]])
                         ).then_inc(c_ps, 1)
            win(1, 0).then_inc(win_ps, 1)
            pe.wait_ge(lam_done, 1)
            for k, src in enumerate((12, 13, 14, 15)):
                last = pe.transpose(bank[6][:, P + k * G:P + (k + 1) * G], lam(src), ident32)
            last.then_inc(lam_ps, 1)
            win(2, 0).then_inc(win_ps, 1)
            win(3, 0).then_inc(win_ps, 1)

            def end_states(b):
                pe.wait_ge(wt_done, 4 * (b + 1))
                pe.wait_ge(u_ready[b], 16)
                pe.wait_ge(zs_done, NB)
                if b >= 2:
                    pe.wait_ge(e_done, 4 * (b - 1))
                for ri in range(2):
                    for g in range(GB):
                        last = mm(bank[2 * (b % 2) + ri][:, g * NCH:(g + 1) * NCH],
                                  at(moe, ALL, M_WT + (b % 2) * 2048 + ri * 1024 + g * P, [[1, P]]),
                                  rv(R_U + (b * GB + g) * NCH, NCH), True, True)
                last.then_inc(e_ps, 1)

            pe.wait_ge(c_done, 2)
            pe.wait_ge(vec_done, 1)
            pe.wait_ge(lam_lane, 2)
            for b in range(NB):
                pe.wait_ge(w_built, 2 * (b + 1))
                least(pe, wt_done, 4 * b)
                for ri in range(2):
                    for g in range(GB):
                        last = pe.transpose(bank[4 + 2 * ri + g // 4][:, (g % 4) * P:(g % 4 + 1) * P],
                                            rv(R_W + ri * 1024 + g * P, P), ident)
                last.then_inc(wt_ps, 1)
                end_states(b)
            pe.wait_ge(wt_done, 4 * NB)
            pe.wait_ge(cw_built, NB)
            for hh in range(2):
                least(pe, k_done, 3 * hh)
                for i in range(4):
                    for q in range(4):
                        g = hh * 16 + 4 * i + q
                        rows = slice(32 * q, 32 * q + 32)
                        for dst, parts, slot, n in ((4, FWD, 1, 112), (5, BWD, 2, 112), (6, ALL, 0, 16)):
                            for k, (b_off, c_off) in enumerate(((R_BB, R_CW), (R_BBI, R_CWN))):
                                last = mm(bank[dst][rows, i * n:(i + 1) * n], rv(b_off + g * CH, 32, parts),
                                          rv(c_off + g * 9 * CH + slot * CH, n, parts), k == 0, k == 1)
                last.then_inc(k_ps, 1)
            pe.wait_ge(toep_ready, 16 * L)
            pe.wait_ge(e_done, 4 * NB)
            for b in range(NB):
                for g in range(GB):
                    gg = b * GB + g
                    last = mm(bank[b][:, g * NCH:(g + 1) * NCH], rv(R_T + gg * P, P), rv(R_U + gg * NCH, NCH),
                              g == 0, False, True)
            last.then_inc(tu_done, 1)
            pe.wait_ge(ld_win1, 16)
            pe.wait_ge(k_done, 6)
            for m in range(4):
                win(4 + m, KC * DP).then_inc(zp_ps, 1)
            pe.wait_ge(ld_poolw, 16 * 8)
            for m in range(4):
                pe.wait_ge(diff_done, m + 1)
                pe.wait_ge(zp_done, 4)
                mm(bank[4 + m][:, :], at(moe, ALL, M_PW + m * P, [[1, P]]),
                   at(zbuf, ALL, Z_POOL + m * PW_ + PAD, [[1, T]]), True, True).then_inc(a_ps, 1)

            def wout(n, dst, chunks):
                t, half = n // 2, n % 2
                for c in chunks:
                    last = mm(bank[dst][:, :], at(ut, ALL, c * T + t * P, [[1, P]]),
                              at(big, ALL, c * DM + half * 512, [[1, 512]]), c == chunks[0], c == chunks[-1])
                return last

            pe.wait_ge(ld_wout0, 16)
            pe.wait_ge(a_done, 4)
            for n in range(2 * NT):
                least(pe, wo0_sb, n - 3)
                wout(n, 4 + n % 4, range(4)).then_inc(wo0_ps, 1)
            for b in range(NB):
                pe.wait_ge(xo_re, 2 * (b // 2 + 1))
                pe.wait_ge(xo_im, 2 * (b // 2 + 1))
                for g in range(GB):
                    gg = b * GB + g
                    for ri, c_off in enumerate((R_CW, R_CWN)):
                        last = mm(bank[b][:, g * NCH:(g + 1) * NCH], rv(c_off + gg * 9 * CH + CH, P),
                                  at(moe, ALL, M_XO + ri * 2048 + gg * NCH, [[1, NCH]]), False,
                                  g == GB - 1 and ri == 1, True)
                last.then_inc(y_ps, 1)
            pe.wait_ge(ld_glu, 16)
            pe.wait_ge(wo0_sb, 2 * NT)
            for m in range(NB):
                for c in range(NB):
                    pe.wait_ge(zg_done, c + 1)
                    last = mm(bank[4 + m][:, :], rv(R_GLU + c * DP + m * P, P), rv(R_ZG + c * T, T),
                              c == 0, c == NB - 1)
                last.then_inc(glu_ps, 1)
            pe.wait_ge(ld_wout1, 16)
            pe.wait_ge(cat_done, NB)
            pe.wait_ge(y_sb, NB)
            for n in range(2 * NT):
                wout(n, n % 8, range(4, 8)).then_inc(wo1_ps, 1)
            pe.wait_ge(h_done, 2 * NT)
            transposed(big, 0, v_done)
            pe.wait_ge(ld_poolw, 16 * 8)
            pe.wait_ge(ut_done, 2 * KC)
            for t in range(NT):
                dst = bank[0][:, t * 36:(t + 1) * 36]
                for j in range(KC):
                    mm(dst, at(ut, ALL, j * T + t * P, [[1, P]]), at(rw, ALL, j * 36, [[1, 36]]), j == 0, False)
                mm(dst, at(cst, (0, 1), C_ONE, [[1, P]]), at(rbias, (0, 1), 0, [[1, 36]]), False, True
                   ).then_inc(log_ps, 1)
            pe.wait_ge(ld_ppw, 32)
            for t in range(NT):
                for j in range(2):
                    last = pe.transpose(bank[1 + j][:, t * P:(t + 1) * P],
                                        at(moe, ALL, M_PIN + t * DPLE + j * P, [[1, P]]), ident)
            last.then_inc(ppt_ps, 1)
            pe.wait_ge(ppt_sb, 2)

            def proj(n):
                t, half = n // 2, n % 2
                least(pe, pp_done, n - 3)
                for j in range(2):
                    last = mm(bank[3 + n % 4][:, :], at(moe, ALL, M_PPT + j * T + t * P, [[1, P]]),
                              at(moe, ALL, M_PPW + j * DM + half * 512, [[1, 512]]), j == 0, j == 1)
                last.then_inc(pp_ps, 1)

            for n in range(4):
                proj(n)
            pe.wait_ge(mask_done, 1)
            for t in range(NT + 1):
                dst = bank[7][:, t * NE:(t + 1) * NE]
                for k in range(min(t + 1, NT)):
                    last = mm(dst, at(cst, ALL, C_TRI if k == t else C_ONE, [[1, P]]),
                              at(ut, ALL, Q["MS"] + k * NE, [[1, NE]]), k == 0, k == min(t, NT - 1))
            last.then_inc(rank_ps, 1)
            for n in range(4, 2 * NT):
                proj(n)
            pe.wait_ge(pp_done, 2 * NT)

            def x_rows(k):
                for j in range(KC):
                    last = pe.transpose(bank[j // 4 * 6][:, (j % 4) * P:(j % 4 + 1) * P],
                                        at(moe, ALL, M_XG + k * DM + j * P, [[1, P]]), ident)
                return last

            def gate_up(k, odd, slot, dst):
                for j in range(KC):
                    for n in range(2):
                        last = mm(bank[dst][n * CAP:(n + 1) * CAP, 0:DE],
                                  at(moe, ALL, M_XT + k * DM + j * P + odd * CAP, [[1, CAP]]),
                                  rv(slot * SLOT + n * KC * DE + j * DE, DE), j == 0, j == KC - 1)
                return last

            def h_rows():
                return pe.transpose(bank[3][:, 0:P], at(moe, ALL, M_HG, [[1, P]]), ident)

            def down(k, slot, dst):
                for j in range(2):
                    for n in range(2):
                        last = mm(bank[dst][n * CAP:(n + 1) * CAP, :], at(moe, ALL, M_HT + k * P + j * CAP, [[1, CAP]]),
                                  rv(slot * SLOT + 2 * KC * DE + j * DM + n * 512, 512), j == 0, j == 1)
                return last

            def x_step(i, u):
                if not valid(i, u) or u % 2:
                    return
                pe.wait_ge(xg_ready[u // 2], (i + 1) * 16)
                least(pe, xT_sb, i * 4 + u)
                x_rows(u // 2).then_inc(xT_ps, 1)

            def down_step(i, u):
                if not valid(i, u):
                    return
                e = i * RING + u
                pe.wait_ge(hT_sb, e + 1)
                least(pe, dn_sb, e - 1)
                down(u % 2, u, 4 + u % 2).then_inc(dn_ps, 1)

            def step(i, u):
                e = i * RING + u
                pe.wait_ge(xT_sb, i * 4 + (2 if u < 2 else 4))
                pe.wait_ge(w_ready[u], (i + 1) * 48)
                least(pe, hg_sb, 2 * (e - 1))
                gate_up(u // 2, u % 2, u, 1 + u % 2).then_inc(gu_ps, 1)
                x_step(*shift(i, u, 1))
                down_step(*shift(i, u, -1))
                pe.wait_ge(hg_sb, 2 * e + 2)
                least(pe, hT_sb, e)
                h_rows().then_inc(hT_ps, 1)

            pe.wait_ge(log_ps, NT)
            pe.wait_ge(slot_done, 1)
            x_step(0, 0)
            sweep(pe, step)
            down_step(NE // RING - 1, RING - 1)
            with pe.If(most(pe) > CAP):
                with pe.Fori(1, ROUNDS) as r:
                    with pe.Fori(0, NE) as e:
                        turn = pe.snap((r - 1) * NE + e + 1)
                        twice = pe.snap(turn * 2)
                        dma16 = pe.snap(turn * 16)
                        dma48 = pe.snap(turn * 48)
                        pe.wait_ge(o_xg, dma16)
                        x_rows(0).then_inc(o_xT_ps, 1)
                        pe.wait_ge(o_xT, twice)
                        pe.wait_ge(o_w, dma48)
                        gate_up(0, 0, 0, 1).then_inc(o_gu, 1)
                        pe.wait_ge(o_hg, twice)
                        h_rows().then_inc(o_hT_ps, 1)
                        pe.wait_ge(o_hT, turn)
                        down(0, 0, 4).then_inc(o_dn, 1)
            with pe.Else():
                pass
            pe.wait_ge(moe_done, 1)
            transposed(ring, E_RN, r_done)
            pe.wait_ge(ld_wple, 16)
            pe.wait_ge(ld_fin, 32)
            pe.wait_ge(ut_done, 3 * KC)
            for n in range(2 * NT):
                t, half = n // 2, n % 2
                dst = bank[n % 8][:, :]
                for j in range(KC):
                    mm(dst, at(ut, ALL, j * T + t * P, [[1, P]]), at(big, ALL, j * DM + half * 512, [[1, 512]]),
                       j == 0, False)
                mm(dst, at(cst, (0, 1), C_ONE, [[1, P]]), rv(E_BP + half * 512, 512, (0, 1)), False, True
                   ).then_inc(gate_ps, 1)


_INS = ["x", "p", "g_mix", "w_in", "pool_w", "pool_scale", "ssm_a_re", "ssm_a_im", "ssm_log_dt", "ssm_b_re",
        "ssm_b_im", "ssm_c_re", "ssm_c_im", "ssm_d", "glu_w", "glu_b", "w_out", "g_ffn", "router_grp_w",
        "router_grp_b", "router_exp_w", "router_exp_b", "exp_w_gate", "exp_w_up", "exp_w_down", "g_ple",
        "ple_gate_w", "ple_gate_b", "ple_proj_w", "g_final"]


def kernel(**inputs):
    import concourse.bacc as _bacc
    from concourse.bass_utils import run_bass_kernel_spmd as _run

    nc = _bacc.Bacc("TRN2", target_bir_lowering=False, num_devices=1)
    arrays, aps = {}, {}
    given = {n: inputs[n] for n in _INS}
    given["consts"] = constants()
    for name, value in given.items():
        a = np.ascontiguousarray(value)
        arrays[f"in_{name}_dram"] = a
        aps[name] = nc.dram_tensor(f"in_{name}_dram", a.shape, mybir.dt.from_np(a.dtype), kind="ExternalInput").ap()
    out = nc.dram_tensor("out_0_dram", (1, T, DM), F32, kind="ExternalOutput").ap()
    build(nc, aps, out)
    r = _run(nc, [arrays], core_ids=[0])
    return r.results[0]["out_0_dram"]
```

```python
from contextlib import ExitStack

import concourse.bass as bass
import numpy as np
from concourse import mybir

ALU = mybir.AluOpType
ACT = mybir.ActivationFunctionType
AX = mybir.AxisListType
F32 = mybir.dt.float32
I32 = mybir.dt.int32

P = 128
T = 512
DM = 1024
NT = T // P
KC = DM // P
DP = 512
WINDOWS = (2, 4, 8, 16)
PAD = 8
PW_ = T + 2 * PAD
G = 32
CH = 16
NS = 64
L = 8
NCH = T // L
GB = 8
NB = G // GB
NG = 4
NEG = 8
NE = NG * NEG
DE = 256
DPLE = 256
EPS = 1e-6
CAP = 64
ROUNDS = T // CAP
RING = 4
TWO_PI = 6.283185307179586
PI_LO = 3.1415925
TP1 = 6.28125
TP2 = 0.0019350051879882812
TP3 = TWO_PI - TP1 - TP2
ROUND = 12582912.0
EMPTY = 2 * T


def constants():
    ident = np.eye(P, dtype=np.float32)
    tri = np.triu(np.ones((P, P), np.float32), 1)
    ones = np.ones((P, P), np.float32)
    edge = np.ones((4, 2, PAD), np.float32)
    for i, w in enumerate(WINDOWS):
        for k in range(PAD):
            edge[i, 0, k] = w / (min(k - w // 2 + w, T) - max(k - w // 2, 0))
            t = T - PAD + k
            edge[i, 1, k] = w / (min(t - w // 2 + w, T) - max(t - w // 2, 0))
    edge = np.broadcast_to(edge.reshape(1, -1), (P, 64))
    number = np.broadcast_to(np.arange(NE, dtype=np.float32), (P, NE))
    lower = np.broadcast_to(np.arange(NEG, 0, -1).astype(np.float32), (P, NEG))
    pair = (2 * (np.arange(NT)[None, :, None] * P + np.arange(P)[:, None, None])
            + np.arange(2)[None, None, :]).reshape(P, 2 * NT).astype(np.float32)
    half = (np.arange(P) // CAP).astype(np.float32)[:, None]
    return np.ascontiguousarray(np.concatenate([ident, tri, ones, edge, number, lower, pair, half], 1), np.float32)


C_ID, C_TRI, C_ONE, C_EDGE, C_NUM, C_LOW, C_PAIR, C_HALF, C_END = 0, 128, 256, 384, 448, 480, 488, 496, 497


def at(t, parts, off, dims):
    p0, p1 = parts
    width = t.shape[1]
    return bass.AP(t, p0 * width + off, [[width, p1 - p0]] + [list(d) for d in dims])


def dr(a, off, dims):
    return bass.AP(a.tensor, off, [list(d) for d in dims])


def least(eng, sem, value):
    if isinstance(value, int) and value <= 0:
        return
    eng.wait_ge(sem, value)


class Chain:

    def __init__(self, eng, sem):
        self.eng, self.sem, self.n = eng, sem, 0

    def do(self, ins):
        ins.then_inc(self.sem, 1)
        self.n += 1
        return self.n

    def settle(self):
        self.eng.wait_ge(self.sem, self.n)


def build(nc, A, out):
    ctx = ExitStack()
    with ctx:
        def sb(name, width, dt=F32):
            return ctx.enter_context(nc.sbuf_tensor(name, [P, width], dt))

        def sem(name):
            return ctx.enter_context(nc.semaphore(name))

        def scratch(name, shape, dt=F32):
            return nc.dram_tensor(name, shape, dt, kind="Internal").ap()

        ALL = (0, P)
        FWD, BWD = (0, NS), (NS, P)
        SLOT = 3 * KC * DE
        ring = sb("ring", RING * SLOT)
        h = sb("h", NT * DM)
        big = sb("big", KC * DM)
        ut = sb("ut", KC * T)
        moe = sb("moe", 6144)
        zbuf = sb("zbuf", NB * T + 4 * PW_)
        cst = sb("cst", C_END)
        rw = sb("rw", KC * (NG + NE))
        vec = sb("vec", 24 + 12)
        small = sb("small", 64 + 8 * G)
        rbias = sb("rbias", NG + NE)
        logit = sb("logit", NT * (NG + NE))
        tblw = sb("tblw", NE, I32)
        gidx_all = sb("gidx_all", NE // 2 + 1, I32)
        sidx_all = sb("sidx_all", NE, I32)
        gidx = [sb(f"gidx{k}", 1, I32) for k in range(2)]
        sidx = [sb(f"sidx{k}", 1, I32) for k in range(2)]
        flag = sb("flag", 1, I32)
        slot_i = sb("slot_i", 2 * NT, I32)
        pair_i = sb("pair_i", 2 * NT, I32)
        fill = sb("fill", P, I32)
        vrow = sb("vrow", P)
        bank = [ctx.enter_context(nc.psum_tensor(f"bank{k}", [P, 512], F32)) for k in range(8)]

        V_MIX, V_FFN, V_PLE, V_POOL, V_D, V_GLU = 0, 8, 16, 24, 28, 32
        S_SS, S_RS, S_EPS, S_W1, S_W2, S_SS2, S_RS2, S_SS3, S_RS3, S_SS4, S_RS4 = (
            0, 4, 8, 12, 16, 20, 24, 28, 32, 36, 40)
        S_A2, S_T1, S_T2 = 64, 64 + 4 * G, 64 + 6 * G
        R_CW, R_CWN = 0, 4608
        R_U = 9216
        R_BB, R_BBI = R_U + 2048, R_U + 2048 + 528
        R_CL = R_BB + 1056
        R_W = R_CL + 1024
        R_T = R_W + 2048
        R_X = R_T + 4096
        R_CRAW = R_CW
        R_PW = R_T
        R_PIN = R_PW + 18 * G
        R_PC = R_PIN + 16 * G
        R_COEF = R_PC + 18 * G
        R_TMP = R_COEF + 2 * G
        R_GLU = R_T
        R_Y = R_U
        R_YC = R_X
        R_ZG = R_X + 2048
        R_LAM = R_X
        R_BRAW = R_X + 2560
        assert R_TMP + 2 * 1152 <= R_X and R_X + 65 * 64 <= RING * SLOT
        M_WT, M_XO, M_XN = 0, 0, 0
        M_PT, M_PW = 4096, 4096 + 2 * PW_
        M_PPW, M_PIN, M_PPT = 0, 2048, 3072
        M_XT, M_HG, M_SG, M_HT, M_Y, M_XG = 0, 2048, 2176, 2432, 2688, 4096
        Z_SSM, Z_POOL = 0, NB * T
        Q = {}
        q = 0
        for name, n in (("gm", NT), ("d4", NT * 4), ("e4", NT * 4), ("gs", NT), ("gp", NT),
                        ("g1", NT * 4), ("g2", NT), ("goh", NT * 4), ("pr", NT * 32), ("sel", NT * 8),
                        ("m1", NT), ("q1", NT * 8), ("q2", NT), ("oh1", NT * 8), ("s2", NT * 8), ("m2", NT),
                        ("q3", NT * 8), ("q4", NT), ("oh2", NT * 8), ("df", NT), ("ex", NT), ("dn", NT),
                        ("M1", NT * 32), ("M2", NT * 32), ("MS", NT * 32), ("rk", NT * 32), ("tot", 32),
                        ("pa", NT * 32), ("pb", NT * 32), ("r1", NT), ("r2", NT), ("e1", NT), ("e2", NT),
                        ("sf", 2 * NT), ("mx", 1)):
            Q[name] = q
            q += n
        assert q <= 4096

        z_d = scratch("z_d", [P, G * NCH])
        y_d = scratch("y_d", [P, G * NCH])
        k_d = scratch("k_d", [G * CH, 15 * CH])
        v_d = scratch("v_d", [T, DM])
        tbl_d = scratch("tbl_d", [T * NE, 1], I32)
        pairs_d = scratch("pairs_d", [4 * T, DM // 2])

        ld_c, ld_small, ld_vec, ld_win0, ld_win1, ld_b, ld_craw, ld_poolw = (
            sem(n) for n in ("ld_c", "ld_small", "ld_vec", "ld_win0", "ld_win1", "ld_b", "ld_craw", "ld_poolw"))
        ld_x = [sem(f"ld_x{t}") for t in range(NT)]
        ld_wout0, ld_wout1, ld_glu, ld_ppw, ld_wple, ld_fin = (
            sem(n) for n in ("ld_wout0", "ld_wout1", "ld_glu", "ld_ppw", "ld_wple", "ld_fin"))
        w_ready = [sem(f"w_ready{k}") for k in range(RING)]
        dve_step, pool_step = sem("dve_step"), sem("pool_step")
        ss_done, rms_root, rstd_done, turned_ps, ut_done = (
            sem(n) for n in ("ss_done", "rms_root", "rstd_done", "turned_ps", "ut_done"))
        xn_done, vec_done = sem("xn_done"), sem("vec_done")
        vec_ps, c_ps, c_done, lam_dt, lam_arg, lam_exp, lam_red, lam_sin, lam_done, lam_ps, lam_lane = (
            sem(n) for n in ("vec_ps", "c_ps", "c_done", "lam_dt", "lam_arg", "lam_exp", "lam_red", "lam_sin",
                             "lam_done", "lam_ps", "lam_lane"))
        pow_done, pin_done, pc_done = sem("pow_done"), sem("pin_done"), sem("pc_done")
        win_ps, zs_done, zs_stored = sem("win_ps"), sem("zs_done"), sem("zs_stored")
        u_ready = [sem(f"u_ready{m}") for m in range(NB)]
        yc_ready = [sem(f"yc_ready{m}") for m in range(NB)]
        w_built, wt_ps, wt_done, e_ps, e_done = (
            sem(n) for n in ("w_built", "wt_ps", "wt_done", "e_ps", "e_done"))
        cw_built, k_ps, k_done, k_stored, toep_ready, tu_done = (
            sem(n) for n in ("cw_built", "k_ps", "k_done", "k_stored", "toep_ready", "tu_done"))
        zp_ps, zp_done, diff_done, a_ps, a_done, wo0_ps, wo0_sb, wo0_done = (
            sem(n) for n in ("zp_ps", "zp_done", "diff_done", "a_ps", "a_done", "wo0_ps", "wo0_sb", "wo0_done"))
        scan_a, scan_b, xo_re, xo_im, y_ps, y_sb, y_stored = (
            sem(n) for n in ("scan_a", "scan_b", "xo_re", "xo_im", "y_ps", "y_sb", "y_stored"))
        yd_done, zg_done, glu_ps, gate_done, cat_done, wo1_ps, h_done = (
            sem(n) for n in ("yd_done", "zg_done", "glu_ps", "gate_done", "cat_done", "wo1_ps", "h_done"))
        v_done, v_stored, log_ps = sem("v_done"), sem("v_stored"), sem("log_ps")
        d4_done, df_done, ex_done, mask_done, rank_ps, slot_done, tbl_filled, tbl_set, tbl_read, idx_done = (
            sem(n) for n in ("d4_done", "df_done", "ex_done", "mask_done", "rank_ps", "slot_done",
                             "tbl_filled", "tbl_set", "tbl_read", "idx_done"))
        ppt_ps, ppt_sb, pp_ps, pp_done = sem("ppt_ps"), sem("ppt_sb"), sem("pp_ps"), sem("pp_done")
        x_zero = sem("x_zero")
        xg_ready = [sem(f"xg_ready{k}") for k in range(2)]
        ys_stored = [sem(f"ys_stored{k}") for k in range(2)]
        gi_set, si_set = sem("gi_set"), sem("si_set")
        xT_ps, xT_sb, gu_ps, sg_sb, hg_sb, hT_ps, hT_sb, dn_ps, dn_sb = (
            sem(n) for n in ("xT_ps", "xT_sb", "gu_ps", "sg_sb", "hg_sb", "hT_ps", "hT_sb", "dn_ps", "dn_sb"))
        o_w, o_tbl, o_idx, o_xg, o_xT_ps, o_xT, o_gu, o_sg, o_hg, o_hT_ps, o_hT, o_dn, o_dn_sb, o_st, o_turn = (
            sem("o_" + n) for n in ("w", "tbl", "idx", "xg", "xT_ps", "xT", "gu", "sg", "hg", "hT_ps", "hT",
                                    "dn", "dn_sb", "st", "turn"))
        moe_done, eps_set = sem("moe_done"), sem("eps_set")
        ld_pairs = [sem(f"ld_pairs{t}") for t in range(NT)]
        comb, r_done, gate_ps, gate_in, gate_sb, gated, fin_done = (
            sem(n) for n in ("comb", "r_done", "gate_ps", "gate_in", "gate_sb", "gated", "fin_done"))
        stored = sem("stored")

        ident = at(cst, ALL, C_ID, [[1, P]])
        ident32 = at(cst, (0, 32), C_ID, [[1, 32]])
        K_BANKS = ((4, 5, 6), (7, 2, 3))
        E_YP, E_RN, E_SG, E_GF, E_BP, E_O = 0, 4096, 8192, 12288, 13312, 14336

        x_d = A["x"].rearrange("b s d -> (b s) d")
        wg_d = A["exp_w_gate"].rearrange("l g e d f -> (l g e) d f")
        wu_d = A["exp_w_up"].rearrange("l g e d f -> (l g e) d f")
        wd_d = A["exp_w_down"].rearrange("l g e f d -> (l g e) f d")
        out_d = out.rearrange("b s d -> (b s) d")

        block = ctx.enter_context(nc.Block())

        def vcol(c):
            return at(vec, ALL, c, [[1, 1]])

        def lam(k):
            return at(ring, (0, G), R_LAM + k * P, [[1, P]])

        def shift(i, u, d):
            return i + (u + d) // RING, (u + d) % RING

        def valid(i, u):
            return not isinstance(i, int) or 0 <= i < NE // RING

        def sweep(eng, step):
            for u in range(RING):
                step(0, u)
            with eng.Fori(1, NE // RING - 1) as i:
                for u in range(RING):
                    step(i, u)
            for u in range(RING):
                step(NE // RING - 1, u)

        def most(eng):
            return eng.value_load(at(flag, (0, 1), 0, [[1, 1]]), min_val=0, max_val=T)

        def load_expert(eng, e, slot, done):
            base = slot * SLOT
            for n, w in enumerate((wg_d, wu_d)):
                eng.dma_start(at(ring, ALL, base + n * KC * DE, [[1, KC * DE]]),
                              w[e].rearrange("(p j) f -> p (j f)", p=P)).then_inc(done, 16)
            eng.dma_start(at(ring, ALL, base + 2 * KC * DE, [[1, 2 * DM]]),
                          wd_d[e].rearrange("(p j) d -> p (j d)", p=P)).then_inc(done, 16)

        @block.sync
        def _(sp):
            sp.dma_start(cst[:, :], A["consts"]).then_inc(ld_c, 16)
            for t in range(NT):
                sp.dma_start(at(h, ALL, t * DM, [[1, DM]]), x_d[t * P:(t + 1) * P, :]).then_inc(ld_x[t], 16)
            for n, name in enumerate(("ssm_a_re", "ssm_a_im")):
                sp.dma_start(at(ring, (0, G), R_LAM + n * P, [[NS, 2], [1, NS]]),
                             dr(A[name], 0, [[NS, G], [G * NS, 2], [1, NS]])).then_inc(ld_small, 16)
            for d in range(2):
                sp.dma_start(at(ring, (0, G), R_LAM + 2 * P + d, [[1, 1]]),
                             dr(A["ssm_log_dt"], d * G, [[1, G], [1, 1]])).then_inc(ld_small, 16)
            for n, name in enumerate(("g_mix", "g_ffn", "g_ple")):
                sp.dma_start(at(vec, ALL, 8 * n, [[1, KC]]), dr(A[name], 0, [[KC, P], [1, KC]])).then_inc(ld_vec, 16)
            for n, name in enumerate(("pool_scale", "ssm_d", "glu_b")):
                sp.dma_start(at(vrow, (4 * n, 4 * n + 4), 0, [[1, P]]),
                             dr(A[name], 0, [[P, 4], [1, P]])).then_inc(ld_vec, 16)
            sp.dma_start(at(big, ALL, 0, [[DP, KC], [1, DP]]),
                         dr(A["w_in"], DP, [[KC * DM, P], [DM, KC], [1, DP]])).then_inc(ld_win0, 16)
            for n, name in enumerate(("ssm_c_re", "ssm_c_im")):
                for d in range(2):
                    sp.dma_start(at(ring, ALL, R_CRAW + n * 4 * P + d * NS, [[P, NB], [1, NS]]),
                                 dr(A[name], d * G * CH * NS, [[NS, P], [GB * CH * NS, NB], [1, NS]])
                                 ).then_inc(ld_craw, 16)
            for n, name in enumerate(("ssm_b_re", "ssm_b_im")):
                for d in range(2):
                    sp.dma_start(at(ring, (d * NS, d * NS + NS), R_BRAW + n * G * CH, [[CH, G], [1, CH]]),
                                 dr(A[name], d * G * NS * CH, [[CH, NS], [NS * CH, G], [1, CH]])
                                 ).then_inc(ld_b, 16)
            sp.dma_start(at(big, ALL, KC * DP, [[DP, KC], [1, DP]]),
                         dr(A["w_in"], 0, [[KC * DM, P], [DM, KC], [1, DP]])).then_inc(ld_win1, 16)
            sp.wait_ge(turned_ps, 1)
            sp.dma_start(at(moe, ALL, M_PW, [[P, 4], [1, P]]),
                         dr(A["pool_w"], 0, [[P, P], [P * P, 4], [1, P]])).then_inc(ld_poolw, 16)
            sp.dma_start(at(rw, ALL, 0, [[NG + NE, KC], [1, NG]]),
                         dr(A["router_grp_w"], 0, [[KC * NG, P], [NG, KC], [1, NG]])).then_inc(ld_poolw, 16)
            for g in range(NG):
                sp.dma_start(at(rw, ALL, NG + g * NEG, [[NG + NE, KC], [1, NEG]]),
                             dr(A["router_exp_w"], g * DM * NEG, [[KC * NEG, P], [NEG, KC], [1, NEG]])
                             ).then_inc(ld_poolw, 16)
            sp.dma_start(at(rbias, (0, 1), 0, [[1, NG]]), dr(A["router_grp_b"], 0, [[NG, 1], [1, NG]])
                         ).then_inc(ld_poolw, 16)
            sp.dma_start(at(rbias, (0, 1), NG, [[1, NE]]), dr(A["router_exp_b"], 0, [[NE, 1], [1, NE]])
                         ).then_inc(ld_poolw, 16)
            for m in range(NB):
                sp.wait_ge(zs_done, m + 1)
                for g in range(GB):
                    sp.dma_start(dr(z_d, (m * GB + g) * NCH, [[G * NCH, CH], [CH * G * NCH, L], [1, NCH]]),
                                 at(zbuf, (CH * g, CH * g + CH), Z_SSM + m * T, [[NCH, L], [1, NCH]])
                                 ).then_inc(zs_stored, 16)
                sp.wait_ge(zs_stored, 16 * GB * (m + 1))
                sp.dma_start(at(ring, ALL, R_U + m * T, [[1, T]]),
                             dr(z_d, m * T, [[G * NCH, P], [1, T]])).then_inc(u_ready[m], 16)
            sp.wait_ge(win_ps, NB)
            sp.dma_start(at(big, ALL, 0, [[DM, 4], [1, DM]]),
                         dr(A["w_out"], 0, [[DM, P], [P * DM, 4], [1, DM]])).then_inc(ld_wout0, 16)
            for hh in range(2):
                sp.wait_ge(k_done, 3 * (hh + 1))
                for q in range(4):
                    sp.dma_start(dr(k_d, (hh * 16 + q) * CH * 15 * CH,
                                    [[15 * CH, CH], [4 * CH * 15 * CH, 4], [1, 15 * CH]]),
                                 at(ring, (32 * q, 32 * q + CH), R_W + hh * 960, [[240, 4], [1, 240]])
                                 ).then_inc(k_stored, 16)
            sp.wait_ge(k_stored, 16 * 8)
            sp.wait_ge(cw_built, NB)
            for s in range(L):
                sp.dma_start(at(ring, (CH * s, CH * s + CH), R_T, [[P, G], [1, P]]),
                             dr(k_d, (L - 1 - s) * CH, [[15 * CH, CH], [CH * 15 * CH, G], [1, P]])
                             ).then_inc(toep_ready, 16)
            sp.wait_ge(zp_ps, NB)
            sp.dma_start(at(big, ALL, 4 * DM, [[DM, 4], [1, DM]]),
                         dr(A["w_out"], 4 * P * DM, [[DM, P], [P * DM, 4], [1, DM]])).then_inc(ld_wout1, 16)
            sp.wait_ge(tu_done, 1)
            sp.dma_start(at(ring, ALL, R_GLU, [[DP, 4], [1, DP]]),
                         dr(A["glu_w"], 0, [[DP, P], [P * DP, 4], [1, DP]])).then_inc(ld_glu, 16)
            sp.wait_ge(xo_re, 4)
            sp.wait_ge(xo_im, 4)
            for m in range(NB):
                sp.wait_ge(y_sb, m + 1)
                sp.dma_start(dr(y_d, m * T, [[G * NCH, P], [1, T]]),
                             at(ring, ALL, R_Y + m * T, [[1, T]])).then_inc(y_stored, 16)
                sp.wait_ge(y_stored, 16 * (m + 1))
                for g in range(GB):
                    sp.dma_start(at(ring, (CH * g, CH * g + CH), R_YC + m * T, [[NCH, L], [1, NCH]]),
                                 dr(y_d, (m * GB + g) * NCH, [[G * NCH, CH], [CH * G * NCH, L], [1, NCH]])
                                 ).then_inc(yc_ready[m], 16)
            load_expert(sp, 0, 0, w_ready[0])
            sp.dma_start(at(moe, ALL, M_PIN, [[DPLE, NT], [1, DPLE]]),
                         dr(A["p"], 0, [[DPLE, P], [P * DPLE, NT], [1, DPLE]])).then_inc(ld_ppw, 16)
            sp.dma_start(at(moe, ALL, M_PPW, [[DM, 2], [1, DM]]),
                         dr(A["ple_proj_w"], 0, [[DM, P], [P * DM, 2], [1, DM]])).then_inc(ld_ppw, 16)
            load_expert(sp, 1, 1, w_ready[1])
            sp.wait_ge(cat_done, NB)
            load_expert(sp, 2, 2, w_ready[2])
            load_expert(sp, 3, 3, w_ready[3])
            for t in range(NT):
                sp.wait_ge(v_done, t + 1)
                sp.dma_start(v_d[t * P:(t + 1) * P, :], at(zbuf, ALL, t * DM, [[1, DM]])).then_inc(v_stored, 16)
            sp.wait_ge(wo1_ps, 2 * NT)
            sp.dma_start(at(big, ALL, 0, [[1, KC * DM]]),
                         dr(A["ple_gate_w"], 0, [[KC * DM, P], [1, KC * DM]])).then_inc(ld_wple, 16)
            with sp.Fori(1, NE // RING) as i:
                for u in range(RING):
                    e = sp.snap(i * RING + u)
                    free = sp.snap(i * RING + (u - RING + 1))
                    sp.wait_ge(dn_ps, free)
                    load_expert(sp, e, u, w_ready[u])
            with sp.If(most(sp) > CAP):
                with sp.Fori(1, ROUNDS) as r:
                    with sp.Fori(0, NE) as e0:
                        e = sp.snap(e0 + 0)
                        turn = sp.snap((r - 1) * NE + e0 + 1)
                        sp.wait_ge(o_turn, turn)
                        load_expert(sp, e, 0, o_w)
            with sp.Else():
                pass
            sp.wait_ge(moe_done, 1)
            for t in range(NT):
                if t >= 2:
                    sp.wait_ge(comb, 2 * (t - 1))
                sp.dma_start(at(ring, ALL, E_YP + (t % 2) * 2 * DM, [[1, 2 * DM]]),
                             dr(pairs_d, t * P * 2 * DM, [[2 * DM, P], [1, 2 * DM]])).then_inc(ld_pairs[t], 16)
            sp.dma_start(at(ring, ALL, E_BP, [[1, DM]]),
                         dr(A["ple_gate_b"], 0, [[0, P], [1, DM]])).then_inc(ld_fin, 16)
            sp.dma_start(at(ring, ALL, E_GF, [[1, DM]]),
                         dr(A["g_final"], 0, [[0, P], [1, DM]])).then_inc(ld_fin, 16)
            for t in range(NT):
                sp.wait_ge(fin_done, t + 1)
                sp.dma_start(out_d[t * P:(t + 1) * P, :], at(ring, ALL, E_O + t * DM, [[1, DM]])
                             ).then_inc(stored, 16)
            sp.wait_ge(stored, 16 * NT)

        @block.scalar
        def _(act):

            def copy(o, i, signal):
                act.activation(o, i, ACT.Copy).then_inc(signal, 1)

            def mean_root(src, junk, ss, t, done):
                act.activation(junk, src, ACT.Square, accum_out=at(small, ALL, ss + t, [[1, 1]])).then_inc(done, 1)

            act.wait_ge(eps_set, 1)
            for t in range(NT):
                act.wait_ge(ld_x[t], 16)
                mean_root(at(h, ALL, t * DM, [[1, DM]]), at(moe, ALL, M_XN + t * DM, [[1, DM]]), S_SS, t, ss_done)
            act.wait_ge(ss_done, NT)
            act.activation(at(small, ALL, S_RS, [[1, NT]]), at(small, ALL, S_SS, [[1, NT]]), ACT.Sqrt,
                           bias=at(small, ALL, S_EPS, [[1, 1]]), scale=1.0 / DM).then_inc(rms_root, 1)
            act.wait_ge(ld_small, 64)
            act.activation(at(ring, (0, G), R_LAM + 2 * P + 2, [[1, 2]]), at(ring, (0, G), R_LAM + 2 * P, [[1, 2]]),
                           ACT.Exp).then_inc(lam_dt, 1)
            act.wait_ge(lam_arg, 1)
            act.activation(lam(4), lam(3), ACT.Exp).then_inc(lam_exp, 1)
            act.wait_ge(lam_red, 1)
            act.activation(lam(8), lam(7), ACT.Sin).then_inc(lam_sin, 1)
            act.activation(lam(9), lam(7), ACT.Sin, scale=0.5).then_inc(lam_sin, 1)
            act.wait_ge(turned_ps, 1)
            act.wait_ge(ld_vec, 96)
            for j in range(KC):
                act.activation(at(ut, ALL, j * T, [[1, T]]), bank[j][:, :], ACT.Copy, scale=vcol(V_MIX + j)
                               ).then_inc(ut_done, 1)
            act.wait_ge(lam_ps, 1)
            copy(at(ring, ALL, R_PW + G, [[9 * G, 2], [1, G]]), at(bank[7], ALL, 0, [[G, 2], [1, G]]), lam_lane)
            copy(at(ring, ALL, R_COEF, [[1, 2 * G]]), bank[7][:, 64:128], lam_lane)
            act.wait_ge(c_ps, 1)
            act.activation(at(ring, ALL, R_CL, [[1, 512]]), bank[4][:, :], ACT.Copy).then_inc(c_done, 1)
            act.activation(at(ring, ALL, R_CL + 512, [[1, 512]]), bank[5][:, :], ACT.Copy, scale=-1.0
                           ).then_inc(c_done, 1)
            act.activation(at(vec, ALL, V_POOL, [[1, 12]]), bank[6][:, 0:12], ACT.Copy).then_inc(vec_done, 1)
            act.wait_ge(pow_done, 1)
            for ri in range(2):
                pw, pin = R_PW + ri * 9 * G, R_PIN + ri * 8 * G
                copy(at(ring, FWD, pin, [[G, L], [1, G]]), at(ring, FWD, pw + 7 * G, [[-G, L], [1, G]]), pin_done)
                copy(at(ring, BWD, pin, [[1, L * G]]), at(ring, BWD, pw, [[1, L * G]]), pin_done)

            def zs_out(m):
                act.wait_ge(win_ps, m + 1)
                copy(at(zbuf, ALL, Z_SSM + m * T, [[1, NCH], [NCH, L]]),
                     at(bank[m], ALL, 0, [[L, NCH], [1, L]]), zs_done)

            def wt_out(b):
                for hb in range(2):
                    act.wait_ge(wt_ps, 2 * b + hb + 1)
                    if b >= 2:
                        act.wait_ge(e_ps, b - 1)
                    for ri in range(2):
                        copy(at(moe, ALL, M_WT + (b % 2) * 2048 + ri * 1024 + hb * 512, [[1, 512]]),
                             bank[4 + 2 * ri + hb][:, :], wt_done)

            def e_out(b):
                act.wait_ge(e_ps, b + 1)
                for ri in range(2):
                    src = bank[2 * (b % 2) + ri]
                    copy(at(ring, FWD, R_X + 64 + ri * G + b * GB, [[1, GB], [64, NCH]]),
                         at(src, FWD, 0, [[NCH, GB], [1, NCH]]), e_done)
                    copy(at(ring, BWD, R_X + 64 * NCH + ri * G + b * GB, [[1, GB], [-64, NCH]]),
                         at(src, BWD, 0, [[NCH, GB], [1, NCH]]), e_done)

            for m in range(3):
                zs_out(m)
            wt_out(0)
            zs_out(3)
            for b in range(1, NB):
                wt_out(b)
                e_out(b - 1)
            e_out(NB - 1)
            def zp_out(m):
                act.wait_ge(zp_ps, m + 1)
                copy(at(zbuf, ALL, Z_POOL + m * PW_ + PAD, [[1, T]]), bank[m % 2][:, :], zp_done)

            zp_out(0)
            zp_out(1)
            act.wait_ge(wt_ps, 2 * NB)
            for hh in range(2):
                act.wait_ge(k_ps, hh + 1)
                for src, off, n in ((K_BANKS[hh][1], 0, 112), (K_BANKS[hh][2], 112, 16), (K_BANKS[hh][0], 128, 112)):
                    copy(at(ring, ALL, R_W + hh * 960 + off, [[240, 4], [1, n]]),
                         at(bank[src], ALL, 0, [[n, 4], [1, n]]), k_done)
            zp_out(2)
            zp_out(3)
            for m in range(4):
                act.wait_ge(a_ps, m + 1)
                act.activation(at(ut, ALL, m * T, [[1, T]]), bank[4 + m][:, :], ACT.Copy, scale=vcol(V_POOL + m)
                               ).then_inc(a_done, 1)
            def wo0_out(n):
                act.wait_ge(wo0_ps, n + 1)
                least(act, wo0_done, n - 1)
                copy(at(moe, ALL, M_PT + (n % 2) * 512, [[1, 512]]), bank[4 + n % 4][:, :], wo0_sb)

            for n in range(4):
                wo0_out(n)
            act.wait_ge(scan_b, NCH - 1)
            for gh in range(2):
                copy(at(moe, FWD, M_XO + gh * 16 * NCH, [[NCH, 16], [1, NCH]]),
                     at(ring, FWD, R_X + gh * 16, [[1, 16], [64, NCH]]), xo_re)
                copy(at(moe, BWD, M_XO + gh * 16 * NCH, [[NCH, 16], [1, NCH]]),
                     at(ring, BWD, R_X + 64 * (NCH - 1) + gh * 16, [[1, 16], [-64, NCH]]), xo_re)
            act.wait_ge(tu_done, 1)
            for b in range(NB):
                act.wait_ge(y_ps, b + 1)
                copy(at(ring, ALL, R_Y + b * T, [[1, T]]), bank[b][:, :], y_sb)
            for n in range(4, 2 * NT):
                wo0_out(n)
            for m in range(NB):
                act.wait_ge(yd_done, m + 1)
                act.activation(at(ring, ALL, R_ZG + m * T, [[1, T]]), at(ring, ALL, R_YC + m * T, [[1, T]]),
                               ACT.Gelu_apprx_tanh).then_inc(zg_done, 1)
            for m in range(NB):
                act.wait_ge(glu_ps, m + 1)
                act.activation(at(ring, ALL, R_YC + m * T, [[1, T]]), bank[4 + m][:, :], ACT.Sigmoid,
                               bias=vcol(V_GLU + m)).then_inc(gate_done, 1)
            for t in range(NT):
                act.wait_ge(h_done, 2 * (t + 1))
                mean_root(at(h, ALL, t * DM, [[1, DM]]), at(zbuf, ALL, t * DM, [[1, DM]]), S_SS2, t, ss_done)
                act.wait_ge(ss_done, NT + t + 1)
                act.activation(at(small, ALL, S_RS2 + t, [[1, 1]]), at(small, ALL, S_SS2 + t, [[1, 1]]), ACT.Sqrt,
                               bias=at(small, ALL, S_EPS, [[1, 1]]), scale=1.0 / DM).then_inc(rms_root, 1)
            act.wait_ge(d4_done, 1)
            act.activation(at(ut, ALL, Q["e4"], [[1, NT * 4]]), at(ut, ALL, Q["d4"], [[1, NT * 4]]), ACT.Exp
                           ).then_inc(ex_done, 1)
            act.wait_ge(df_done, 1)
            act.activation(at(ut, ALL, Q["ex"], [[1, NT]]), at(ut, ALL, Q["df"], [[1, NT]]), ACT.Exp
                           ).then_inc(ex_done, 1)
            act.wait_ge(ppt_ps, 1)
            for j in range(2):
                copy(at(moe, ALL, M_PPT + j * T, [[1, T]]), bank[1 + j][:, :], ppt_sb)
            act.wait_ge(v_stored, 16 * NT)
            act.wait_ge(turned_ps, 1 + NT)
            for n in range(2 * NT):
                act.wait_ge(pp_ps, n + 1)
                copy(at(zbuf, ALL, n * 512, [[1, 512]]), bank[3 + n % 4][:, :], pp_done)

            def silu(i, u):
                e = i * RING + u
                act.wait_ge(gu_ps, e + 1)
                least(act, hg_sb, 2 * e)
                act.activation(at(moe, (0, CAP), M_SG, [[1, DE]]), at(bank[1 + u % 2], (0, CAP), 0, [[1, DE]]),
                               ACT.Silu).then_inc(sg_sb, 1)

            def y_out(i, u):
                if not valid(i, u):
                    return
                act.wait_ge(dn_ps, i * RING + u + 1)
                least(act, ys_stored[u % 2], i * 32 + 16 * (u // 2))
                copy(at(moe, ALL, M_Y + (u % 2) * 512, [[1, 512]]), bank[4 + u % 2][:, :], dn_sb)

            def step(i, u):
                silu(i, u)
                y_out(*shift(i, u, -1))

            sweep(act, step)
            y_out(NE // RING - 1, RING - 1)
            with act.If(most(act) > CAP):
                act.wait_ge(dn_sb, NE)
                with act.Fori(1, ROUNDS) as r:
                    with act.Fori(0, NE) as e:
                        turn = act.snap((r - 1) * NE + e + 1)
                        act.wait_ge(o_gu, turn)
                        act.activation(at(moe, (0, CAP), M_SG, [[1, DE]]), at(bank[1], (0, CAP), 0, [[1, DE]]),
                                       ACT.Silu).then_inc(o_sg, 1)
                        act.wait_ge(o_dn, turn)
                        copy(at(moe, ALL, M_Y, [[1, 512]]), bank[4][:, :], o_dn_sb)
            with act.Else():
                pass
            for t in range(NT):
                act.wait_ge(comb, 2 * (t + 1))
                mean_root(at(h, ALL, t * DM, [[1, DM]]), at(ring, ALL, E_RN + t * DM, [[1, DM]]), S_SS3, t, ss_done)
                act.wait_ge(ss_done, 2 * NT + t + 1)
                act.activation(at(small, ALL, S_RS3 + t, [[1, 1]]), at(small, ALL, S_SS3 + t, [[1, 1]]), ACT.Sqrt,
                               bias=at(small, ALL, S_EPS, [[1, 1]]), scale=1.0 / DM).then_inc(rms_root, 1)
            for n in range(2 * NT):
                act.wait_ge(gate_in, n + 1)
                sg = at(ring, ALL, E_SG + n * 512, [[1, 512]])
                act.activation(sg, sg, ACT.Sigmoid).then_inc(gate_sb, 1)
                if n % 2:
                    t = n // 2
                    act.wait_ge(gated, 2 * (t + 1))
                    mean_root(at(h, ALL, t * DM, [[1, DM]]), at(ring, ALL, E_SG + t * DM, [[1, DM]]), S_SS4, t, ss_done)
                    act.wait_ge(ss_done, 3 * NT + t + 1)
                    act.activation(at(small, ALL, S_RS4 + t, [[1, 1]]), at(small, ALL, S_SS4 + t, [[1, 1]]), ACT.Sqrt,
                                   bias=at(small, ALL, S_EPS, [[1, 1]]), scale=1.0 / DM).then_inc(rms_root, 1)

        @block.vector
        def _(dve):
            own = Chain(dve, dve_step)

            def tt(o, a, b, op):
                return dve.tensor_tensor(o, a, b, op)

            def seq(ins):
                own.do(ins)
                own.settle()

            def inverse(col, n, count):
                dve.wait_ge(rms_root, count)
                o = at(small, ALL, col, [[1, n]])
                dve.reciprocal(o, o).then_inc(rstd_done, 1)
                dve.wait_ge(rstd_done, count)

            def normalise(dst, base, t, col):
                return dve.tensor_scalar(at(dst, ALL, base + t * DM, [[1, P], [P, KC]]),
                                         at(h, ALL, t * DM, [[KC, P], [1, KC]]),
                                         at(small, ALL, col + t, [[1, 1]]), None, ALU.mult)

            dve.memset(at(small, ALL, S_EPS, [[1, 1]]), EPS).then_inc(eps_set, 1)
            inverse(S_RS, NT, 1)
            for t in range(NT):
                normalise(moe, M_XN, t, S_RS).then_inc(xn_done, 1)
            gdn = [[NS, 2], [1, NS]]
            are, aim, dt = lam(0), lam(1), at(ring, (0, G), R_LAM + 2 * P + 2, [[1, 2], [0, NS]])

            def lam3(k):
                return at(ring, (0, G), R_LAM + k * P, gdn)

            dve.wait_ge(lam_dt, 1)
            tt(lam3(3), lam3(0), dt, ALU.mult).then_inc(lam_arg, 1)
            seq(tt(lam3(5), lam3(1), dt, ALU.mult))
            seq(dve.tensor_scalar(lam(6), lam(5), 1.0 / TWO_PI, ROUND, ALU.mult, ALU.add))
            seq(dve.tensor_scalar(lam(6), lam(6), ROUND, None, ALU.subtract))
            seq(dve.scalar_tensor_tensor(lam(5), lam(6), -TP1, lam(5), ALU.mult, ALU.add))
            seq(dve.scalar_tensor_tensor(lam(5), lam(6), -TP2, lam(5), ALU.mult, ALU.add))
            seq(dve.scalar_tensor_tensor(lam(5), lam(6), -TP3, lam(5), ALU.mult, ALU.add))
            dve.tensor_scalar(lam(7), lam(5), PI_LO, -PI_LO, ALU.min, ALU.max).then_inc(lam_red, 1)
            seq(tt(lam(10), are, are, ALU.mult))
            seq(tt(lam(11), aim, aim, ALU.mult))
            seq(tt(lam(10), lam(10), lam(11), ALU.add))
            seq(dve.reciprocal(lam(10), lam(10)))
            dve.wait_ge(lam_sin, 2)
            seq(tt(lam(9), lam(9), lam(9), ALU.mult))
            seq(dve.tensor_scalar(lam(9), lam(9), -2.0, 1.0, ALU.mult, ALU.add))
            dve.wait_ge(lam_exp, 1)
            seq(tt(lam(12), lam(4), lam(9), ALU.mult))
            seq(tt(lam(13), lam(4), lam(8), ALU.mult))
            seq(dve.tensor_scalar(lam(5), lam(12), 1.0, None, ALU.subtract))
            seq(tt(lam(6), lam(5), are, ALU.mult))
            seq(tt(lam(7), lam(13), aim, ALU.mult))
            seq(tt(lam(6), lam(6), lam(7), ALU.add))
            seq(tt(lam(14), lam(6), lam(10), ALU.mult))
            seq(tt(lam(6), lam(13), are, ALU.mult))
            seq(tt(lam(7), lam(5), aim, ALU.mult))
            seq(tt(lam(6), lam(6), lam(7), ALU.subtract))
            tt(lam(15), lam(6), lam(10), ALU.mult).then_inc(lam_done, 1)

            def grid(off, dims):
                return at(ring, ALL, off, dims)

            dve.wait_ge(lam_lane, 2)
            pr, pi = R_PW, R_PW + 9 * G
            own.do(dve.memset(grid(pr, [[1, G]]), 1.0))
            own.do(dve.memset(grid(pi, [[1, G]]), 0.0))
            for lo, n in ((1, 1), (1, 2), (1, 4)):
                by = lo + n - 1
                rng, cst_ = [[G, n], [1, G]], [[0, n], [1, G]]
                src_r, src_i = grid(pr + lo * G, rng), grid(pi + lo * G, rng)
                by_r, by_i = grid(pr + by * G, cst_), grid(pi + by * G, cst_)
                dst_r, dst_i = grid(pr + (by + 1) * G, rng), grid(pi + (by + 1) * G, rng)
                tmp_r, tmp_i = grid(R_TMP, rng), grid(R_TMP + n * G, rng)
                own.settle()
                own.do(tt(dst_r, src_r, by_r, ALU.mult))
                own.do(tt(tmp_r, src_i, by_i, ALU.mult))
                own.do(tt(dst_i, src_r, by_i, ALU.mult))
                own.do(tt(tmp_i, src_i, by_r, ALU.mult))
                own.settle()
                own.do(tt(dst_r, dst_r, tmp_r, ALU.subtract))
                ins = tt(dst_i, dst_i, tmp_i, ALU.add)
                if n < 4:
                    own.do(ins)
                else:
                    ins.then_inc(pow_done, 1)
            dve.wait_ge(pow_done, 1)
            own.settle()
            own.do(dve.tensor_copy(at(small, ALL, S_A2, [[G, 2], [1, G]]), grid(pr + 8 * G, [[0, 2], [1, G]])))
            own.do(dve.tensor_copy(at(small, ALL, S_A2 + 2 * G, [[1, G]]), grid(pi + 8 * G, [[1, G]])))
            own.do(dve.tensor_scalar(at(small, ALL, S_A2 + 3 * G, [[1, G]]), grid(pi + 8 * G, [[1, G]]), -1.0, None, ALU.mult))
            dve.wait_ge(ld_b, 64)
            gc = [[CH, G], [1, CH]]
            cr, ci = grid(R_COEF, [[1, G], [0, CH]]), grid(R_COEF + G, [[1, G], [0, CH]])
            br, bi = grid(R_BRAW, gc), grid(R_BRAW + 512, gc)
            own.do(dve.memset(grid(R_BB + 512, [[1, 16]]), 0.0))
            own.do(dve.memset(grid(R_BBI + 512, [[1, 16]]), 0.0))
            own.do(tt(grid(R_BB, gc), cr, br, ALU.mult))
            own.do(tt(grid(R_TMP, gc), ci, bi, ALU.mult))
            own.do(tt(grid(R_BBI, gc), cr, bi, ALU.mult))
            own.do(tt(grid(R_TMP + 512, gc), ci, br, ALU.mult))
            own.settle()
            own.do(tt(grid(R_BB, gc), grid(R_BB, gc), grid(R_TMP, gc), ALU.subtract))
            own.do(tt(grid(R_BBI, gc), grid(R_BBI, gc), grid(R_TMP + 512, gc), ALU.add))
            dve.wait_ge(pin_done, 4)
            for b in range(NB):
                for hb in range(2):
                    if b:
                        dve.wait_ge(wt_ps, 2 * b + hb - 1)
                    g0 = b * GB + hb * 4
                    gsc = [[P, 4], [CH, L], [1, CH]]
                    pw_r = grid(R_PIN + g0, [[1, 4], [G, L], [0, CH]])
                    pw_i = grid(R_PIN + L * G + g0, [[1, 4], [G, L], [0, CH]])
                    b_r = grid(R_BB + g0 * CH, [[CH, 4], [0, L], [1, CH]])
                    b_i = grid(R_BBI + g0 * CH, [[CH, 4], [0, L], [1, CH]])
                    w_r, w_i = grid(R_W + hb * 512, gsc), grid(R_W + 1024 + hb * 512, gsc)
                    t_r, t_i = grid(R_TMP, gsc), grid(R_TMP + 512, gsc)
                    own.settle()
                    own.do(tt(w_r, pw_r, b_r, ALU.mult))
                    own.do(tt(t_r, pw_i, b_i, ALU.mult))
                    own.do(tt(w_i, pw_r, b_i, ALU.mult))
                    own.do(tt(t_i, pw_i, b_r, ALU.mult))
                    own.settle()
                    own.do(tt(w_r, w_r, t_r, ALU.subtract))
                    tt(w_i, w_i, t_i, ALU.add).then_inc(w_built, 1)
                    dve.wait_ge(w_built, 2 * b + hb + 1)
            dve.memset(grid(R_X, [[1, 64]]), 0.0).then_inc(x_zero, 1)
            dve.wait_ge(e_done, 16)
            a_re2, a_im2 = at(small, ALL, S_A2, [[G, 2], [1, G]]), at(small, ALL, S_A2 + 2 * G, [[G, 2], [1, G]])
            t1, t2 = at(small, ALL, S_T1, [[G, 2], [1, G]]), at(small, ALL, S_T2, [[G, 2], [1, G]])
            UNROLL = 9

            def scan_step(n):
                prev, new = R_X + n * 64 + 64, R_X + n * 64 + 128
                tt(t1, a_re2, grid(prev, [[G, 2], [1, G]]), ALU.mult).then_inc(scan_a, 1)
                tt(t2, a_im2, grid(prev, [[G, 2], [1, G]]), ALU.mult).then_inc(scan_a, 1)
                dve.wait_ge(scan_a, n * 3 + 1)
                tt(grid(new, [[1, 2 * G]]), grid(new, [[1, 2 * G]]), at(small, ALL, S_T1, [[1, 2 * G]]),
                   ALU.add).then_inc(scan_a, 1)
                dve.wait_ge(scan_a, n * 3 + 3)
                tt(grid(new, [[G, 2], [1, G]]), grid(new, [[G, 2], [1, G]]),
                   at(small, ALL, S_T2 + G, [[-G, 2], [1, G]]), ALU.add).then_inc(scan_b, 1)
                dve.wait_ge(scan_b, n + 1)

            assert (NCH - 1) % UNROLL == 0
            with dve.Fori(0, (NCH - 1) // UNROLL) as i:
                for u in range(UNROLL):
                    scan_step(i * UNROLL + u)
            for gh in range(2):
                dve.tensor_copy(at(moe, FWD, M_XO + 2048 + gh * 16 * NCH, [[NCH, 16], [1, NCH]]),
                                at(ring, FWD, R_X + G + gh * 16, [[1, 16], [64, NCH]])).then_inc(xo_im, 1)
                dve.tensor_copy(at(moe, BWD, M_XO + 2048 + gh * 16 * NCH, [[NCH, 16], [1, NCH]]),
                                at(ring, BWD, R_X + 64 * (NCH - 1) + G + gh * 16, [[1, 16], [-64, NCH]])
                                ).then_inc(xo_im, 1)
            for m in range(NB):
                dve.wait_ge(yc_ready[m], 16 * GB)
                yc = at(ring, ALL, R_YC + m * T, [[1, T]])
                dve.scalar_tensor_tensor(yc, at(zbuf, ALL, Z_SSM + m * T, [[1, T]]), vcol(V_D + m), yc,
                                         ALU.mult, ALU.add).then_inc(yd_done, 1)
            for m in range(NB):
                dve.wait_ge(gate_done, m + 1)
                tt(at(ut, ALL, (4 + m) * T, [[1, L], [L, NCH]]), at(ring, ALL, R_ZG + m * T, [[NCH, L], [1, NCH]]),
                   at(ring, ALL, R_YC + m * T, [[NCH, L], [1, NCH]]), ALU.mult).then_inc(cat_done, 1)
            def residual(t):
                for n in (2 * t, 2 * t + 1):
                    dve.wait_ge(wo1_ps, n + 1)
                    hv = at(h, ALL, n * 512, [[1, 512]])
                    tt(hv, bank[n][:, :], hv, ALU.add).then_inc(h_done, 1)

            def norm(t):
                inverse(S_RS2 + t, 1, 2 + t)
                normalise(zbuf, 0, t, S_RS2).then_inc(v_done, 1)

            def turned(t, count, gain, signal):
                dve.wait_ge(turned_ps, count)
                for n in range(2):
                    tt(at(ut, ALL, 4 * n * T + t * P, [[T, 4], [1, P]]), at(bank[2 * t + n], ALL, 0, [[P, 4], [1, P]]),
                       at(vec, ALL, gain + 4 * n, [[1, 4], [0, P]]), ALU.mult).then_inc(signal, 1)

            def logits(t):
                dve.wait_ge(log_ps, t + 1)
                tt_l = at(logit, ALL, t * 36, [[1, 36]])
                own.do(dve.tensor_copy(tt_l, bank[2 * t][:, 0:36]))

            dve.wait_ge(wo0_done, 2 * NT)
            for step_t in range(NT + 3):
                if step_t < NT:
                    residual(step_t)
                if 0 <= step_t - 1 < NT:
                    norm(step_t - 1)
                if 0 <= step_t - 2 < NT:
                    turned(step_t - 2, step_t, V_FFN, ut_done)
                if 0 <= step_t - 3 < NT:
                    logits(step_t - 3)

            def qv(name, dims, off=0):
                return at(ut, ALL, Q[name] + off, dims)

            def cv(off, dims):
                return at(cst, ALL, off, dims)

            def peak(o, i, op=ALU.max):
                seq(dve.tensor_reduce(o, i, AX.X, op))

            one, four, eight = [[1, NT]], [[4, NT], [1, 4]], [[NEG, NT], [1, NEG]]
            tge = [[NE, NT], [NEG, NG], [1, NEG]]
            own.settle()
            peak(qv("gm", one), at(logit, ALL, 0, [[36, NT], [1, 4]]))
            tt(qv("d4", four), at(logit, ALL, 0, [[36, NT], [1, 4]]), qv("gm", [[1, NT], [0, 4]]), ALU.subtract
               ).then_inc(d4_done, 1)
            dve.wait_ge(d4_done, 1)
            seq(dve.scalar_tensor_tensor(qv("g1", four), qv("d4", four), 0.0, cv(C_LOW, [[0, NT], [1, 4]]),
                                         ALU.is_equal, ALU.mult))
            peak(qv("g2", one), qv("g1", four))
            seq(tt(qv("goh", four), qv("g1", four), qv("g2", [[1, NT], [0, 4]]), ALU.is_equal))
            seq(tt(qv("pr", tge), qv("goh", [[4, NT], [1, 4], [0, NEG]]), at(logit, ALL, 4, [[36, NT], [NEG, NG], [1, NEG]]),
                   ALU.mult))
            peak(qv("sel", eight), qv("pr", [[NE, NT], [1, NEG], [NEG, NG]]), ALU.add)

            def first_best(src, best, a, b, hot):
                peak(qv(best, one), qv(src, eight))
                seq(tt(qv(a, eight), qv(src, eight), qv(best, [[1, NT], [0, NEG]]), ALU.is_equal))
                seq(tt(qv(a, eight), qv(a, eight), cv(C_LOW, [[0, NT], [1, NEG]]), ALU.mult))
                peak(qv(b, one), qv(a, eight))
                seq(tt(qv(hot, eight), qv(a, eight), qv(b, [[1, NT], [0, NEG]]), ALU.is_equal))

            first_best("sel", "m1", "q1", "q2", "oh1")
            seq(dve.scalar_tensor_tensor(qv("s2", eight), qv("oh1", eight), -3.0e38, qv("sel", eight),
                                         ALU.mult, ALU.add))
            first_best("s2", "m2", "q3", "q4", "oh2")
            tt(qv("df", one), qv("m2", one), qv("m1", one), ALU.subtract).then_inc(df_done, 1)
            for k in (1, 2):
                own.do(tt(qv(f"M{k}", tge), qv("goh", [[4, NT], [1, 4], [0, NEG]]),
                          qv(f"oh{k}", [[NEG, NT], [0, NG], [1, NEG]]), ALU.mult))
            own.settle()
            tt(qv("MS", [[1, NT * NE]]), qv("M1", [[1, NT * NE]]), qv("M2", [[1, NT * NE]]), ALU.add
               ).then_inc(mask_done, 1)
            dve.wait_ge(rank_ps, 1)
            te = [[NE, NT], [1, NE]]
            for k in (1, 2):
                seq(tt(qv("pa", te), qv(f"M{k}", te), at(bank[7], ALL, 0, te), ALU.mult))
                peak(qv(f"r{k}", one), qv("pa", te), ALU.add)
                seq(tt(qv("pb", te), qv(f"M{k}", te), cv(C_NUM, [[0, NT], [1, NE]]), ALU.mult))
                peak(qv(f"e{k}", one), qv("pb", te), ALU.add)
                seq(dve.scalar_tensor_tensor(at(slot_i, ALL, k - 1, [[2, NT]]), qv(f"r{k}", one), float(NE),
                                             qv(f"e{k}", one), ALU.mult, ALU.add))
            dve.tensor_reduce(at(flag, ALL, 0, [[1, 1]]), at(bank[7], ALL, NT * NE, [[1, NE]]), AX.X, ALU.max
                              ).then_inc(slot_done, 1)

            def tokens(o, table, done):
                dve.tensor_scalar(o, table, 1, None, ALU.logical_shift_right).then_inc(done, 1)

            def half_rows(o, table, done):
                dve.tensor_scalar(o, table, 2.0, cv(C_HALF, [[1, 1]]), ALU.mult, ALU.add).then_inc(done, 1)

            dve.wait_ge(ex_done, 2)
            peak(qv("gs", one), qv("e4", four), ALU.add)
            seq(dve.reciprocal(qv("gp", one), qv("gs", one)))
            seq(dve.tensor_scalar(qv("dn", one), qv("ex", one), 1.0, None, ALU.add))
            seq(dve.reciprocal(qv("dn", one), qv("dn", one)))
            seq(tt(at(small, ALL, S_W1, one), qv("gp", one), qv("dn", one), ALU.mult))
            seq(tt(at(small, ALL, S_W2, one), at(small, ALL, S_W1, one), qv("ex", one), ALU.mult))
            dve.wait_ge(tbl_read, 32)
            for n, parts in enumerate(((0, CAP), (CAP, P))):
                tokens(at(gidx_all, parts, 0, [[1, NE // 2]]), at(tblw, parts, n, [[2, NE // 2]]), idx_done)
            half_rows(at(sidx_all, ALL, 0, [[1, NE]]), at(tblw, ALL, 0, [[1, NE]]), idx_done)

            def x_out(k, signal):
                for n in range(2):
                    tt(at(moe, ALL, M_XT + k * DM + n * 512, [[P, 4], [1, P]]), at(bank[n * 6], ALL, 0, [[P, 4], [1, P]]),
                       at(vec, ALL, V_FFN + 4 * n, [[1, 4], [0, P]]), ALU.mult).then_inc(signal, 1)

            def hidden(src, signal):
                for j in range(2):
                    tt(at(moe, (j * CAP, j * CAP + CAP), M_HG, [[1, P]]), at(moe, (0, CAP), M_SG + j, [[2, P]]),
                       at(src, (CAP, P), j, [[2, P]]), ALU.mult).then_inc(signal, 1)

            def x_step(i, u):
                if not valid(i, u) or u % 2:
                    return
                e = i * RING + u
                dve.wait_ge(xT_ps, i * 2 + u // 2 + 1)
                least(dve, gu_ps, e - 2)
                x_out(u // 2, xT_sb)

            def step(i, u):
                e = i * RING + u
                dve.wait_ge(sg_sb, e + 1)
                least(dve, hT_ps, e)
                hidden(bank[1 + u % 2], hg_sb)
                x_step(*shift(i, u, 1))
                dve.wait_ge(hT_ps, e + 1)
                least(dve, dn_ps, e - 1)
                dve.tensor_copy(at(moe, ALL, M_HT + (u % 2) * P, [[1, P]]), bank[3][:, 0:P]).then_inc(hT_sb, 1)

            dve.wait_ge(pp_ps, 2 * NT)
            x_step(0, 0)
            sweep(dve, step)
            with dve.If(most(dve) > CAP):
                with dve.Fori(1, ROUNDS) as r:
                    with dve.Fori(0, NE) as e:
                        turn = dve.snap((r - 1) * NE + e + 1)
                        twice = dve.snap(turn * 32)
                        dve.wait_ge(o_tbl, twice)
                        tokens(at(gidx[0], ALL, 0, [[1, 1]]), at(tblw, ALL, e, [[1, 1]]), o_idx)
                        half_rows(at(sidx[0], ALL, 0, [[1, 1]]), at(tblw, ALL, e, [[1, 1]]), o_idx)
                        dve.wait_ge(o_xT_ps, turn)
                        x_out(0, o_xT)
                        dve.wait_ge(o_sg, turn)
                        hidden(bank[1], o_hg)
                        dve.wait_ge(o_hT_ps, turn)
                        dve.tensor_copy(at(moe, ALL, M_HT, [[1, P]]), bank[3][:, 0:P]).then_inc(o_hT, 1)
            with dve.Else():
                pass
            def combine(t):
                dve.wait_ge(ld_pairs[t], 16)
                hv = at(h, ALL, t * DM, [[1, DM]])
                for k, col in enumerate((S_W1, S_W2)):
                    dve.scalar_tensor_tensor(hv, at(ring, ALL, E_YP + (t % 2) * 2 * DM + k * DM, [[1, DM]]),
                                             at(small, ALL, col + t, [[1, 1]]), hv, ALU.mult, ALU.add
                                             ).then_inc(comb, 1)
                    dve.wait_ge(comb, 2 * t + k + 1)

            def rows(t):
                inverse(S_RS3 + t, 1, 2 + NT + t)
                normalise(ring, E_RN, t, S_RS3).then_inc(r_done, 1)

            def gate(n):
                dve.wait_ge(gate_ps, n + 1)
                sg, hv = at(ring, ALL, E_SG + n * 512, [[1, 512]]), at(h, ALL, n * 512, [[1, 512]])
                tt(sg, bank[n][:, :], at(ring, ALL, E_BP + n % 2 * 512, [[1, 512]]), ALU.add).then_inc(gate_in, 1)
                dve.wait_ge(gate_sb, n + 1)
                seq(tt(sg, sg, at(zbuf, ALL, n * 512, [[1, 512]]), ALU.mult))
                tt(hv, hv, sg, ALU.add).then_inc(gated, 1)

            def final(t):
                inverse(S_RS4 + t, 1, 2 + 2 * NT + t)
                dve.scalar_tensor_tensor(at(ring, ALL, E_O + t * DM, [[1, DM]]), at(h, ALL, t * DM, [[1, DM]]),
                                         at(small, ALL, S_RS4 + t, [[1, 1]]), at(ring, ALL, E_GF, [[1, DM]]),
                                         ALU.mult, ALU.mult).then_inc(fin_done, 1)

            for step_t in range(NT + 2):
                if step_t < NT:
                    combine(step_t)
                if 0 <= step_t - 1 < NT:
                    rows(step_t - 1)
                if 0 <= step_t - 2 < NT:
                    turned(step_t - 2, 1 + NT + step_t - 1, V_PLE, ut_done)
            dve.wait_ge(ld_fin, 32)
            for t in range(NT):
                gate(2 * t)
                gate(2 * t + 1)
                final(t)

        @block.gpsimd
        def _(pool):
            own = Chain(pool, pool_step)

            def seq(ins):
                own.do(ins)
                own.settle()

            own.do(pool.memset(at(gidx_all, ALL, NE // 2, [[1, 1]]), 0))
            seq(pool.memset(fill[:, :], EMPTY))
            pool.dma_start(dr(tbl_d, 0, [[P, P], [1, P]]), fill[:, :]).then_inc(tbl_filled, 16)
            pool.wait_ge(ld_c, 16)
            own.do(pool.tensor_copy(pair_i[:, :], at(cst, ALL, C_PAIR, [[1, 2 * NT]])))
            for off in (0, PAD + T):
                own.do(pool.memset(at(zbuf, ALL, Z_POOL + off, [[PW_, 4], [1, PAD]]), 0.0))
            def grid(off, dims):
                return at(ring, ALL, off, dims)

            pool.wait_ge(pow_done, 1)
            for ri in range(2):
                pw, pc = R_PW + ri * 9 * G, R_PC + ri * 9 * G
                own.settle()
                seq(pool.tensor_copy(at(ring, FWD, pc, [[1, 9 * G]]), at(ring, FWD, pw, [[1, 9 * G]])))
                seq(pool.tensor_copy(at(ring, BWD, pc, [[1, G]]), at(ring, BWD, pw, [[1, G]])))
                seq(pool.tensor_copy(at(ring, BWD, pc + G, [[G, 8], [1, G]]),
                                        at(ring, BWD, pw + 8 * G, [[-G, 8], [1, G]])))
            pool.wait_ge(c_done, 2)
            for b in range(NB):
                g0 = b * GB
                gsc = [[9 * CH, GB], [CH, 9], [1, CH]]
                pw_r = grid(R_PC + g0, [[1, GB], [G, 9], [0, CH]])
                pw_i = grid(R_PC + 9 * G + g0, [[1, GB], [G, 9], [0, CH]])
                c_r = grid(R_CL + g0 * CH, [[CH, GB], [0, 9], [1, CH]])
                c_n = grid(R_CL + 512 + g0 * CH, [[CH, GB], [0, 9], [1, CH]])
                o_r, o_n = grid(R_CW + g0 * 9 * CH, gsc), grid(R_CWN + g0 * 9 * CH, gsc)
                tmp = grid(R_TMP + 1152, gsc)
                own.settle()
                own.do(pool.tensor_tensor(o_r, pw_r, c_r, ALU.mult))
                own.do(pool.tensor_tensor(tmp, pw_i, c_n, ALU.mult))
                own.do(pool.tensor_tensor(o_n, pw_r, c_n, ALU.mult))
                own.settle()
                seq(pool.tensor_tensor(o_r, o_r, tmp, ALU.add))
                seq(pool.tensor_tensor(tmp, pw_i, c_r, ALU.mult))
                pool.tensor_tensor(o_n, o_n, tmp, ALU.subtract).then_inc(cw_built, 1)
                pool.wait_ge(cw_built, b + 1)
            for i, w in enumerate(WINDOWS):
                pool.wait_ge(zp_done, i + 1)
                z = Z_POOL + i * PW_
                src, base, n, k = zbuf, z, 1, 0
                own.settle()
                while n < w:
                    width = PW_ - 2 * n + 1
                    dst = M_PT + k * PW_
                    seq(pool.tensor_tensor(at(moe, ALL, dst, [[1, width]]), at(src, ALL, base, [[1, width]]),
                                           at(src, ALL, base + n, [[1, width]]), ALU.add))
                    src, base, n, k = moe, dst, 2 * n, 1 - k
                mean = M_PT + k * PW_
                seq(pool.tensor_scalar(at(moe, ALL, mean, [[1, T]]), at(moe, ALL, base + PAD - w // 2, [[1, T]]),
                                       1.0 / w, None, ALU.mult))
                for side in range(2):
                    ev = at(moe, ALL, mean + side * (T - PAD), [[1, PAD]])
                    own.do(pool.tensor_tensor(ev, ev, at(cst, ALL, C_EDGE + (2 * i + side) * PAD, [[1, PAD]]),
                                              ALU.mult))
                own.settle()
                zi = at(zbuf, ALL, z + PAD, [[1, T]])
                pool.tensor_tensor(zi, at(moe, ALL, mean, [[1, T]]), zi, ALU.subtract).then_inc(diff_done, 1)
                pool.wait_ge(diff_done, i + 1)
            for n in range(2 * NT):
                pool.wait_ge(wo0_sb, n + 1)
                hv = at(h, ALL, n * 512, [[1, 512]])
                pool.tensor_tensor(hv, hv, at(moe, ALL, M_PT + (n % 2) * 512, [[1, 512]]), ALU.add
                                   ).then_inc(wo0_done, 1)
            pool.wait_ge(wo0_done, 2 * NT)
            own.do(pool.memset(at(moe, ALL, M_XG, [[1, 2 * DM]]), 0.0))
            pool.wait_ge(slot_done, 1)
            pool.wait_ge(tbl_filled, 16)
            own.settle()
            for c in range(2 * NT):
                pool.indirect_dma_start(tbl_d, bass.IndirectOffsetOnAxis(ap=slot_i[:, c:c + 1], axis=0),
                                        pair_i[:, c:c + 1], None).then_inc(tbl_set, 16)
            pool.wait_ge(tbl_set, 16 * 2 * NT)
            for k in range(2):
                pool.dma_start(at(tblw, (k * CAP, (k + 1) * CAP), 0, [[1, NE]]),
                               dr(tbl_d, 0, [[NE, CAP], [1, NE]])).then_inc(tbl_read, 16)
            pool.wait_ge(idx_done, 3)
            pool.wait_ge(v_stored, 16 * NT)
            pairs = pairs_d

            def rows_in(k, done):
                pool.indirect_dma_start(at(moe, ALL, M_XG + k * DM, [[1, DM]]), None, v_d,
                                        bass.IndirectOffsetOnAxis(ap=gidx[k][:, 0:1], axis=0),
                                        bounds_check=T - 1, oob_is_err=False).then_inc(done, 16)

            def rows_out(k, done):
                pool.indirect_dma_start(pairs, bass.IndirectOffsetOnAxis(ap=sidx[k][:, 0:1], axis=0),
                                        at(moe, ALL, M_Y + k * 512, [[1, 512]]), None,
                                        bounds_check=4 * T - 1, oob_is_err=False).then_inc(done, 16)

            def set_gather(pair, k):
                pool.tensor_copy(gidx[k][:, 0:1], at(gidx_all, ALL, pair, [[1, 1]])).then_inc(gi_set, 1)

            def set_scatter(e, k):
                pool.tensor_copy(sidx[k][:, 0:1], at(sidx_all, ALL, e, [[1, 1]])).then_inc(si_set, 1)

            def gather(i, u):
                if not valid(i, u) or u % 2:
                    return
                q, k = i * 2 + u // 2, u // 2
                least(pool, xT_ps, q - 1)
                pool.wait_ge(gi_set, q + 1)
                if u:
                    pool.wait_ge(xg_ready[0], (i + 1) * 16)
                else:
                    least(pool, xg_ready[1], i * 16)
                set_gather(q + 1, 1 - k)
                rows_in(k, xg_ready[k])

            def scatter(i, u):
                if not valid(i, u):
                    return
                e, k = i * RING + u, u % 2
                pool.wait_ge(si_set, e + 1)
                pool.wait_ge(dn_sb, e + 1)
                if not (isinstance(i, int) and e == NE - 1):
                    least(pool, ys_stored[1 - k], i * 32 + 16 * ((u + 1) // 2))
                    set_scatter(e + 1, 1 - k)
                rows_out(k, ys_stored[k])

            def step(i, u):
                gather(*shift(i, u, 3))
                scatter(*shift(i, u, -1))

            set_gather(0, 0)
            set_scatter(0, 0)
            gather(0, 0)
            gather(0, 2)
            sweep(pool, step)
            scatter(NE // RING - 1, RING - 1)
            for k in range(2):
                pool.wait_ge(ys_stored[k], 16 * NE // 2)

            def note(k):
                return pool.tensor_tensor(at(fill, (0, 1), 4 + k, [[1, 1]]), at(fill, (0, 1), 0, [[1, 1]]),
                                          at(fill, (0, 1), 1, [[1, 1]]), ALU.add)

            with pool.If(most(pool) > CAP):
                note(3).then_inc(o_turn, 1)
                with pool.Fori(1, ROUNDS) as r:
                    with pool.Fori(0, NE) as e:
                        turn = pool.snap((r - 1) * NE + e + 1)
                        dma16 = pool.snap(turn * 16)
                        both = pool.snap(turn * 2)
                        place = pool.snap(r * (CAP * NE))
                        pool.wait_ge(o_turn, turn)
                        for k in range(2):
                            pool.dma_start(at(tblw, (k * CAP, (k + 1) * CAP), 0, [[1, NE]]),
                                           dr(tbl_d, place, [[NE, CAP], [1, NE]])).then_inc(o_tbl, 16)
                        pool.wait_ge(o_idx, both)
                        note(0)
                        rows_in(0, o_xg)
                        pool.wait_ge(o_dn_sb, turn)
                        note(1)
                        rows_out(0, o_st)
                        pool.wait_ge(o_st, dma16)
                        note(2).then_inc(o_turn, 1)
            with pool.Else():
                pass
            pool.memset(at(fill, (0, 1), 12, [[1, 1]]), 0).then_inc(moe_done, 1)

        @block.tensor
        def _(pe):
            def mm(o, a, b, start, stop, loose=False):
                return pe.matmul(o, a, b, start=start, stop=stop, skip_group_check=loose)

            def rv(off, n, parts=ALL):
                return at(ring, parts, off, [[1, n]])

            def win(m, dst, col):
                for j in range(KC):
                    last = mm(bank[dst][:, :], at(big, ALL, col + j * DP + m * P, [[1, P]]),
                              at(ut, ALL, j * T, [[1, T]]), j == 0, j == KC - 1)
                return last

            pe.wait_ge(ld_c, 16)
            for t in range(NT):
                pe.wait_ge(xn_done, t + 1)
                for j in range(KC):
                    last = pe.transpose(bank[j][:, t * P:(t + 1) * P], at(moe, ALL, M_XN + t * DM + j * P, [[1, P]]),
                                        ident)
            last.then_inc(turned_ps, 1)
            pe.wait_ge(ut_done, KC)
            pe.wait_ge(lam_done, 1)
            for k, src in enumerate((12, 13, 14, 15)):
                last = pe.transpose(bank[7][:, k * G:(k + 1) * G], lam(src), ident32)
            last.then_inc(lam_ps, 1)
            pe.wait_ge(ld_craw, 64)
            pe.wait_ge(ld_vec, 96)
            for ri in range(2):
                for m in range(NB):
                    pe.transpose(bank[4 + ri][:, m * P:(m + 1) * P], rv(R_CRAW + ri * 512 + m * P, P), ident)
            pe.transpose(bank[6][:, 0:12], at(vrow, (0, 12), 0, [[1, P]]), at(cst, (0, 12), C_ID, [[1, 12]])
                         ).then_inc(c_ps, 1)
            pe.wait_ge(ld_win0, 16)
            for m in range(3):
                win(m, m, 0).then_inc(win_ps, 1)

            def end_states(b):
                pe.wait_ge(wt_done, 4 * (b + 1))
                pe.wait_ge(u_ready[b], 16)
                pe.wait_ge(zs_done, NB)
                if b >= 2:
                    pe.wait_ge(e_done, 4 * (b - 1))
                for ri in range(2):
                    for g in range(GB):
                        last = mm(bank[2 * (b % 2) + ri][:, g * NCH:(g + 1) * NCH],
                                  at(moe, ALL, M_WT + (b % 2) * 2048 + ri * 1024 + g * P, [[1, P]]),
                                  rv(R_U + (b * GB + g) * NCH, NCH), True, True)
                last.then_inc(e_ps, 1)

            def w_rows(b):
                for hb in range(2):
                    pe.wait_ge(w_built, 2 * b + hb + 1)
                    least(pe, wt_done, 2 * (2 * b + hb - 1))
                    for ri in range(2):
                        for g in range(4 * hb, 4 * hb + 4):
                            last = pe.transpose(bank[4 + 2 * ri + hb][:, (g % 4) * P:(g % 4 + 1) * P],
                                                rv(R_W + ri * 1024 + g * P, P), ident)
                    last.then_inc(wt_ps, 1)

            pe.wait_ge(c_done, 2)
            pe.wait_ge(vec_done, 1)
            pe.wait_ge(lam_lane, 2)
            w_rows(0)
            win(3, 3, 0).then_inc(win_ps, 1)
            for b in range(1, NB):
                w_rows(b)
                end_states(b - 1)
            end_states(NB - 1)
            pe.wait_ge(ld_win1, 16)
            pe.wait_ge(e_done, 4 * (NB - 1))
            for m in range(2):
                win(m, m, KC * DP).then_inc(zp_ps, 1)
            pe.wait_ge(wt_done, 4 * NB)
            pe.wait_ge(e_done, 4 * NB)
            pe.wait_ge(cw_built, NB)
            for hh in range(2):
                for i in range(4):
                    for q in range(4):
                        g = hh * 16 + 4 * i + q
                        rows = slice(32 * q, 32 * q + 32)
                        for dst, parts, slot, n in ((0, FWD, 1, 112), (1, BWD, 2, 112), (2, ALL, 0, 16)):
                            for k, (b_off, c_off) in enumerate(((R_BB, R_CW), (R_BBI, R_CWN))):
                                last = mm(bank[K_BANKS[hh][dst]][rows, i * n:(i + 1) * n], rv(b_off + g * CH, 32, parts),
                                          rv(c_off + g * 9 * CH + slot * CH, n, parts), k == 0, k == 1)
                last.then_inc(k_ps, 1)
            for m in range(2, 4):
                pe.wait_ge(zp_done, m - 1)
                win(m, m % 2, KC * DP).then_inc(zp_ps, 1)
            pe.wait_ge(toep_ready, 16 * L)
            pe.wait_ge(k_done, 6)
            pe.wait_ge(zp_done, 4)
            for b in range(NB):
                for g in range(GB):
                    gg = b * GB + g
                    last = mm(bank[b][:, g * NCH:(g + 1) * NCH], rv(R_T + gg * P, P), rv(R_U + gg * NCH, NCH),
                              g == 0, False, True)
            last.then_inc(tu_done, 1)
            pe.wait_ge(ld_poolw, 16 * 8)
            for m in range(4):
                pe.wait_ge(diff_done, m + 1)
                mm(bank[4 + m][:, :], at(moe, ALL, M_PW + m * P, [[1, P]]),
                   at(zbuf, ALL, Z_POOL + m * PW_ + PAD, [[1, T]]), True, True).then_inc(a_ps, 1)

            def wout(n, dst, chunks):
                t, half = n // 2, n % 2
                for c in chunks:
                    last = mm(bank[dst][:, :], at(ut, ALL, c * T + t * P, [[1, P]]),
                              at(big, ALL, c * DM + half * 512, [[1, 512]]), c == chunks[0], c == chunks[-1])
                return last

            def wout0(n):
                least(pe, wo0_sb, n - 3)
                wout(n, 4 + n % 4, range(4)).then_inc(wo0_ps, 1)

            pe.wait_ge(ld_wout0, 16)
            pe.wait_ge(a_done, 4)
            for n in range(4):
                wout0(n)
            for b in range(NB):
                pe.wait_ge(xo_re, 2 * (b // 2 + 1))
                pe.wait_ge(xo_im, 2 * (b // 2 + 1))
                for g in range(GB):
                    gg = b * GB + g
                    for ri, c_off in enumerate((R_CW, R_CWN)):
                        last = mm(bank[b][:, g * NCH:(g + 1) * NCH], rv(c_off + gg * 9 * CH + CH, P),
                                  at(moe, ALL, M_XO + ri * 2048 + gg * NCH, [[1, NCH]]), False,
                                  g == GB - 1 and ri == 1, True)
                last.then_inc(y_ps, 1)
            for n in range(4, 2 * NT):
                wout0(n)
            pe.wait_ge(ld_glu, 16)
            pe.wait_ge(wo0_sb, 2 * NT)
            for m in range(NB):
                for c in range(NB):
                    pe.wait_ge(zg_done, c + 1)
                    last = mm(bank[4 + m][:, :], rv(R_GLU + c * DP + m * P, P), rv(R_ZG + c * T, T),
                              c == 0, c == NB - 1)
                last.then_inc(glu_ps, 1)
            pe.wait_ge(ld_wout1, 16)
            pe.wait_ge(cat_done, NB)
            pe.wait_ge(y_sb, NB)
            def turned(src, base, ready, t):
                pe.wait_ge(ready, t + 1)
                for j in range(KC):
                    last = pe.transpose(bank[2 * t + j // 4][:, (j % 4) * P:(j % 4 + 1) * P],
                                        at(src, ALL, base + t * DM + j * P, [[1, P]]), ident)
                last.then_inc(turned_ps, 1)

            def logits(t):
                pe.wait_ge(ut_done, KC + 2 * (t + 1))
                dst = bank[2 * t][:, 0:36]
                for j in range(KC):
                    mm(dst, at(ut, ALL, j * T + t * P, [[1, P]]), at(rw, ALL, j * 36, [[1, 36]]), j == 0, False)
                mm(dst, at(cst, (0, 1), C_ONE, [[1, P]]), at(rbias, (0, 1), 0, [[1, 36]]), False, True
                   ).then_inc(log_ps, 1)

            for step_t in range(NT + 2):
                if step_t < NT:
                    for n in (2 * step_t, 2 * step_t + 1):
                        wout(n, n, range(4, 8)).then_inc(wo1_ps, 1)
                if 0 <= step_t - 1 < NT:
                    turned(zbuf, 0, v_done, step_t - 1)
                if 0 <= step_t - 2 < NT:
                    logits(step_t - 2)
            pe.wait_ge(mask_done, 1)
            for t in range(NT + 1):
                dst = bank[7][:, t * NE:(t + 1) * NE]
                for k in range(min(t + 1, NT)):
                    last = mm(dst, at(cst, ALL, C_TRI if k == t else C_ONE, [[1, P]]),
                              at(ut, ALL, Q["MS"] + k * NE, [[1, NE]]), k == 0, k == min(t, NT - 1))
            last.then_inc(rank_ps, 1)
            pe.wait_ge(ld_ppw, 32)
            for t in range(NT):
                for j in range(2):
                    last = pe.transpose(bank[1 + j][:, t * P:(t + 1) * P],
                                        at(moe, ALL, M_PIN + t * DPLE + j * P, [[1, P]]), ident)
            last.then_inc(ppt_ps, 1)
            pe.wait_ge(ppt_sb, 2)

            def proj(n):
                t, half = n // 2, n % 2
                least(pe, pp_done, n - 3)
                for j in range(2):
                    last = mm(bank[3 + n % 4][:, :], at(moe, ALL, M_PPT + j * T + t * P, [[1, P]]),
                              at(moe, ALL, M_PPW + j * DM + half * 512, [[1, 512]]), j == 0, j == 1)
                last.then_inc(pp_ps, 1)

            for n in range(2 * NT):
                proj(n)
            pe.wait_ge(pp_done, 2 * NT)

            def x_rows(k):
                for j in range(KC):
                    last = pe.transpose(bank[j // 4 * 6][:, (j % 4) * P:(j % 4 + 1) * P],
                                        at(moe, ALL, M_XG + k * DM + j * P, [[1, P]]), ident)
                return last

            def gate_up(k, odd, slot, dst):
                for j in range(KC):
                    for n in range(2):
                        last = mm(bank[dst][n * CAP:(n + 1) * CAP, 0:DE],
                                  at(moe, ALL, M_XT + k * DM + j * P + odd * CAP, [[1, CAP]]),
                                  rv(slot * SLOT + n * KC * DE + j * DE, DE), j == 0, j == KC - 1)
                return last

            def h_rows():
                return pe.transpose(bank[3][:, 0:P], at(moe, ALL, M_HG, [[1, P]]), ident)

            def down(k, slot, dst):
                for j in range(2):
                    for n in range(2):
                        last = mm(bank[dst][n * CAP:(n + 1) * CAP, :], at(moe, ALL, M_HT + k * P + j * CAP, [[1, CAP]]),
                                  rv(slot * SLOT + 2 * KC * DE + j * DM + n * 512, 512), j == 0, j == 1)
                return last

            def x_step(i, u):
                if not valid(i, u) or u % 2:
                    return
                pe.wait_ge(xg_ready[u // 2], (i + 1) * 16)
                least(pe, xT_sb, i * 4 + u)
                x_rows(u // 2).then_inc(xT_ps, 1)

            def down_step(i, u):
                if not valid(i, u):
                    return
                e = i * RING + u
                pe.wait_ge(hT_sb, e + 1)
                least(pe, dn_sb, e - 1)
                down(u % 2, u, 4 + u % 2).then_inc(dn_ps, 1)

            def step(i, u):
                e = i * RING + u
                pe.wait_ge(xT_sb, i * 4 + (2 if u < 2 else 4))
                pe.wait_ge(w_ready[u], (i + 1) * 48)
                least(pe, hg_sb, 2 * (e - 1))
                gate_up(u // 2, u % 2, u, 1 + u % 2).then_inc(gu_ps, 1)
                x_step(*shift(i, u, 1))
                down_step(*shift(i, u, -1))
                pe.wait_ge(hg_sb, 2 * e + 2)
                least(pe, hT_sb, e)
                h_rows().then_inc(hT_ps, 1)

            pe.wait_ge(log_ps, NT)
            pe.wait_ge(slot_done, 1)
            x_step(0, 0)
            sweep(pe, step)
            down_step(NE // RING - 1, RING - 1)
            with pe.If(most(pe) > CAP):
                with pe.Fori(1, ROUNDS) as r:
                    with pe.Fori(0, NE) as e:
                        turn = pe.snap((r - 1) * NE + e + 1)
                        twice = pe.snap(turn * 2)
                        dma16 = pe.snap(turn * 16)
                        dma48 = pe.snap(turn * 48)
                        pe.wait_ge(o_xg, dma16)
                        x_rows(0).then_inc(o_xT_ps, 1)
                        pe.wait_ge(o_xT, twice)
                        pe.wait_ge(o_w, dma48)
                        gate_up(0, 0, 0, 1).then_inc(o_gu, 1)
                        pe.wait_ge(o_hg, twice)
                        h_rows().then_inc(o_hT_ps, 1)
                        pe.wait_ge(o_hT, turn)
                        down(0, 0, 4).then_inc(o_dn, 1)
            with pe.Else():
                pass
            pe.wait_ge(moe_done, 1)
            def gate(n):
                t, half = n // 2, n % 2
                for j in range(KC):
                    last = mm(bank[n][:, :], at(ut, ALL, j * T + t * P, [[1, P]]), at(big, ALL, j * DM + half * 512, [[1, 512]]),
                              j == 0, j == KC - 1)
                last.then_inc(gate_ps, 1)

            pe.wait_ge(ld_wple, 16)
            for step_t in range(NT + 1):
                if step_t < NT:
                    turned(ring, E_RN, r_done, step_t)
                if step_t >= 1:
                    pe.wait_ge(ut_done, KC + 2 * NT + 2 * step_t)
                    gate(2 * step_t - 2)
                    gate(2 * step_t - 1)


_INS = ["x", "p", "g_mix", "w_in", "pool_w", "pool_scale", "ssm_a_re", "ssm_a_im", "ssm_log_dt", "ssm_b_re",
        "ssm_b_im", "ssm_c_re", "ssm_c_im", "ssm_d", "glu_w", "glu_b", "w_out", "g_ffn", "router_grp_w",
        "router_grp_b", "router_exp_w", "router_exp_b", "exp_w_gate", "exp_w_up", "exp_w_down", "g_ple",
        "ple_gate_w", "ple_gate_b", "ple_proj_w", "g_final"]


def kernel(**inputs):
    import concourse.bacc as _bacc
    from concourse.bass_utils import run_bass_kernel_spmd as _run

    nc = _bacc.Bacc("TRN2", target_bir_lowering=False, num_devices=1)
    arrays, aps = {}, {}
    given = {n: inputs[n] for n in _INS}
    given["consts"] = constants()
    for name, value in given.items():
        a = np.ascontiguousarray(value)
        arrays[f"in_{name}_dram"] = a
        aps[name] = nc.dram_tensor(f"in_{name}_dram", a.shape, mybir.dt.from_np(a.dtype), kind="ExternalInput").ap()
    out = nc.dram_tensor("out_0_dram", (1, T, DM), F32, kind="ExternalOutput").ap()
    build(nc, aps, out)
    r = _run(nc, [arrays], core_ids=[0])
    return r.results[0]["out_0_dram"]
```

```python
from contextlib import ExitStack

import concourse.bass as bass
import numpy as np
from concourse import mybir

ALU = mybir.AluOpType
ACT = mybir.ActivationFunctionType
AX = mybir.AxisListType
F32 = mybir.dt.float32
I32 = mybir.dt.int32

P = 128
T = 512
DM = 1024
NT = T // P
KC = DM // P
DP = 512
WINDOWS = (2, 4, 8, 16)
PAD = 8
PW_ = T + 2 * PAD
G = 32
CH = 16
NS = 64
L = 8
NCH = T // L
GB = 8
NB = G // GB
NG = 4
NEG = 8
NE = NG * NEG
DE = 256
DPLE = 256
EPS = 1e-6
CAP = 64
ROUNDS = T // CAP
RING = 4
TURN = 8
TWO_PI = 6.283185307179586
PI_LO = 3.1415925
TP1 = 6.28125
TP2 = 0.0019350051879882812
TP3 = TWO_PI - TP1 - TP2
ROUND = 12582912.0
EMPTY = 2 * T


def constants():
    ident = np.eye(P, dtype=np.float32)
    tri = np.triu(np.ones((P, P), np.float32), 1)
    ones = np.ones((P, P), np.float32)
    edge = np.ones((4, 2, PAD), np.float32)
    for i, w in enumerate(WINDOWS):
        for k in range(PAD):
            edge[i, 0, k] = w / (min(k - w // 2 + w, T) - max(k - w // 2, 0))
            t = T - PAD + k
            edge[i, 1, k] = w / (min(t - w // 2 + w, T) - max(t - w // 2, 0))
    edge = np.broadcast_to(edge.reshape(1, -1), (P, 64))
    number = np.broadcast_to(np.arange(NE, dtype=np.float32), (P, NE))
    lower = np.broadcast_to(np.arange(NEG, 0, -1).astype(np.float32), (P, NEG))
    pair = (2 * (np.arange(NT)[None, :, None] * P + np.arange(P)[:, None, None])
            + np.arange(2)[None, None, :]).reshape(P, 2 * NT).astype(np.float32)
    half = (np.arange(P) // CAP).astype(np.float32)[:, None]
    place = np.broadcast_to((np.arange(P) % CAP).astype(np.float32), (P, P))
    return np.ascontiguousarray(np.concatenate([ident, tri, ones, edge, number, lower, pair, half, place], 1),
                                np.float32)


C_ID, C_TRI, C_ONE, C_EDGE, C_NUM, C_LOW, C_PAIR, C_HALF, C_PLACE, C_END = (
    0, 128, 256, 384, 448, 480, 488, 496, 497, 625)


def at(t, parts, off, dims):
    p0, p1 = parts
    width = t.shape[1]
    return bass.AP(t, p0 * width + off, [[width, p1 - p0]] + [list(d) for d in dims])


def dr(a, off, dims):
    return bass.AP(a.tensor, off, [list(d) for d in dims])


def least(eng, sem, value):
    if isinstance(value, int) and value <= 0:
        return
    eng.wait_ge(sem, value)


class Chain:

    def __init__(self, eng, sem):
        self.eng, self.sem, self.n = eng, sem, 0

    def do(self, ins):
        ins.then_inc(self.sem, 1)
        self.n += 1
        return self.n

    def settle(self):
        self.eng.wait_ge(self.sem, self.n)


def build(nc, A, out):
    ctx = ExitStack()
    with ctx:
        def sb(name, width, dt=F32):
            return ctx.enter_context(nc.sbuf_tensor(name, [P, width], dt))

        def sem(name):
            return ctx.enter_context(nc.semaphore(name))

        def scratch(name, shape, dt=F32):
            return nc.dram_tensor(name, shape, dt, kind="Internal").ap()

        ALL = (0, P)
        FWD, BWD = (0, NS), (NS, P)
        SLOT = 3 * KC * DE
        ring = sb("ring", RING * SLOT)
        h = sb("h", NT * DM)
        big = sb("big", KC * DM)
        ut = sb("ut", KC * T)
        moe = sb("moe", 6144)
        zbuf = sb("zbuf", NB * T + 4 * PW_)
        cst = sb("cst", C_END)
        rw = sb("rw", KC * (NG + NE))
        vec = sb("vec", 24 + 12)
        small = sb("small", 64 + 8 * G)
        rbias = sb("rbias", NG + NE)
        logit = sb("logit", NT * (NG + NE))
        tblw = sb("tblw", NE, I32)
        gidx_all = sb("gidx_all", NE // 2 + 1, I32)
        sidx_all = sb("sidx_all", NE, I32)
        gidx = [sb(f"gidx{k}", 1, I32) for k in range(TURN // 2)]
        sidx = [sb(f"sidx{k}", 1, I32) for k in range(RING)]
        flag = sb("flag", 1, I32)
        slot_i = sb("slot_i", 2 * NT, I32)
        pair_i = sb("pair_i", 2 * NT, I32)
        fill = sb("fill", P, I32)
        vrow = sb("vrow", P)
        bank = [ctx.enter_context(nc.psum_tensor(f"bank{k}", [P, 512], F32)) for k in range(8)]

        V_MIX, V_FFN, V_PLE, V_POOL, V_D, V_GLU = 0, 8, 16, 24, 28, 32
        S_SS, S_RS, S_EPS, S_W1, S_W2, S_SS2, S_RS2, S_SS3, S_RS3, S_SS4, S_RS4, S_WARM = (
            0, 4, 8, 12, 16, 20, 24, 28, 32, 36, 40, 44)
        S_A2, S_T1, S_T2 = 64, 64 + 4 * G, 64 + 6 * G
        R_CW, R_CWN = 0, 4608
        R_U = 9216
        R_BB, R_BBI = R_U + 2048, R_U + 2048 + 528
        R_CL = R_BB + 1056
        R_W = R_CL + 1024
        R_T = R_W + 2048
        R_X = R_T + 4096
        R_CRAW = R_CW
        R_PW = R_T
        R_PIN = R_PW + 18 * G
        R_PC = R_PIN + 16 * G
        R_COEF = R_PC + 18 * G
        R_TMP = R_COEF + 2 * G
        R_GLU = R_T
        R_Y = R_U
        R_YC = R_X
        R_ZG = R_X + 2048
        R_LAM = R_X
        R_BRAW = R_X + 2560
        assert R_TMP + 2 * 1152 <= R_X and R_X + 65 * 64 <= RING * SLOT
        M_WT, M_XO, M_XN = 0, 0, 0
        M_PT, M_PW = 4096, 4096 + 2 * PW_
        M_PPW, M_PIN, M_PPT = 0, 2048, 3072
        M_XT, M_HG, M_SG, M_HT, M_XG = 0, 2048, 2176, 2432, 4096
        XG = ((moe, M_XG), (moe, M_XG + DM), (ut, 2 * DM), (ut, 3 * DM))
        Z_SSM, Z_POOL = 0, NB * T
        Q = {}
        q = 0
        for name, n in (("gm", NT), ("d4", NT * 4), ("e4", NT * 4), ("gs", NT), ("gp", NT),
                        ("g1", NT * 4), ("g2", NT), ("goh", NT * 4), ("pr", NT * 32), ("sel", NT * 8),
                        ("m1", NT), ("q1", NT * 8), ("q2", NT), ("oh1", NT * 8), ("s2", NT * 8), ("m2", NT),
                        ("q3", NT * 8), ("q4", NT), ("oh2", NT * 8), ("df", NT), ("ex", NT), ("dn", NT),
                        ("M1", NT * 32), ("M2", NT * 32), ("MS", NT * 32), ("px", (NT + 1) * 32), ("oh", 2 * NT * 128),
                        ("rh", 2 * NT * 32), ("pm", 2 * NT),
                        ("pa", 2 * NT * 32), ("pb", 2 * NT * 32), ("r1", NT), ("r2", NT), ("e1", NT), ("e2", NT), ("mx", 1)):
            Q[name] = q
            q += n
        assert q <= 4096

        z_d = scratch("z_d", [P, G * NCH])
        y_d = scratch("y_d", [P, G * NCH])
        k_d = scratch("k_d", [G * CH, 15 * CH])
        v_d = scratch("v_d", [T, DM])
        tbl_d = scratch("tbl_d", [T * NE, 1], I32)
        pairs_d = scratch("pairs_d", [4 * T, DM // 2])

        ld_c, ld_small, ld_vec, ld_win0, ld_win1, ld_b, ld_craw, ld_poolw = (
            sem(n) for n in ("ld_c", "ld_small", "ld_vec", "ld_win0", "ld_win1", "ld_b", "ld_craw", "ld_poolw"))
        ld_x = [sem(f"ld_x{t}") for t in range(NT)]
        ld_wout0, ld_wout1, ld_glu, ld_ppw, ld_wple, ld_fin = (
            sem(n) for n in ("ld_wout0", "ld_wout1", "ld_glu", "ld_ppw", "ld_wple", "ld_fin"))
        gu_ready = [sem(f"gu_ready{k}") for k in range(RING)]
        down_ready = [sem(f"down_ready{k}") for k in range(RING)]
        dve_step, pool_step = sem("dve_step"), sem("pool_step")
        ss_done, rms_root, rstd_done, turned_ps, ut_done = (
            sem(n) for n in ("ss_done", "rms_root", "rstd_done", "turned_ps", "ut_done"))
        xn_done, vec_done = sem("xn_done"), sem("vec_done")
        c_ps, c_done, lam_dt, lam_arg, lam_exp, lam_red, lam_sin, lam_done, lam_ps, lam_lane = (
            sem(n) for n in ("c_ps", "c_done", "lam_dt", "lam_arg", "lam_exp", "lam_red", "lam_sin",
                             "lam_done", "lam_ps", "lam_lane"))
        pow_done, pin_done = sem("pow_done"), sem("pin_done")
        win_ps, zs_done, zs_stored = sem("win_ps"), sem("zs_done"), sem("zs_stored")
        u_ready = [sem(f"u_ready{m}") for m in range(NB)]
        yc_ready = [sem(f"yc_ready{m}") for m in range(NB)]
        w_built, wt_ps, wt_done, e_ps, e_done = (
            sem(n) for n in ("w_built", "wt_ps", "wt_done", "e_ps", "e_done"))
        cw_built, k_ps, k_done, k_stored, toep_ready, tu_done = (
            sem(n) for n in ("cw_built", "k_ps", "k_done", "k_stored", "toep_ready", "tu_done"))
        zp_ps, zp_done, diff_done, a_ps, a_done, wo0_ps, wo0_sb, wo0_done = (
            sem(n) for n in ("zp_ps", "zp_done", "diff_done", "a_ps", "a_done", "wo0_ps", "wo0_sb", "wo0_done"))
        scan_a, scan_b, xo_re, xo_im, y_ps, y_sb, y_stored = (
            sem(n) for n in ("scan_a", "scan_b", "xo_re", "xo_im", "y_ps", "y_sb", "y_stored"))
        yd_done, zg_done, glu_ps, gate_done, cat_done, wo1_ps, h_done = (
            sem(n) for n in ("yd_done", "zg_done", "glu_ps", "gate_done", "cat_done", "wo1_ps", "h_done"))
        v_done, v_stored, log_ps, logit_sb = sem("v_done"), sem("v_stored"), sem("log_ps"), sem("logit_sb")
        d4_done, df_done, ex_done, mask_done, rank_ps, place_done, tbl_ps, slot_done, tbl_filled, tbl_set, idx_done = (
            sem(n) for n in ("d4_done", "df_done", "ex_done", "mask_done", "rank_ps", "place_done", "tbl_ps", "slot_done",
                             "tbl_filled", "tbl_set", "idx_done"))
        ppt_ps, ppt_sb, pp_ps, pp_done = sem("ppt_ps"), sem("ppt_sb"), sem("pp_ps"), sem("pp_done")
        x_zero = sem("x_zero")
        xg_ready = [sem(f"xg_ready{k}") for k in range(TURN // 2)]
        ys_stored = [sem(f"ys_stored{k}") for k in range(RING)]
        gi_set, si_set = sem("gi_set"), sem("si_set")
        xT_ps, xT_sb, gu_ps, sg_sb, hg_sb, hT_ps, hT_sb, dn_ps, dn_sb = (
            sem(n) for n in ("xT_ps", "xT_sb", "gu_ps", "sg_sb", "hg_sb", "hT_ps", "hT_sb", "dn_ps", "dn_sb"))
        o_w, o_tbl, o_idx, o_xg, o_st, o_turn = (sem("o_" + n) for n in ("w", "tbl", "idx", "xg", "st", "turn"))
        moe_done, eps_set = sem("moe_done"), sem("eps_set")
        ld_pairs = [sem(f"ld_pairs{t}") for t in range(NT)]
        comb, r_done, gate_ps, gate_in, gate_sb, gated, fin_done = (
            sem(n) for n in ("comb", "r_done", "gate_ps", "gate_in", "gate_sb", "gated", "fin_done"))
        stored = sem("stored")

        ident = at(cst, ALL, C_ID, [[1, P]])
        ident32 = at(cst, (0, 32), C_ID, [[1, 32]])
        ZP_BANK = (2, 0, 0, 1)
        K_BANKS = ((4, 5, 6), (7, 2, 3))
        ROOT3 = tuple(NT + t + 1 for t in range(NT))
        ROOT4 = tuple(2 * NT + t + 1 for t in range(NT))
        E_YP = (8192, 10240, 12288, 14336)
        E_RN, E_SG, E_O = 16384, 20480, 16384
        M_GF, M_BP = 4096, 5120

        x_d = A["x"].rearrange("b s d -> (b s) d")
        wg_d = A["exp_w_gate"].rearrange("l g e d f -> (l g e) d f")
        wu_d = A["exp_w_up"].rearrange("l g e d f -> (l g e) d f")
        wd_d = A["exp_w_down"].rearrange("l g e f d -> (l g e) f d")
        out_d = out.rearrange("b s d -> (b s) d")


        block = ctx.enter_context(nc.Block())

        def vcol(c):
            return at(vec, ALL, c, [[1, 1]])

        def lam(k):
            return at(ring, (0, G), R_LAM + k * P, [[1, P]])

        def shift(i, u, d):
            return i + (u + d) // TURN, (u + d) % TURN

        def valid(i, u):
            return not isinstance(i, int) or 0 <= i < NE // TURN

        def sweep(eng, step):
            for u in range(TURN):
                step(0, u)
            with eng.Fori(1, NE // TURN - 1) as i:
                for u in range(TURN):
                    step(i, u)
            for u in range(TURN):
                step(NE // TURN - 1, u)

        def most(eng):
            return eng.value_load(at(flag, (0, 1), 0, [[1, 1]]), min_val=0, max_val=T)

        def load_gate_up(eng, e, slot, done):
            for n, w in enumerate((wg_d, wu_d)):
                eng.dma_start(at(ring, ALL, slot * SLOT + n * KC * DE, [[1, KC * DE]]),
                              w[e].rearrange("(p j) f -> p (j f)", p=P)).then_inc(done, 16)

        def load_down(eng, e, slot, done):
            eng.dma_start(at(ring, ALL, slot * SLOT + 2 * KC * DE, [[1, 2 * DM]]),
                          wd_d[e].rearrange("(p j) d -> p (j d)", p=P)).then_inc(done, 16)

        @block.sync
        def _(sp):
            sp.dma_start(cst[:, :], A["consts"]).then_inc(ld_c, 16)
            for t in range(NT):
                sp.dma_start(at(h, ALL, t * DM, [[1, DM]]), x_d[t * P:(t + 1) * P, :]).then_inc(ld_x[t], 16)
            for n, name in enumerate(("g_mix", "g_ffn", "g_ple")):
                sp.dma_start(at(vec, ALL, 8 * n, [[1, KC]]), dr(A[name], 0, [[KC, P], [1, KC]])).then_inc(ld_vec, 16)
            for n, name in enumerate(("pool_scale", "ssm_d", "glu_b")):
                sp.dma_start(at(vrow, (4 * n, 4 * n + 4), 0, [[1, P]]),
                             dr(A[name], 0, [[P, 4], [1, P]])).then_inc(ld_vec, 16)
            sp.dma_start(at(big, ALL, 0, [[DP, KC], [1, DP]]),
                         dr(A["w_in"], DP, [[KC * DM, P], [DM, KC], [1, DP]])).then_inc(ld_win0, 16)
            for n, name in enumerate(("ssm_a_re", "ssm_a_im")):
                sp.dma_start(at(ring, (0, G), R_LAM + n * P, [[NS, 2], [1, NS]]),
                             dr(A[name], 0, [[NS, G], [G * NS, 2], [1, NS]])).then_inc(ld_small, 16)
            for d in range(2):
                sp.dma_start(at(ring, (0, G), R_LAM + 2 * P + d, [[1, 1]]),
                             dr(A["ssm_log_dt"], d * G, [[1, G], [1, 1]])).then_inc(ld_small, 16)
            for n, name in enumerate(("ssm_c_re", "ssm_c_im")):
                for d in range(2):
                    sp.dma_start(at(ring, ALL, R_CRAW + n * 4 * P + d * NS, [[P, NB], [1, NS]]),
                                 dr(A[name], d * G * CH * NS, [[NS, P], [GB * CH * NS, NB], [1, NS]])
                                 ).then_inc(ld_craw, 16)
            for n, name in enumerate(("ssm_b_re", "ssm_b_im")):
                for d in range(2):
                    sp.dma_start(at(ring, (d * NS, d * NS + NS), R_BRAW + n * G * CH, [[CH, G], [1, CH]]),
                                 dr(A[name], d * G * NS * CH, [[CH, NS], [NS * CH, G], [1, CH]])
                                 ).then_inc(ld_b, 16)
            sp.dma_start(at(big, ALL, KC * DP, [[DP, KC], [1, DP]]),
                         dr(A["w_in"], 0, [[KC * DM, P], [DM, KC], [1, DP]])).then_inc(ld_win1, 16)
            sp.wait_ge(turned_ps, 1)
            sp.dma_start(at(moe, ALL, M_PW, [[P, 4], [1, P]]),
                         dr(A["pool_w"], 0, [[P, P], [P * P, 4], [1, P]])).then_inc(ld_poolw, 16)
            sp.dma_start(at(rw, ALL, 0, [[NG + NE, KC], [1, NG]]),
                         dr(A["router_grp_w"], 0, [[KC * NG, P], [NG, KC], [1, NG]])).then_inc(ld_poolw, 16)
            for g in range(NG):
                sp.dma_start(at(rw, ALL, NG + g * NEG, [[NG + NE, KC], [1, NEG]]),
                             dr(A["router_exp_w"], g * DM * NEG, [[KC * NEG, P], [NEG, KC], [1, NEG]])
                             ).then_inc(ld_poolw, 16)
            sp.dma_start(at(rbias, (0, 1), 0, [[1, NG]]), dr(A["router_grp_b"], 0, [[NG, 1], [1, NG]])
                         ).then_inc(ld_poolw, 16)
            sp.dma_start(at(rbias, (0, 1), NG, [[1, NE]]), dr(A["router_exp_b"], 0, [[NE, 1], [1, NE]])
                         ).then_inc(ld_poolw, 16)
            for m in range(NB):
                sp.wait_ge(zs_done, m + 1)
                for g in range(GB):
                    sp.dma_start(dr(z_d, (m * GB + g) * NCH, [[G * NCH, CH], [CH * G * NCH, L], [1, NCH]]),
                                 at(zbuf, (CH * g, CH * g + CH), Z_SSM + m * T, [[NCH, L], [1, NCH]])
                                 ).then_inc(zs_stored, 16)
                sp.wait_ge(zs_stored, 16 * GB * (m + 1))
                sp.dma_start(at(ring, ALL, R_U + m * T, [[1, T]]),
                             dr(z_d, m * T, [[G * NCH, P], [1, T]])).then_inc(u_ready[m], 16)
            sp.wait_ge(win_ps, NB)
            sp.dma_start(at(big, ALL, 0, [[DM, 4], [1, DM]]),
                         dr(A["w_out"], 0, [[DM, P], [P * DM, 4], [1, DM]])).then_inc(ld_wout0, 16)
            for hh in range(2):
                sp.wait_ge(k_done, 3 * (hh + 1))
                for q in range(4):
                    sp.dma_start(dr(k_d, (hh * 16 + q) * CH * 15 * CH,
                                    [[15 * CH, CH], [4 * CH * 15 * CH, 4], [1, 15 * CH]]),
                                 at(ring, (32 * q, 32 * q + CH), R_W + hh * 960, [[240, 4], [1, 240]])
                                 ).then_inc(k_stored, 16)
            sp.wait_ge(k_stored, 16 * 8)
            sp.wait_ge(cw_built, NB)
            for s in range(L):
                sp.dma_start(at(ring, (CH * s, CH * s + CH), R_T, [[P, G], [1, P]]),
                             dr(k_d, (L - 1 - s) * CH, [[15 * CH, CH], [CH * 15 * CH, G], [1, P]])
                             ).then_inc(toep_ready, 16)
            sp.wait_ge(zp_ps, NB)
            sp.dma_start(at(big, ALL, 4 * DM, [[DM, 4], [1, DM]]),
                         dr(A["w_out"], 4 * P * DM, [[DM, P], [P * DM, 4], [1, DM]])).then_inc(ld_wout1, 16)
            sp.wait_ge(tu_done, 1)
            sp.dma_start(at(ring, ALL, R_GLU, [[DP, 4], [1, DP]]),
                         dr(A["glu_w"], 0, [[DP, P], [P * DP, 4], [1, DP]])).then_inc(ld_glu, 16)
            sp.wait_ge(xo_re, 4)
            sp.wait_ge(xo_im, 4)
            for m in range(NB):
                sp.wait_ge(y_sb, m + 1)
                sp.dma_start(dr(y_d, m * T, [[G * NCH, P], [1, T]]),
                             at(ring, ALL, R_Y + m * T, [[1, T]])).then_inc(y_stored, 16)
                sp.wait_ge(y_stored, 16 * (m + 1))
                for g in range(GB):
                    sp.dma_start(at(ring, (CH * g, CH * g + CH), R_YC + m * T, [[NCH, L], [1, NCH]]),
                                 dr(y_d, (m * GB + g) * NCH, [[G * NCH, CH], [CH * G * NCH, L], [1, NCH]])
                                 ).then_inc(yc_ready[m], 16)
            load_gate_up(sp, 0, 0, gu_ready[0])
            load_down(sp, 0, 0, down_ready[0])
            sp.dma_start(at(moe, ALL, M_PIN, [[DPLE, NT], [1, DPLE]]),
                         dr(A["p"], 0, [[DPLE, P], [P * DPLE, NT], [1, DPLE]])).then_inc(ld_ppw, 16)
            sp.dma_start(at(moe, ALL, M_PPW, [[DM, 2], [1, DM]]),
                         dr(A["ple_proj_w"], 0, [[DM, P], [P * DM, 2], [1, DM]])).then_inc(ld_ppw, 16)
            load_gate_up(sp, 1, 1, gu_ready[1])
            load_down(sp, 1, 1, down_ready[1])
            sp.wait_ge(cat_done, NB)
            load_gate_up(sp, 2, 2, gu_ready[2])
            load_down(sp, 2, 2, down_ready[2])
            load_gate_up(sp, 3, 3, gu_ready[3])
            load_down(sp, 3, 3, down_ready[3])
            for t in range(NT):
                sp.wait_ge(v_done, t + 1)
                sp.dma_start(v_d[t * P:(t + 1) * P, :], at(zbuf, ALL, t * DM, [[1, DM]])).then_inc(v_stored, 16)
            sp.wait_ge(wo1_ps, 2 * NT)
            sp.dma_start(at(big, ALL, 0, [[1, KC * DM]]),
                         dr(A["ple_gate_w"], 0, [[KC * DM, P], [1, KC * DM]])).then_inc(ld_wple, 16)
            with sp.Fori(1, NE // RING) as i:
                for u in range(RING):
                    e = sp.snap(i * RING + u)
                    free = sp.snap(i * RING + (u - RING + 1))
                    sp.wait_ge(gu_ps, free)
                    load_gate_up(sp, e, u, gu_ready[u])
                    sp.wait_ge(dn_ps, free)
                    load_down(sp, e, u, down_ready[u])
            with sp.If(most(sp) > CAP):
                with sp.Fori(1, ROUNDS) as r:
                    with sp.Fori(0, NE) as e0:
                        e = sp.snap(e0 + 0)
                        turn = sp.snap((r - 1) * NE + e0 + 1)
                        sp.wait_ge(o_turn, turn)
                        load_gate_up(sp, e, RING - 1, o_w)
                        load_down(sp, e, RING - 1, o_w)
            with sp.Else():
                pass
            sp.wait_ge(moe_done, 1)
            for t in range(NT):
                sp.dma_start(at(ring, ALL, E_YP[t], [[1, 2 * DM]]),
                             dr(pairs_d, t * P * 2 * DM, [[2 * DM, P], [1, 2 * DM]])).then_inc(ld_pairs[t], 16)
            sp.dma_start(at(moe, ALL, M_BP, [[1, DM]]),
                         dr(A["ple_gate_b"], 0, [[0, P], [1, DM]])).then_inc(ld_fin, 16)
            sp.dma_start(at(moe, ALL, M_GF, [[1, DM]]),
                         dr(A["g_final"], 0, [[0, P], [1, DM]])).then_inc(ld_fin, 16)
            for t in range(NT):
                sp.wait_ge(fin_done, t + 1)
                sp.dma_start(out_d[t * P:(t + 1) * P, :], at(ring, ALL, E_O + t * DM, [[1, DM]])
                             ).then_inc(stored, 16)
            sp.wait_ge(stored, 16 * NT)

        @block.scalar
        def _(act):

            def copy(o, i, signal):
                act.activation(o, i, ACT.Copy).then_inc(signal, 1)

            def mean_root(src, junk, ss, t, done):
                act.activation(junk, src, ACT.Square, accum_out=at(small, ALL, ss + t, [[1, 1]])).then_inc(done, 1)

            def warm(k):
                act.activation(at(small, ALL, S_WARM + k, [[1, 1]]), at(small, ALL, S_EPS, [[1, 1]]), ACT.Sqrt)

            def take(j, gain):
                act.activation(at(ut, ALL, j * T, [[1, T]]), bank[j][:, :], ACT.Copy, scale=vcol(gain + j)
                               ).then_inc(ut_done, 1)

            act.wait_ge(eps_set, 1)
            warm(0)
            for t in range(NT):
                act.wait_ge(ld_x[t], 16)
                mean_root(at(h, ALL, t * DM, [[1, DM]]), at(moe, ALL, M_XN + t * DM, [[1, DM]]), S_SS, t, ss_done)
                act.wait_ge(ss_done, t + 1)
                act.activation(at(small, ALL, S_RS + t, [[1, 1]]), at(small, ALL, S_SS + t, [[1, 1]]), ACT.Sqrt,
                               bias=at(small, ALL, S_EPS, [[1, 1]]), scale=1.0 / DM).then_inc(rms_root, 1)
            act.wait_ge(turned_ps, 1)
            act.wait_ge(ld_vec, 96)
            for j in range(0, KC, 2):
                take(j, V_MIX)
            act.wait_ge(ld_small, 64)
            act.activation(at(ring, (0, G), R_LAM + 2 * P + 2, [[1, 2]]), at(ring, (0, G), R_LAM + 2 * P, [[1, 2]]),
                           ACT.Exp).then_inc(lam_dt, 1)
            act.wait_ge(lam_arg, 1)
            act.activation(lam(4), lam(3), ACT.Exp).then_inc(lam_exp, 1)
            act.wait_ge(lam_red, 1)
            act.activation(lam(8), lam(7), ACT.Sin).then_inc(lam_sin, 1)
            act.activation(lam(9), lam(7), ACT.Sin, scale=0.5).then_inc(lam_sin, 1)
            act.wait_ge(lam_ps, 1)
            copy(at(ring, ALL, R_PW + G, [[9 * G, 2], [1, G]]), at(bank[7], ALL, 0, [[G, 2], [1, G]]), lam_lane)
            copy(at(ring, ALL, R_COEF, [[1, 2 * G]]), bank[7][:, 64:128], lam_lane)
            act.wait_ge(c_ps, 1)
            act.activation(at(ring, ALL, R_CL, [[1, 512]]), bank[4][:, :], ACT.Copy).then_inc(c_done, 1)
            act.activation(at(ring, ALL, R_CL + 512, [[1, 512]]), bank[5][:, :], ACT.Copy, scale=-1.0
                           ).then_inc(c_done, 1)
            act.activation(at(vec, ALL, V_POOL, [[1, 12]]), bank[6][:, 0:12], ACT.Copy).then_inc(vec_done, 1)
            act.wait_ge(pow_done, 1)
            for ri in range(2):
                pw, pin = R_PW + ri * 9 * G, R_PIN + ri * 8 * G
                copy(at(ring, FWD, pin, [[G, L], [1, G]]), at(ring, FWD, pw + 7 * G, [[-G, L], [1, G]]), pin_done)
                copy(at(ring, BWD, pin, [[1, L * G]]), at(ring, BWD, pw, [[1, L * G]]), pin_done)

            def zs_out(m):
                act.wait_ge(win_ps, m + 1)
                copy(at(zbuf, ALL, Z_SSM + m * T, [[1, NCH], [NCH, L]]),
                     at(bank[m], ALL, 0, [[L, NCH], [1, L]]), zs_done)

            def wt_out(b):
                for hb in range(2):
                    act.wait_ge(wt_ps, 2 * b + hb + 1)
                    if b >= 2:
                        act.wait_ge(e_ps, b - 1)
                    for ri in range(2):
                        copy(at(moe, ALL, M_WT + (b % 2) * 2048 + ri * 1024 + hb * 512, [[1, 512]]),
                             bank[4 + 2 * ri + hb][:, :], wt_done)

            def e_out(b):
                act.wait_ge(e_ps, b + 1)
                for ri in range(2):
                    src = bank[2 * (b % 2) + ri]
                    copy(at(ring, FWD, R_X + 64 + ri * G + b * GB, [[1, GB], [64, NCH]]),
                         at(src, FWD, 0, [[NCH, GB], [1, NCH]]), e_done)
                    copy(at(ring, BWD, R_X + 64 * NCH + ri * G + b * GB, [[1, GB], [-64, NCH]]),
                         at(src, BWD, 0, [[NCH, GB], [1, NCH]]), e_done)

            for m in range(3):
                zs_out(m)
            wt_out(0)
            zs_out(3)

            def zp_out(m):
                act.wait_ge(zp_ps, m + 1)
                copy(at(zbuf, ALL, Z_POOL + m * PW_ + PAD, [[1, T]]), bank[ZP_BANK[m]][:, :], zp_done)

            for b in range(1, NB):
                wt_out(b)
                e_out(b - 1)
                if b <= 2:
                    zp_out(b - 1)
            e_out(NB - 1)
            zp_out(2)
            act.wait_ge(wt_ps, 2 * NB)
            for hh in range(2):
                act.wait_ge(k_ps, hh + 1)
                for src, off, n in ((K_BANKS[hh][1], 0, 112), (K_BANKS[hh][2], 112, 16), (K_BANKS[hh][0], 128, 112)):
                    copy(at(ring, ALL, R_W + hh * 960 + off, [[240, 4], [1, n]]),
                         at(bank[src], ALL, 0, [[n, 4], [1, n]]), k_done)
            zp_out(3)
            for m in range(4):
                act.wait_ge(a_ps, m + 1)
                act.activation(at(ut, ALL, m * T, [[1, T]]), bank[4 + m][:, :], ACT.Copy, scale=vcol(V_POOL + m)
                               ).then_inc(a_done, 1)
            def wo0_out(n):
                act.wait_ge(wo0_ps, n + 1)
                least(act, wo0_done, n - 1)
                copy(at(moe, ALL, M_PT + (n % 2) * 512, [[1, 512]]), bank[4 + n % 4][:, :], wo0_sb)

            for n in range(4):
                wo0_out(n)
            act.wait_ge(scan_b, NCH - 1)
            for gh in range(2):
                copy(at(moe, FWD, M_XO + gh * 16 * NCH, [[NCH, 16], [1, NCH]]),
                     at(ring, FWD, R_X + gh * 16, [[1, 16], [64, NCH]]), xo_re)
                copy(at(moe, BWD, M_XO + gh * 16 * NCH, [[NCH, 16], [1, NCH]]),
                     at(ring, BWD, R_X + 64 * (NCH - 1) + gh * 16, [[1, 16], [-64, NCH]]), xo_re)
            wo0_out(4)
            wo0_out(5)
            act.wait_ge(tu_done, 1)
            for b in range(NB):
                act.wait_ge(y_ps, b + 1)
                copy(at(ring, ALL, R_Y + b * T, [[1, T]]), bank[b][:, :], y_sb)
            for m in range(NB):
                act.wait_ge(yd_done, m + 1)
                act.activation(at(ring, ALL, R_ZG + m * T, [[1, T]]), at(ring, ALL, R_YC + m * T, [[1, T]]),
                               ACT.Gelu_apprx_tanh).then_inc(zg_done, 1)
                if m >= 2:
                    wo0_out(m + 4)
            for m in range(NB):
                act.wait_ge(glu_ps, m + 1)
                act.activation(at(ring, ALL, R_YC + m * T, [[1, T]]), bank[m][:, :], ACT.Sigmoid,
                               bias=vcol(V_GLU + m)).then_inc(gate_done, 1)
            for t in range(NT):
                act.wait_ge(h_done, 2 * (t + 1))
                mean_root(at(h, ALL, t * DM, [[1, DM]]), at(zbuf, ALL, t * DM, [[1, DM]]), S_SS2, t, ss_done)
                act.wait_ge(ss_done, NT + t + 1)
                act.activation(at(small, ALL, S_RS2 + t, [[1, 1]]), at(small, ALL, S_SS2 + t, [[1, 1]]), ACT.Sqrt,
                               bias=at(small, ALL, S_EPS, [[1, 1]]), scale=1.0 / DM).then_inc(rms_root, 1)
            act.wait_ge(ppt_ps, 1)
            for j in range(2):
                copy(at(moe, ALL, M_PPT + j * T, [[1, T]]), bank[1 + 2 * j][:, :], ppt_sb)
            act.wait_ge(v_stored, 16 * NT)
            act.wait_ge(turned_ps, 1 + NT)
            for n in range(2 * NT):
                act.wait_ge(pp_ps, n + 1)
                copy(at(zbuf, ALL, n * 512, [[1, 512]]), bank[(4, 5, 0, 2)[n % 4]][:, :], pp_done)
            act.wait_ge(d4_done, 1)
            act.activation(at(ut, ALL, Q["e4"], [[1, NT * 4]]), at(ut, ALL, Q["d4"], [[1, NT * 4]]), ACT.Exp
                           ).then_inc(ex_done, 1)
            act.wait_ge(df_done, 1)
            act.activation(at(ut, ALL, Q["ex"], [[1, NT]]), at(ut, ALL, Q["df"], [[1, NT]]), ACT.Exp
                           ).then_inc(ex_done, 1)

            def silu(i, u):
                e = i * TURN + u
                act.wait_ge(gu_ps, e + 1)
                least(act, hg_sb, 2 * e)
                act.activation(at(moe, (0, CAP), M_SG, [[1, DE]]), at(bank[1 + u % 2], (0, CAP), 0, [[1, DE]]),
                               ACT.Silu).then_inc(sg_sb, 1)

            def y_out(i, u):
                if not valid(i, u):
                    return
                act.wait_ge(dn_ps, i * TURN + u + 1)
                least(act, ys_stored[u % RING], (2 * i + u // RING) * 16)
                copy(at(ut, ALL, u % RING * 512, [[1, 512]]), bank[4 + u % 2][:, :], dn_sb)

            def step(i, u):
                silu(i, u)
                y_out(i, u)

            sweep(act, step)
            with act.If(most(act) > CAP):
                act.wait_ge(dn_sb, NE)
                with act.Fori(1, ROUNDS) as r:
                    with act.Fori(0, NE) as e:
                        turn = act.snap((r - 1) * NE + e + 1)
                        count = act.snap(turn + NE)
                        act.wait_ge(gu_ps, count)
                        act.activation(at(moe, (0, CAP), M_SG, [[1, DE]]), at(bank[1], (0, CAP), 0, [[1, DE]]),
                                       ACT.Silu).then_inc(sg_sb, 1)
                        act.wait_ge(dn_ps, count)
                        copy(at(ut, ALL, 0, [[1, 512]]), bank[4][:, :], dn_sb)
            with act.Else():
                pass
            warm(1)
            def root(ss, rs, junk, t, count):
                mean_root(at(h, ALL, t * DM, [[1, DM]]), at(ring, ALL, junk + t * DM, [[1, DM]]), ss, t, ss_done)
                act.wait_ge(ss_done, NT + count)
                act.activation(at(small, ALL, rs + t, [[1, 1]]), at(small, ALL, ss + t, [[1, 1]]), ACT.Sqrt,
                               bias=at(small, ALL, S_EPS, [[1, 1]]), scale=1.0 / DM).then_inc(rms_root, 1)

            def sigmoid(t):
                for n in (2 * t, 2 * t + 1):
                    act.wait_ge(gate_in, n + 1)
                    sg = at(ring, ALL, E_SG + n * 512, [[1, 512]])
                    act.activation(sg, sg, ACT.Sigmoid).then_inc(gate_sb, 1)
                warm(2 + t)

            def norm3(t):
                act.wait_ge(comb, 2 * (t + 1))
                root(S_SS3, S_RS3, E_RN, t, ROOT3[t])

            def norm4(t):
                act.wait_ge(gated, 2 * (t + 1))
                root(S_SS4, S_RS4, E_SG, t, ROOT4[t])

            for t in range(NT - 1):
                norm3(t)
            for t in range(NT):
                sigmoid(t)
                if t == 0:
                    norm3(NT - 1)
                norm4(t)

        @block.vector
        def _(dve):
            own = Chain(dve, dve_step)

            def tt(o, a, b, op):
                return dve.tensor_tensor(o, a, b, op)

            def seq(ins):
                own.do(ins)
                own.settle()

            def inverse(col, n, count):
                dve.wait_ge(rms_root, count)
                o = at(small, ALL, col, [[1, n]])
                dve.reciprocal(o, o).then_inc(rstd_done, 1)
                dve.wait_ge(rstd_done, count)

            def normalise(dst, base, t, col):
                return dve.tensor_scalar(at(dst, ALL, base + t * DM, [[1, P], [P, KC]]),
                                         at(h, ALL, t * DM, [[KC, P], [1, KC]]),
                                         at(small, ALL, col + t, [[1, 1]]), None, ALU.mult)

            dve.memset(at(small, ALL, S_EPS, [[1, 1]]), EPS).then_inc(eps_set, 1)
            for t in range(NT):
                inverse(S_RS + t, 1, t + 1)
                normalise(moe, M_XN, t, S_RS).then_inc(xn_done, 1)
            dve.wait_ge(turned_ps, 1)
            dve.wait_ge(ld_vec, 96)
            for j in range(1, KC, 2):
                dve.tensor_scalar(at(ut, ALL, j * T, [[1, T]]), bank[j][:, :], vcol(V_MIX + j), None, ALU.mult
                                  ).then_inc(ut_done, 1)
            gdn = [[NS, 2], [1, NS]]
            are, aim, dt = lam(0), lam(1), at(ring, (0, G), R_LAM + 2 * P + 2, [[1, 2], [0, NS]])

            def lam3(k):
                return at(ring, (0, G), R_LAM + k * P, gdn)

            dve.wait_ge(lam_dt, 1)
            tt(lam3(3), lam3(0), dt, ALU.mult).then_inc(lam_arg, 1)
            seq(tt(lam3(5), lam3(1), dt, ALU.mult))
            seq(dve.tensor_scalar(lam(6), lam(5), 1.0 / TWO_PI, ROUND, ALU.mult, ALU.add))
            seq(dve.tensor_scalar(lam(6), lam(6), ROUND, None, ALU.subtract))
            seq(dve.scalar_tensor_tensor(lam(5), lam(6), -TP1, lam(5), ALU.mult, ALU.add))
            seq(dve.scalar_tensor_tensor(lam(5), lam(6), -TP2, lam(5), ALU.mult, ALU.add))
            seq(dve.scalar_tensor_tensor(lam(5), lam(6), -TP3, lam(5), ALU.mult, ALU.add))
            dve.tensor_scalar(lam(7), lam(5), PI_LO, -PI_LO, ALU.min, ALU.max).then_inc(lam_red, 1)
            seq(tt(lam(10), are, are, ALU.mult))
            seq(tt(lam(11), aim, aim, ALU.mult))
            seq(tt(lam(10), lam(10), lam(11), ALU.add))
            seq(dve.reciprocal(lam(10), lam(10)))
            dve.wait_ge(lam_sin, 2)
            seq(tt(lam(9), lam(9), lam(9), ALU.mult))
            seq(dve.tensor_scalar(lam(9), lam(9), -2.0, 1.0, ALU.mult, ALU.add))
            dve.wait_ge(lam_exp, 1)
            seq(tt(lam(12), lam(4), lam(9), ALU.mult))
            seq(tt(lam(13), lam(4), lam(8), ALU.mult))
            seq(dve.tensor_scalar(lam(5), lam(12), 1.0, None, ALU.subtract))
            seq(tt(lam(6), lam(5), are, ALU.mult))
            seq(tt(lam(7), lam(13), aim, ALU.mult))
            seq(tt(lam(6), lam(6), lam(7), ALU.add))
            seq(tt(lam(14), lam(6), lam(10), ALU.mult))
            seq(tt(lam(6), lam(13), are, ALU.mult))
            seq(tt(lam(7), lam(5), aim, ALU.mult))
            seq(tt(lam(6), lam(6), lam(7), ALU.subtract))
            tt(lam(15), lam(6), lam(10), ALU.mult).then_inc(lam_done, 1)

            def grid(off, dims):
                return at(ring, ALL, off, dims)

            dve.wait_ge(lam_lane, 2)
            pr, pi = R_PW, R_PW + 9 * G
            own.do(dve.memset(grid(pr, [[1, G]]), 1.0))
            own.do(dve.memset(grid(pi, [[1, G]]), 0.0))
            for lo, n in ((1, 1), (1, 2), (1, 4)):
                by = lo + n - 1
                rng, cst_ = [[G, n], [1, G]], [[0, n], [1, G]]
                src_r, src_i = grid(pr + lo * G, rng), grid(pi + lo * G, rng)
                by_r, by_i = grid(pr + by * G, cst_), grid(pi + by * G, cst_)
                dst_r, dst_i = grid(pr + (by + 1) * G, rng), grid(pi + (by + 1) * G, rng)
                tmp_r, tmp_i = grid(R_TMP, rng), grid(R_TMP + n * G, rng)
                own.settle()
                own.do(tt(dst_r, src_r, by_r, ALU.mult))
                own.do(tt(tmp_r, src_i, by_i, ALU.mult))
                own.do(tt(dst_i, src_r, by_i, ALU.mult))
                own.do(tt(tmp_i, src_i, by_r, ALU.mult))
                own.settle()
                own.do(tt(dst_r, dst_r, tmp_r, ALU.subtract))
                ins = tt(dst_i, dst_i, tmp_i, ALU.add)
                if n < 4:
                    own.do(ins)
                else:
                    ins.then_inc(pow_done, 1)
            dve.wait_ge(pow_done, 1)
            own.settle()
            own.do(dve.tensor_copy(at(small, ALL, S_A2, [[G, 2], [1, G]]), grid(pr + 8 * G, [[0, 2], [1, G]])))
            own.do(dve.tensor_copy(at(small, ALL, S_A2 + 2 * G, [[1, G]]), grid(pi + 8 * G, [[1, G]])))
            own.do(dve.tensor_scalar(at(small, ALL, S_A2 + 3 * G, [[1, G]]), grid(pi + 8 * G, [[1, G]]), -1.0, None, ALU.mult))
            dve.wait_ge(ld_b, 64)
            gc = [[CH, G], [1, CH]]
            cr, ci = grid(R_COEF, [[1, G], [0, CH]]), grid(R_COEF + G, [[1, G], [0, CH]])
            br, bi = grid(R_BRAW, gc), grid(R_BRAW + 512, gc)
            own.do(dve.memset(grid(R_BB + 512, [[1, 16]]), 0.0))
            own.do(dve.memset(grid(R_BBI + 512, [[1, 16]]), 0.0))
            own.do(tt(grid(R_BB, gc), cr, br, ALU.mult))
            own.do(tt(grid(R_TMP, gc), ci, bi, ALU.mult))
            own.do(tt(grid(R_BBI, gc), cr, bi, ALU.mult))
            own.do(tt(grid(R_TMP + 512, gc), ci, br, ALU.mult))
            own.settle()
            own.do(tt(grid(R_BB, gc), grid(R_BB, gc), grid(R_TMP, gc), ALU.subtract))
            own.do(tt(grid(R_BBI, gc), grid(R_BBI, gc), grid(R_TMP + 512, gc), ALU.add))
            dve.wait_ge(pin_done, 4)
            for b in range(NB):
                for hb in range(2):
                    if b:
                        dve.wait_ge(wt_ps, 2 * b + hb - 1)
                    g0 = b * GB + hb * 4
                    gsc = [[P, 4], [CH, L], [1, CH]]
                    pw_r = grid(R_PIN + g0, [[1, 4], [G, L], [0, CH]])
                    pw_i = grid(R_PIN + L * G + g0, [[1, 4], [G, L], [0, CH]])
                    b_r = grid(R_BB + g0 * CH, [[CH, 4], [0, L], [1, CH]])
                    b_i = grid(R_BBI + g0 * CH, [[CH, 4], [0, L], [1, CH]])
                    w_r, w_i = grid(R_W + hb * 512, gsc), grid(R_W + 1024 + hb * 512, gsc)
                    t_r, t_i = grid(R_TMP, gsc), grid(R_TMP + 512, gsc)
                    own.settle()
                    own.do(tt(w_r, pw_r, b_r, ALU.mult))
                    own.do(tt(t_r, pw_i, b_i, ALU.mult))
                    own.do(tt(w_i, pw_r, b_i, ALU.mult))
                    own.do(tt(t_i, pw_i, b_r, ALU.mult))
                    own.settle()
                    own.do(tt(w_r, w_r, t_r, ALU.subtract))
                    tt(w_i, w_i, t_i, ALU.add).then_inc(w_built, 1)
                    dve.wait_ge(w_built, 2 * b + hb + 1)
            dve.memset(grid(R_X, [[1, 64]]), 0.0).then_inc(x_zero, 1)
            dve.wait_ge(e_done, 16)
            a_re2, a_im2 = at(small, ALL, S_A2, [[G, 2], [1, G]]), at(small, ALL, S_A2 + 2 * G, [[G, 2], [1, G]])
            t1, t2 = at(small, ALL, S_T1, [[G, 2], [1, G]]), at(small, ALL, S_T2, [[G, 2], [1, G]])
            UNROLL = 9

            def scan_step(n):
                prev, new = R_X + n * 64 + 64, R_X + n * 64 + 128
                tt(t1, a_re2, grid(prev, [[G, 2], [1, G]]), ALU.mult).then_inc(scan_a, 1)
                tt(t2, a_im2, grid(prev, [[G, 2], [1, G]]), ALU.mult).then_inc(scan_a, 1)
                dve.wait_ge(scan_a, n * 3 + 1)
                tt(grid(new, [[1, 2 * G]]), grid(new, [[1, 2 * G]]), at(small, ALL, S_T1, [[1, 2 * G]]),
                   ALU.add).then_inc(scan_a, 1)
                dve.wait_ge(scan_a, n * 3 + 3)
                tt(grid(new, [[G, 2], [1, G]]), grid(new, [[G, 2], [1, G]]),
                   at(small, ALL, S_T2 + G, [[-G, 2], [1, G]]), ALU.add).then_inc(scan_b, 1)
                dve.wait_ge(scan_b, n + 1)

            assert (NCH - 1) % UNROLL == 0
            with dve.Fori(0, (NCH - 1) // UNROLL) as i:
                for u in range(UNROLL):
                    scan_step(i * UNROLL + u)
            for gh in range(2):
                dve.tensor_copy(at(moe, FWD, M_XO + 2048 + gh * 16 * NCH, [[NCH, 16], [1, NCH]]),
                                at(ring, FWD, R_X + G + gh * 16, [[1, 16], [64, NCH]])).then_inc(xo_im, 1)
                dve.tensor_copy(at(moe, BWD, M_XO + 2048 + gh * 16 * NCH, [[NCH, 16], [1, NCH]]),
                                at(ring, BWD, R_X + 64 * (NCH - 1) + G + gh * 16, [[1, 16], [-64, NCH]])
                                ).then_inc(xo_im, 1)
            for m in range(NB):
                dve.wait_ge(yc_ready[m], 16 * GB)
                yc = at(ring, ALL, R_YC + m * T, [[1, T]])
                dve.scalar_tensor_tensor(yc, at(zbuf, ALL, Z_SSM + m * T, [[1, T]]), vcol(V_D + m), yc,
                                         ALU.mult, ALU.add).then_inc(yd_done, 1)
            for m in range(NB):
                dve.wait_ge(gate_done, m + 1)
                tt(at(ut, ALL, (4 + m) * T, [[1, L], [L, NCH]]), at(ring, ALL, R_ZG + m * T, [[NCH, L], [1, NCH]]),
                   at(ring, ALL, R_YC + m * T, [[NCH, L], [1, NCH]]), ALU.mult).then_inc(cat_done, 1)
            def residual(t):
                for n in (2 * t, 2 * t + 1):
                    dve.wait_ge(wo1_ps, n + 1)
                    hv = at(h, ALL, n * 512, [[1, 512]])
                    tt(hv, bank[n][:, :], hv, ALU.add).then_inc(h_done, 1)

            def norm(t):
                inverse(S_RS2 + t, 1, NT + 1 + t)
                normalise(zbuf, 0, t, S_RS2).then_inc(v_done, 1)

            def turned(t, count, gain, signal):
                dve.wait_ge(turned_ps, count)
                for n in range(2):
                    tt(at(ut, ALL, 4 * n * T + t * P, [[T, 4], [1, P]]), at(bank[2 * t + n], ALL, 0, [[P, 4], [1, P]]),
                       at(vec, ALL, gain + 4 * n, [[1, 4], [0, P]]), ALU.mult).then_inc(signal, 1)

            def logits(t):
                dve.wait_ge(log_ps, t + 1)
                tt_l = at(logit, ALL, t * 36, [[1, 36]])
                dve.tensor_copy(tt_l, bank[2 * t][:, 0:36]).then_inc(logit_sb, 1)

            dve.wait_ge(wo0_done, 2 * NT)
            residual(0)
            residual(1)
            norm(0)
            residual(2)
            norm(1)
            norm(2)
            turned(0, 2, V_FFN, ut_done)
            residual(3)
            turned(1, 3, V_FFN, ut_done)
            logits(0)
            norm(3)
            for t in (2, 3):
                turned(t, t + 2, V_FFN, ut_done)
                logits(t - 1)
            logits(3)

            def qv(name, dims, off=0):
                return at(ut, ALL, Q[name] + off, dims)

            def cv(off, dims):
                return at(cst, ALL, off, dims)

            def peak(o, i, op=ALU.max):
                seq(dve.tensor_reduce(o, i, AX.X, op))

            one, four, eight = [[1, NT]], [[4, NT], [1, 4]], [[NEG, NT], [1, NEG]]
            tge = [[NE, NT], [NEG, NG], [1, NEG]]
            dve.wait_ge(logit_sb, NT)
            peak(qv("gm", one), at(logit, ALL, 0, [[36, NT], [1, 4]]))
            tt(qv("d4", four), at(logit, ALL, 0, [[36, NT], [1, 4]]), qv("gm", [[1, NT], [0, 4]]), ALU.subtract
               ).then_inc(d4_done, 1)
            dve.wait_ge(d4_done, 1)
            seq(dve.scalar_tensor_tensor(qv("g1", four), qv("d4", four), 0.0, cv(C_LOW, [[0, NT], [1, 4]]),
                                         ALU.is_equal, ALU.mult))
            peak(qv("g2", one), qv("g1", four))
            seq(tt(qv("goh", four), qv("g1", four), qv("g2", [[1, NT], [0, 4]]), ALU.is_equal))
            seq(tt(qv("pr", tge), qv("goh", [[4, NT], [1, 4], [0, NEG]]), at(logit, ALL, 4, [[36, NT], [NEG, NG], [1, NEG]]),
                   ALU.mult))
            peak(qv("sel", eight), qv("pr", [[NE, NT], [1, NEG], [NEG, NG]]), ALU.add)

            def first_best(src, best, a, b, hot):
                peak(qv(best, one), qv(src, eight))
                seq(tt(qv(a, eight), qv(src, eight), qv(best, [[1, NT], [0, NEG]]), ALU.is_equal))
                seq(tt(qv(a, eight), qv(a, eight), cv(C_LOW, [[0, NT], [1, NEG]]), ALU.mult))
                peak(qv(b, one), qv(a, eight))
                seq(tt(qv(hot, eight), qv(a, eight), qv(b, [[1, NT], [0, NEG]]), ALU.is_equal))

            first_best("sel", "m1", "q1", "q2", "oh1")
            seq(dve.scalar_tensor_tensor(qv("s2", eight), qv("oh1", eight), -3.0e38, qv("sel", eight),
                                         ALU.mult, ALU.add))
            first_best("s2", "m2", "q3", "q4", "oh2")
            tt(qv("df", one), qv("m2", one), qv("m1", one), ALU.subtract).then_inc(df_done, 1)
            for k in (1, 2):
                own.do(tt(qv(f"M{k}", tge), qv("goh", [[4, NT], [1, 4], [0, NEG]]),
                          qv(f"oh{k}", [[NEG, NT], [0, NG], [1, NEG]]), ALU.mult))
            own.settle()
            seq(tt(qv("MS", [[1, NT * NE]]), qv("M1", [[1, NT * NE]]), qv("M2", [[1, NT * NE]]), ALU.add))
            own.do(dve.memset(qv("px", [[1, NE]]), 0.0))
            seq(dve.tensor_copy(qv("px", [[1, NE]], NE), qv("MS", [[1, NE]])))
            for t in range(1, NT):
                ins = tt(qv("px", [[1, NE]], (t + 1) * NE), qv("px", [[1, NE]], t * NE), qv("MS", [[1, NE]], t * NE),
                         ALU.add)
                if t < NT - 1:
                    seq(ins)
                else:
                    ins.then_inc(mask_done, 1)
            own.do(dve.tensor_scalar(qv("pm", [[1, 2 * NT]]), cv(C_PAIR, [[1, 2 * NT]]), float(EMPTY), None,
                                     ALU.subtract))
            own.settle()
            for k in (1, 2):
                own.do(tt(qv("rh", [[NE, NT], [1, NE]], (k - 1) * NT * NE), qv(f"M{k}", [[NE, NT], [1, NE]]),
                          qv("pm", [[2, NT], [0, NE]], k - 1), ALU.mult))
            dve.wait_ge(rank_ps, 1)
            te = [[NE, NT], [1, NE]]
            for k in (1, 2):
                own.do(tt(qv("pa", te, (k - 1) * NT * NE), qv(f"M{k}", te), at(bank[7], ALL, 0, te), ALU.mult))
            own.settle()
            peak(qv("r1", [[1, 2 * NT]]), qv("pa", [[NE, 2 * NT], [1, NE]]), ALU.add)
            tt(qv("oh", [[P, 2 * NT], [1, P]]), cv(C_PLACE, [[0, 2 * NT], [1, P]]), qv("r1", [[1, 2 * NT], [0, P]]),
               ALU.is_equal).then_inc(place_done, 1)
            own.do(dve.tensor_reduce(at(flag, ALL, 0, [[1, 1]]), at(bank[7], ALL, NT * NE, [[1, NE]]), AX.X, ALU.max))

            def tokens(o, table, done):
                dve.tensor_scalar(o, table, 1, None, ALU.logical_shift_right).then_inc(done, 1)

            def half_rows(o, table, done):
                dve.tensor_scalar(o, table, 2.0, cv(C_HALF, [[1, 1]]), ALU.mult, ALU.add).then_inc(done, 1)

            dve.wait_ge(tbl_ps, 1)
            seq(dve.tensor_scalar(at(tblw, ALL, 0, [[1, NE]]), bank[6][:, 0:NE], float(EMPTY), None, ALU.add))
            for n, parts in enumerate(((0, CAP), (CAP, P))):
                tokens(at(gidx_all, parts, 0, [[1, NE // 2]]), at(tblw, parts, n, [[2, NE // 2]]), idx_done)
            half_rows(at(sidx_all, ALL, 0, [[1, NE]]), at(tblw, ALL, 0, [[1, NE]]), idx_done)

            def x_out(k, signal):
                for n in range(2):
                    tt(at(moe, ALL, M_XT + k * DM + n * 512, [[P, 4], [1, P]]), at(bank[n * 6], ALL, 0, [[P, 4], [1, P]]),
                       at(vec, ALL, V_FFN + 4 * n, [[1, 4], [0, P]]), ALU.mult).then_inc(signal, 1)

            def hidden(src, signal):
                for j in range(2):
                    tt(at(moe, (j * CAP, j * CAP + CAP), M_HG, [[1, P]]), at(moe, (0, CAP), M_SG + j, [[2, P]]),
                       at(src, (CAP, P), j, [[2, P]]), ALU.mult).then_inc(signal, 1)

            def x_step(i, u):
                if not valid(i, u) or u % 2:
                    return
                e = i * TURN + u
                dve.wait_ge(xT_ps, i * (TURN // 2) + u // 2 + 1)
                least(dve, gu_ps, e - 2)
                x_out(u // 2 % 2, xT_sb)

            def step(i, u):
                e = i * TURN + u
                dve.wait_ge(sg_sb, e + 1)
                least(dve, hT_ps, e)
                hidden(bank[1 + u % 2], hg_sb)
                x_step(*shift(i, u, 1))
                dve.wait_ge(hT_ps, e + 1)
                least(dve, dn_ps, e - 1)
                dve.tensor_copy(at(moe, ALL, M_HT + (u % 2) * P, [[1, P]]), bank[3][:, 0:P]).then_inc(hT_sb, 1)

            def weights_and_slots():
                dve.wait_ge(ex_done, 2)
                peak(qv("gs", one), qv("e4", four), ALU.add)
                seq(dve.reciprocal(qv("gp", one), qv("gs", one)))
                seq(dve.tensor_scalar(qv("dn", one), qv("ex", one), 1.0, None, ALU.add))
                seq(dve.reciprocal(qv("dn", one), qv("dn", one)))
                seq(tt(at(small, ALL, S_W1, one), qv("gp", one), qv("dn", one), ALU.mult))
                seq(tt(at(small, ALL, S_W2, one), at(small, ALL, S_W1, one), qv("ex", one), ALU.mult))
                for k in (1, 2):
                    own.do(tt(qv("pb", te, (k - 1) * NT * NE), qv(f"M{k}", te), cv(C_NUM, [[0, NT], [1, NE]]),
                              ALU.mult))
                own.settle()
                peak(qv("e1", [[1, 2 * NT]]), qv("pb", [[NE, 2 * NT], [1, NE]]), ALU.add)
                for k in (1, 2):
                    own.do(dve.scalar_tensor_tensor(at(slot_i, ALL, k - 1, [[2, NT]]), qv(f"r{k}", one), float(NE),
                                                    qv(f"e{k}", one), ALU.mult, ALU.add))
                own.settle()
                dve.memset(qv("mx", [[1, 1]]), 0.0).then_inc(slot_done, 1)

            dve.wait_ge(pp_ps, 2 * NT)
            x_step(0, 0)
            weights_and_slots()
            sweep(dve, step)
            with dve.If(most(dve) > CAP):
                with dve.Fori(1, ROUNDS) as r:
                    with dve.Fori(0, NE) as e:
                        turn = dve.snap((r - 1) * NE + e + 1)
                        twice = dve.snap(turn * 32)
                        count = dve.snap(turn + NE)
                        rows_count = dve.snap(turn + NE // 2)
                        dve.wait_ge(o_tbl, twice)
                        tokens(at(gidx[0], ALL, 0, [[1, 1]]), at(tblw, ALL, e, [[1, 1]]), o_idx)
                        half_rows(at(sidx[0], ALL, 0, [[1, 1]]), at(tblw, ALL, e, [[1, 1]]), o_idx)
                        dve.wait_ge(xT_ps, rows_count)
                        x_out(0, xT_sb)
                        dve.wait_ge(sg_sb, count)
                        hidden(bank[1], hg_sb)
                        dve.wait_ge(hT_ps, count)
                        dve.tensor_copy(at(moe, ALL, M_HT, [[1, P]]), bank[3][:, 0:P]).then_inc(hT_sb, 1)
            with dve.Else():
                pass
            def combine(t):
                dve.wait_ge(ld_pairs[t], 16)
                hv = at(h, ALL, t * DM, [[1, DM]])
                for k, col in enumerate((S_W1, S_W2)):
                    dve.scalar_tensor_tensor(hv, at(ring, ALL, E_YP[t] + k * DM, [[1, DM]]),
                                             at(small, ALL, col + t, [[1, 1]]), hv, ALU.mult, ALU.add
                                             ).then_inc(comb, 1)
                    dve.wait_ge(comb, 2 * t + k + 1)

            def rows(t):
                inverse(S_RS3 + t, 1, NT + ROOT3[t])
                normalise(ring, E_RN, t, S_RS3).then_inc(r_done, 1)

            def gate(n):
                dve.wait_ge(gate_ps, n + 1)
                tt(at(ring, ALL, E_SG + n * 512, [[1, 512]]), bank[n][:, :], at(moe, ALL, M_BP + n % 2 * 512, [[1, 512]]),
                   ALU.add).then_inc(gate_in, 1)

            def gated_sum(n):
                sg, hv = at(ring, ALL, E_SG + n * 512, [[1, 512]]), at(h, ALL, n * 512, [[1, 512]])
                dve.wait_ge(gate_sb, n + 1)
                seq(tt(sg, sg, at(zbuf, ALL, n * 512, [[1, 512]]), ALU.mult))
                tt(hv, hv, sg, ALU.add).then_inc(gated, 1)

            def final(t):
                inverse(S_RS4 + t, 1, NT + ROOT4[t])
                dve.scalar_tensor_tensor(at(ring, ALL, E_O + t * DM, [[1, DM]]), at(h, ALL, t * DM, [[1, DM]]),
                                         at(small, ALL, S_RS4 + t, [[1, 1]]), at(moe, ALL, M_GF, [[1, DM]]),
                                         ALU.mult, ALU.mult).then_inc(fin_done, 1)

            def turned_g_ple(t):
                turned(t, 1 + NT + t + 1, V_PLE, ut_done)

            for t in range(2):
                combine(t)
                rows(t)
                turned_g_ple(t)
            combine(2)
            rows(2)
            dve.wait_ge(ld_fin, 32)
            for t in range(NT):
                gate(2 * t)
                if t + 2 < NT:
                    turned_g_ple(t + 2)
                gate(2 * t + 1)
                if t == NT - 1:
                    gated_sum(2 * t)
                    gated_sum(2 * t + 1)
                    final(t - 1)
                if t + 3 < NT:
                    combine(t + 3)
                    rows(t + 3)
                if 0 < t < NT - 1:
                    final(t - 1)
            final(NT - 1)

        @block.gpsimd
        def _(pool):
            own = Chain(pool, pool_step)

            def seq(ins):
                own.do(ins)
                own.settle()

            own.do(pool.memset(at(gidx_all, ALL, NE // 2, [[1, 1]]), 0))
            seq(pool.memset(fill[:, :], EMPTY))
            pool.dma_start(dr(tbl_d, 0, [[P, P], [1, P]]), fill[:, :]).then_inc(tbl_filled, 16)
            pool.wait_ge(ld_c, 16)
            own.do(pool.tensor_copy(pair_i[:, :], at(cst, ALL, C_PAIR, [[1, 2 * NT]])))
            for off in (0, PAD + T):
                own.do(pool.memset(at(zbuf, ALL, Z_POOL + off, [[PW_, 4], [1, PAD]]), 0.0))
            def grid(off, dims):
                return at(ring, ALL, off, dims)

            pool.wait_ge(pow_done, 1)
            for ri in range(2):
                pw, pc = R_PW + ri * 9 * G, R_PC + ri * 9 * G
                own.settle()
                seq(pool.tensor_copy(at(ring, FWD, pc, [[1, 9 * G]]), at(ring, FWD, pw, [[1, 9 * G]])))
                seq(pool.tensor_copy(at(ring, BWD, pc, [[1, G]]), at(ring, BWD, pw, [[1, G]])))
                seq(pool.tensor_copy(at(ring, BWD, pc + G, [[G, 8], [1, G]]),
                                        at(ring, BWD, pw + 8 * G, [[-G, 8], [1, G]])))
            pool.wait_ge(c_done, 2)
            for b in range(NB):
                g0 = b * GB
                gsc = [[9 * CH, GB], [CH, 9], [1, CH]]
                pw_r = grid(R_PC + g0, [[1, GB], [G, 9], [0, CH]])
                pw_i = grid(R_PC + 9 * G + g0, [[1, GB], [G, 9], [0, CH]])
                c_r = grid(R_CL + g0 * CH, [[CH, GB], [0, 9], [1, CH]])
                c_n = grid(R_CL + 512 + g0 * CH, [[CH, GB], [0, 9], [1, CH]])
                o_r, o_n = grid(R_CW + g0 * 9 * CH, gsc), grid(R_CWN + g0 * 9 * CH, gsc)
                tmp = grid(R_TMP + 1152, gsc)
                own.settle()
                own.do(pool.tensor_tensor(o_r, pw_r, c_r, ALU.mult))
                own.do(pool.tensor_tensor(tmp, pw_i, c_n, ALU.mult))
                own.do(pool.tensor_tensor(o_n, pw_r, c_n, ALU.mult))
                own.settle()
                seq(pool.tensor_tensor(o_r, o_r, tmp, ALU.add))
                seq(pool.tensor_tensor(tmp, pw_i, c_r, ALU.mult))
                pool.tensor_tensor(o_n, o_n, tmp, ALU.subtract).then_inc(cw_built, 1)
                pool.wait_ge(cw_built, b + 1)
            for i, w in enumerate(WINDOWS):
                pool.wait_ge(zp_done, i + 1)
                z = Z_POOL + i * PW_
                src, base, n, k = zbuf, z, 1, 0
                own.settle()
                while n < w:
                    width = PW_ - 2 * n + 1
                    dst = M_PT + k * PW_
                    seq(pool.tensor_tensor(at(moe, ALL, dst, [[1, width]]), at(src, ALL, base, [[1, width]]),
                                           at(src, ALL, base + n, [[1, width]]), ALU.add))
                    src, base, n, k = moe, dst, 2 * n, 1 - k
                mean = M_PT + k * PW_
                seq(pool.tensor_scalar(at(moe, ALL, mean, [[1, T]]), at(moe, ALL, base + PAD - w // 2, [[1, T]]),
                                       1.0 / w, None, ALU.mult))
                for side in range(2):
                    ev = at(moe, ALL, mean + side * (T - PAD), [[1, PAD]])
                    own.do(pool.tensor_tensor(ev, ev, at(cst, ALL, C_EDGE + (2 * i + side) * PAD, [[1, PAD]]),
                                              ALU.mult))
                own.settle()
                zi = at(zbuf, ALL, z + PAD, [[1, T]])
                pool.tensor_tensor(zi, at(moe, ALL, mean, [[1, T]]), zi, ALU.subtract).then_inc(diff_done, 1)
                pool.wait_ge(diff_done, i + 1)
            for n in range(2 * NT):
                pool.wait_ge(wo0_sb, n + 1)
                hv = at(h, ALL, n * 512, [[1, 512]])
                pool.tensor_tensor(hv, hv, at(moe, ALL, M_PT + (n % 2) * 512, [[1, 512]]), ALU.add
                                   ).then_inc(wo0_done, 1)
            pool.wait_ge(wo0_done, 2 * NT)
            own.do(pool.memset(at(moe, ALL, M_XG, [[1, 2 * DM]]), 0.0))
            pool.wait_ge(tbl_filled, 16)
            own.settle()
            pool.wait_ge(idx_done, 3)
            pool.wait_ge(v_stored, 16 * NT)
            pairs = pairs_d

            def rows_in(k, done):
                pool.indirect_dma_start(at(XG[k][0], ALL, XG[k][1], [[1, DM]]), None, v_d,
                                        bass.IndirectOffsetOnAxis(ap=gidx[k][:, 0:1], axis=0),
                                        bounds_check=T - 1, oob_is_err=False).then_inc(done, 16)

            def rows_out(u, done):
                pool.indirect_dma_start(pairs, bass.IndirectOffsetOnAxis(ap=sidx[u][:, 0:1], axis=0),
                                        at(ut, ALL, u * 512, [[1, 512]]), None,
                                        bounds_check=4 * T - 1, oob_is_err=False).then_inc(done, 16)

            def set_gather(pair, k):
                pool.tensor_copy(gidx[k][:, 0:1], at(gidx_all, ALL, pair, [[1, 1]])).then_inc(gi_set, 1)

            def set_scatter(e, k):
                pool.tensor_copy(sidx[k][:, 0:1], at(sidx_all, ALL, e, [[1, 1]])).then_inc(si_set, 1)

            def gather(i, u):
                if not valid(i, u) or u % 2:
                    return
                q, k, after = i * (TURN // 2) + u // 2, u // 2, (u // 2 + 1) % (TURN // 2)
                least(pool, xT_ps, q - 3)
                pool.wait_ge(gi_set, q + 1)
                least(pool, xg_ready[after], (i + (after == 0)) * 16)
                set_gather(q + 1, after)
                rows_in(k, xg_ready[k])

            def scatter(i, u):
                e, k, after = i * TURN + u, u % RING, (u + 1) % RING
                pool.wait_ge(si_set, e + 1)
                pool.wait_ge(dn_sb, e + 1)
                if not (isinstance(i, int) and e == NE - 1):
                    least(pool, ys_stored[after], (2 * i + u // RING + (after == 0)) * 16)
                    set_scatter(e + 1, after)
                rows_out(k, ys_stored[k])

            def step(i, u):
                gather(*shift(i, u, TURN))
                scatter(i, u)

            set_gather(0, 0)
            set_scatter(0, 0)
            gather(0, 0)
            gather(0, 2)
            pool.wait_ge(slot_done, 1)
            seq(pool.memset(at(ut, ALL, 2 * DM, [[1, 2 * DM]]), 0.0))
            gather(0, 4)
            gather(0, 6)
            sweep(pool, step)
            for k in range(RING):
                pool.wait_ge(ys_stored[k], 16 * NE // RING)

            def note(k):
                return pool.tensor_tensor(at(fill, (0, 1), 4 + k, [[1, 1]]), at(fill, (0, 1), 0, [[1, 1]]),
                                          at(fill, (0, 1), 1, [[1, 1]]), ALU.add)

            with pool.If(most(pool) > CAP):
                pool.wait_ge(slot_done, 1)
                for c in range(2 * NT):
                    pool.indirect_dma_start(tbl_d, bass.IndirectOffsetOnAxis(ap=slot_i[:, c:c + 1], axis=0),
                                            pair_i[:, c:c + 1], None).then_inc(tbl_set, 16)
                pool.wait_ge(tbl_set, 16 * 2 * NT)
                note(3).then_inc(o_turn, 1)
                with pool.Fori(1, ROUNDS) as r:
                    with pool.Fori(0, NE) as e:
                        turn = pool.snap((r - 1) * NE + e + 1)
                        dma16 = pool.snap(turn * 16)
                        both = pool.snap(turn * 2)
                        count = pool.snap(turn + NE)
                        place = pool.snap(r * (CAP * NE))
                        pool.wait_ge(o_turn, turn)
                        for k in range(2):
                            pool.dma_start(at(tblw, (k * CAP, (k + 1) * CAP), 0, [[1, NE]]),
                                           dr(tbl_d, place, [[NE, CAP], [1, NE]])).then_inc(o_tbl, 16)
                        pool.wait_ge(o_idx, both)
                        note(0)
                        rows_in(0, o_xg)
                        pool.wait_ge(dn_sb, count)
                        note(1)
                        rows_out(0, o_st)
                        pool.wait_ge(o_st, dma16)
                        note(2).then_inc(o_turn, 1)
            with pool.Else():
                pass
            pool.memset(at(fill, (0, 1), 12, [[1, 1]]), 0).then_inc(moe_done, 1)
            for n in range(2 * (NT - 1)):
                sg, hv = at(ring, ALL, E_SG + n * 512, [[1, 512]]), at(h, ALL, n * 512, [[1, 512]])
                pool.wait_ge(gate_sb, n + 1)
                seq(pool.tensor_tensor(sg, sg, at(zbuf, ALL, n * 512, [[1, 512]]), ALU.mult))
                pool.tensor_tensor(hv, hv, sg, ALU.add).then_inc(gated, 1)

        @block.tensor
        def _(pe):
            def mm(o, a, b, start, stop, loose=False):
                return pe.matmul(o, a, b, start=start, stop=stop, skip_group_check=loose)

            def rv(off, n, parts=ALL):
                return at(ring, parts, off, [[1, n]])

            def win(m, dst, col):
                for j in range(KC):
                    last = mm(bank[dst][:, :], at(big, ALL, col + j * DP + m * P, [[1, P]]),
                              at(ut, ALL, j * T, [[1, T]]), j == 0, j == KC - 1)
                return last

            pe.wait_ge(ld_c, 16)
            for t in range(NT):
                pe.wait_ge(xn_done, t + 1)
                for j in range(KC):
                    last = pe.transpose(bank[j][:, t * P:(t + 1) * P], at(moe, ALL, M_XN + t * DM + j * P, [[1, P]]),
                                        ident)
            last.then_inc(turned_ps, 1)
            pe.wait_ge(ut_done, KC)
            pe.wait_ge(ld_win0, 16)
            win(0, 0, 0).then_inc(win_ps, 1)
            pe.wait_ge(lam_done, 1)
            for k, src in enumerate((12, 13, 14, 15)):
                last = pe.transpose(bank[7][:, k * G:(k + 1) * G], lam(src), ident32)
            last.then_inc(lam_ps, 1)
            pe.wait_ge(ld_craw, 64)
            pe.wait_ge(ld_vec, 96)
            for ri in range(2):
                for m in range(NB):
                    pe.transpose(bank[4 + ri][:, m * P:(m + 1) * P], rv(R_CRAW + ri * 512 + m * P, P), ident)
            pe.transpose(bank[6][:, 0:12], at(vrow, (0, 12), 0, [[1, P]]), at(cst, (0, 12), C_ID, [[1, 12]])
                         ).then_inc(c_ps, 1)
            for m in range(1, 3):
                win(m, m, 0).then_inc(win_ps, 1)

            def end_states(b):
                pe.wait_ge(wt_done, 4 * (b + 1))
                pe.wait_ge(u_ready[b], 16)
                pe.wait_ge(zs_done, NB)
                if b >= 2:
                    pe.wait_ge(e_done, 4 * (b - 1))
                least(pe, zp_done, min(b, 2))
                for ri in range(2):
                    for g in range(GB):
                        last = mm(bank[2 * (b % 2) + ri][:, g * NCH:(g + 1) * NCH],
                                  at(moe, ALL, M_WT + (b % 2) * 2048 + ri * 1024 + g * P, [[1, P]]),
                                  rv(R_U + (b * GB + g) * NCH, NCH), True, True)
                last.then_inc(e_ps, 1)

            def w_rows(b):
                for hb in range(2):
                    pe.wait_ge(w_built, 2 * b + hb + 1)
                    least(pe, wt_done, 2 * (2 * b + hb - 1))
                    for ri in range(2):
                        for g in range(4 * hb, 4 * hb + 4):
                            last = pe.transpose(bank[4 + 2 * ri + hb][:, (g % 4) * P:(g % 4 + 1) * P],
                                                rv(R_W + ri * 1024 + g * P, P), ident)
                    last.then_inc(wt_ps, 1)

            pe.wait_ge(c_done, 2)
            pe.wait_ge(vec_done, 1)
            pe.wait_ge(lam_lane, 2)
            w_rows(0)
            win(3, 3, 0).then_inc(win_ps, 1)
            for b in range(1, NB):
                w_rows(b)
                end_states(b - 1)
                if b <= 2:
                    pe.wait_ge(ld_win1, 16)
                    least(pe, e_done, 4 * (b - 1))
                    win(b - 1, ZP_BANK[b - 1], KC * DP).then_inc(zp_ps, 1)
            end_states(NB - 1)
            pe.wait_ge(zp_done, 2)
            pe.wait_ge(e_done, 4 * (NB - 1))
            win(2, ZP_BANK[2], KC * DP).then_inc(zp_ps, 1)
            pe.wait_ge(wt_done, 4 * NB)
            pe.wait_ge(e_done, 4 * NB)
            pe.wait_ge(cw_built, NB)
            for hh in range(2):
                for i in range(4):
                    for q in range(4):
                        g = hh * 16 + 4 * i + q
                        rows = slice(32 * q, 32 * q + 32)
                        for dst, parts, slot, n in ((0, FWD, 1, 112), (1, BWD, 2, 112), (2, ALL, 0, 16)):
                            for k, (b_off, c_off) in enumerate(((R_BB, R_CW), (R_BBI, R_CWN))):
                                last = mm(bank[K_BANKS[hh][dst]][rows, i * n:(i + 1) * n], rv(b_off + g * CH, 32, parts),
                                          rv(c_off + g * 9 * CH + slot * CH, n, parts), k == 0, k == 1)
                last.then_inc(k_ps, 1)
            win(3, ZP_BANK[3], KC * DP).then_inc(zp_ps, 1)
            pe.wait_ge(toep_ready, 16 * L)
            pe.wait_ge(k_done, 6)
            pe.wait_ge(zp_done, 4)
            for b in range(NB):
                for g in range(GB):
                    gg = b * GB + g
                    last = mm(bank[b][:, g * NCH:(g + 1) * NCH], rv(R_T + gg * P, P), rv(R_U + gg * NCH, NCH),
                              g == 0, False, True)
            last.then_inc(tu_done, 1)
            pe.wait_ge(ld_poolw, 16 * 8)
            for m in range(4):
                pe.wait_ge(diff_done, m + 1)
                mm(bank[4 + m][:, :], at(moe, ALL, M_PW + m * P, [[1, P]]),
                   at(zbuf, ALL, Z_POOL + m * PW_ + PAD, [[1, T]]), True, True).then_inc(a_ps, 1)

            def wout(n, dst, chunks):
                t, half = n // 2, n % 2
                for c in chunks:
                    if n == 0 and c >= 4:
                        pe.wait_ge(cat_done, c - 3)
                    last = mm(bank[dst][:, :], at(ut, ALL, c * T + t * P, [[1, P]]),
                              at(big, ALL, c * DM + half * 512, [[1, 512]]), c == chunks[0], c == chunks[-1])
                return last

            def wout0(n):
                least(pe, wo0_sb, n - 3)
                wout(n, 4 + n % 4, range(4)).then_inc(wo0_ps, 1)

            pe.wait_ge(ld_wout0, 16)
            pe.wait_ge(a_done, 4)
            for n in range(6):
                wout0(n)
            for b in range(NB):
                pe.wait_ge(xo_re, 2 * (b // 2 + 1))
                pe.wait_ge(xo_im, 2 * (b // 2 + 1))
                for g in range(GB):
                    gg = b * GB + g
                    for ri, c_off in enumerate((R_CW, R_CWN)):
                        last = mm(bank[b][:, g * NCH:(g + 1) * NCH], rv(c_off + gg * 9 * CH + CH, P),
                                  at(moe, ALL, M_XO + ri * 2048 + gg * NCH, [[1, NCH]]), False,
                                  g == GB - 1 and ri == 1, True)
                last.then_inc(y_ps, 1)
            pe.wait_ge(ld_glu, 16)
            pe.wait_ge(y_sb, NB)
            for c, n in enumerate((None, None, 6, 7)):
                if n:
                    wout0(n)
                pe.wait_ge(zg_done, c + 1)
                for m in range(NB):
                    last = mm(bank[m][:, :], rv(R_GLU + c * DP + m * P, P), rv(R_ZG + c * T, T),
                              c == 0, c == NB - 1)
                    if c == NB - 1:
                        last.then_inc(glu_ps, 1)
            pe.wait_ge(ld_wout1, 16)
            def turned(src, base, ready, t):
                pe.wait_ge(ready, t + 1)
                for j in range(KC):
                    last = pe.transpose(bank[2 * t + j // 4][:, (j % 4) * P:(j % 4 + 1) * P],
                                        at(src, ALL, base + t * DM + j * P, [[1, P]]), ident)
                last.then_inc(turned_ps, 1)

            def logits(t):
                pe.wait_ge(ut_done, KC + 2 * (t + 1))
                dst = bank[2 * t][:, 0:36]
                for j in range(KC):
                    mm(dst, at(ut, ALL, j * T + t * P, [[1, P]]), at(rw, ALL, j * 36, [[1, 36]]), j == 0, False)
                mm(dst, at(cst, (0, 1), C_ONE, [[1, P]]), at(rbias, (0, 1), 0, [[1, 36]]), False, True
                   ).then_inc(log_ps, 1)

            for t in range(NT):
                if t == NT - 1:
                    turned(zbuf, 0, v_done, 0)
                for n in (2 * t, 2 * t + 1):
                    wout(n, n, range(4, 8)).then_inc(wo1_ps, 1)
            for t in range(1, NT):
                turned(zbuf, 0, v_done, t)
                logits(t - 1)
                if t == 2:
                    pe.wait_ge(ld_ppw, 32)
                    for k in range(NT):
                        for j in range(2):
                            last = pe.transpose(bank[1 + 2 * j][:, k * P:(k + 1) * P],
                                                at(moe, ALL, M_PIN + k * DPLE + j * P, [[1, P]]), ident)
                    last.then_inc(ppt_ps, 1)
            logits(NT - 1)
            def rank():
                pe.wait_ge(mask_done, 1)
                mm(bank[7][:, 0:NT * NE], at(cst, ALL, C_TRI, [[1, P]]), at(ut, ALL, Q["MS"], [[1, NT * NE]]),
                   True, False, True)
                mm(bank[7][:, 0:(NT + 1) * NE], at(cst, ALL, C_ONE, [[1, P]]),
                   at(ut, ALL, Q["px"], [[1, (NT + 1) * NE]]), False, True, True).then_inc(rank_ps, 1)

            def table():
                pe.wait_ge(place_done, 1)
                for n in range(2 * NT):
                    last = mm(bank[6][:, 0:NE], at(ut, ALL, Q["oh"] + n * P, [[1, P]]),
                              at(ut, ALL, Q["rh"] + n * NE, [[1, NE]]), n == 0, n == 2 * NT - 1)
                last.then_inc(tbl_ps, 1)

            pe.wait_ge(logit_sb, NT)
            pe.wait_ge(ppt_sb, 2)

            def proj(n):
                t, half = n // 2, n % 2
                least(pe, pp_done, n - 3)
                for j in range(2):
                    last = mm(bank[(4, 5, 0, 2)[n % 4]][:, :], at(moe, ALL, M_PPT + j * T + t * P, [[1, P]]),
                              at(moe, ALL, M_PPW + j * DM + half * 512, [[1, 512]]), j == 0, j == 1)
                last.then_inc(pp_ps, 1)

            proj(0)
            proj(1)
            rank()
            proj(2)
            table()
            for n in range(3, 2 * NT):
                proj(n)
            pe.wait_ge(pp_done, 2 * NT)

            def x_rows(k):
                for j in range(KC):
                    last = pe.transpose(bank[j // 4 * 6][:, (j % 4) * P:(j % 4 + 1) * P],
                                        at(XG[k][0], ALL, XG[k][1] + j * P, [[1, P]]), ident)
                return last

            def gate_up(k, odd, slot, dst):
                for j in range(KC):
                    for n in range(2):
                        last = mm(bank[dst][n * CAP:(n + 1) * CAP, 0:DE],
                                  at(moe, ALL, M_XT + k * DM + j * P + odd * CAP, [[1, CAP]]),
                                  rv(slot * SLOT + n * KC * DE + j * DE, DE), j == 0, j == KC - 1)
                return last

            def h_rows():
                return pe.transpose(bank[3][:, 0:P], at(moe, ALL, M_HG, [[1, P]]), ident)

            def down(k, slot, dst):
                for j in range(2):
                    for n in range(2):
                        last = mm(bank[dst][n * CAP:(n + 1) * CAP, :], at(moe, ALL, M_HT + k * P + j * CAP, [[1, CAP]]),
                                  rv(slot * SLOT + 2 * KC * DE + j * DM + n * 512, 512), j == 0, j == 1)
                return last

            def x_step(i, u):
                if not valid(i, u) or u % 2:
                    return
                pe.wait_ge(xg_ready[u // 2], (i + 1) * 16)
                least(pe, xT_sb, i * TURN + u)
                x_rows(u // 2).then_inc(xT_ps, 1)

            def step(i, u):
                e, slot, load = i * TURN + u, u % RING, 2 * i + u // RING + 1
                pe.wait_ge(xT_sb, i * TURN + u // 2 * 2 + 2)
                pe.wait_ge(gu_ready[slot], load * 32)
                least(pe, hg_sb, 2 * (e - 1))
                gate_up(u // 2 % 2, u % 2, slot, 1 + u % 2).then_inc(gu_ps, 1)
                x_step(*shift(i, u, 1))
                pe.wait_ge(hg_sb, 2 * e + 2)
                least(pe, hT_sb, e)
                h_rows().then_inc(hT_ps, 1)
                pe.wait_ge(hT_sb, e + 1)
                pe.wait_ge(down_ready[slot], load * 16)
                least(pe, dn_sb, e - 1)
                down(u % 2, slot, 4 + u % 2).then_inc(dn_ps, 1)

            x_step(0, 0)
            sweep(pe, step)
            pe.wait_ge(slot_done, 1)
            with pe.If(most(pe) > CAP):
                with pe.Fori(1, ROUNDS) as r:
                    with pe.Fori(0, NE) as e:
                        turn = pe.snap((r - 1) * NE + e + 1)
                        count = pe.snap(turn + NE)
                        x_count = pe.snap(turn * 2 + NE)
                        h_count = pe.snap(turn * 2 + 2 * NE)
                        dma16 = pe.snap(turn * 16)
                        dma48 = pe.snap(turn * 48)
                        pe.wait_ge(o_xg, dma16)
                        x_rows(0).then_inc(xT_ps, 1)
                        pe.wait_ge(xT_sb, x_count)
                        pe.wait_ge(o_w, dma48)
                        gate_up(0, 0, RING - 1, 1).then_inc(gu_ps, 1)
                        pe.wait_ge(hg_sb, h_count)
                        h_rows().then_inc(hT_ps, 1)
                        pe.wait_ge(hT_sb, count)
                        down(0, RING - 1, 4).then_inc(dn_ps, 1)
            with pe.Else():
                pass
            pe.wait_ge(moe_done, 1)
            def gate(n):
                t, half = n // 2, n % 2
                for j in range(KC):
                    last = mm(bank[n][:, :], at(ut, ALL, j * T + t * P, [[1, P]]), at(big, ALL, j * DM + half * 512, [[1, 512]]),
                              j == 0, j == KC - 1)
                last.then_inc(gate_ps, 1)

            pe.wait_ge(ld_wple, 16)
            turned(ring, E_RN, r_done, 0)
            for t in range(NT):
                pe.wait_ge(ut_done, KC + 2 * NT + 2 * (t + 1))
                gate(2 * t)
                if t + 1 < NT:
                    turned(ring, E_RN, r_done, t + 1)
                gate(2 * t + 1)


_INS = ["x", "p", "g_mix", "w_in", "pool_w", "pool_scale", "ssm_a_re", "ssm_a_im", "ssm_log_dt", "ssm_b_re",
        "ssm_b_im", "ssm_c_re", "ssm_c_im", "ssm_d", "glu_w", "glu_b", "w_out", "g_ffn", "router_grp_w",
        "router_grp_b", "router_exp_w", "router_exp_b", "exp_w_gate", "exp_w_up", "exp_w_down", "g_ple",
        "ple_gate_w", "ple_gate_b", "ple_proj_w", "g_final"]


def kernel(**inputs):
    import concourse.bacc as _bacc
    from concourse.bass_utils import run_bass_kernel_spmd as _run

    nc = _bacc.Bacc("TRN2", target_bir_lowering=False, num_devices=1)
    arrays, aps = {}, {}
    given = {n: inputs[n] for n in _INS}
    given["consts"] = constants()
    for name, value in given.items():
        a = np.ascontiguousarray(value)
        arrays[f"in_{name}_dram"] = a
        aps[name] = nc.dram_tensor(f"in_{name}_dram", a.shape, mybir.dt.from_np(a.dtype), kind="ExternalInput").ap()
    out = nc.dram_tensor("out_0_dram", (1, T, DM), F32, kind="ExternalOutput").ap()
    build(nc, aps, out)
    r = _run(nc, [arrays], core_ids=[0])
    return r.results[0]["out_0_dram"]
```
